# Optimizing a Trainium2 kernel written in Bass

```python
import jax, jax.numpy as jnp
from jax import lax
import numpy as np

D_MODEL = 1024
BATCH = 1
SEQ = 256
DEPTH = 1

RG_WIDTH = 1024
RG_BLOCKS = 4
RG_BLOCK_DIM = RG_WIDTH // RG_BLOCKS
RG_CONV = 4
RG_C = 8.0
GDN_QK_HEADS = 8
GDN_V_HEADS = 16
GDN_DK = 128
GDN_DV = 128
GDN_KEY_DIM = GDN_QK_HEADS * GDN_DK
GDN_VAL_DIM = GDN_V_HEADS * GDN_DV
GDN_CONV = 4
GDN_CHUNK = 64
N_EXPERTS = 32
TOP_K = 4
D_EXPERT = 1024
SWIGLU_ALPHA = 1.702
SWIGLU_LIMIT = 7.0
MOE_BLOCK = 128
EPS = 1e-6

IN_SIZES = (RG_WIDTH, RG_WIDTH,
            GDN_KEY_DIM, GDN_KEY_DIM, GDN_VAL_DIM,
            GDN_VAL_DIM,
            GDN_V_HEADS, GDN_V_HEADS,
            D_MODEL, D_MODEL)
D_IN = 2 * RG_WIDTH + 2 * GDN_KEY_DIM + 2 * GDN_VAL_DIM + 2 * GDN_V_HEADS + 2 * D_MODEL

kernel_name = "hybrid_rglru_gdn_moe_block"

def rms_norm(x, w):
    xf = x.astype(jnp.float32)
    y = xf * lax.rsqrt(jnp.mean(xf * xf, axis=-1, keepdims=True) + EPS)
    return (y * w.astype(jnp.float32)).astype(x.dtype)

def split_cols(z, sizes):
    outs, off = [], 0
    for s in sizes:
        outs.append(z[..., off:off + s])
        off += s
    return outs

def causal_depthwise_conv(x, w):
    k_w = w.shape[0]
    c = x.shape[-1]
    return lax.conv_general_dilated(x, w[:, None, :].astype(x.dtype), window_strides=(1,),
                                    padding=[(k_w - 1, 0)],
                                    dimension_numbers=('NWC', 'WIO', 'NWC'),
                                    feature_group_count=c)

def block_diag_linear(x, w, b):
    xh = x.reshape(x.shape[:-1] + (RG_BLOCKS, RG_BLOCK_DIM))
    y = jnp.einsum('bthi,hij->bthj', xh, w) + b
    return y.reshape(x.shape)

def rg_lru(x, w_a, b_a, w_x, b_x, lam):
    t_len = x.shape[1]
    xf = x.astype(jnp.float32)
    r = jax.nn.sigmoid(block_diag_linear(x, w_a, b_a).astype(jnp.float32))
    i = jax.nn.sigmoid(block_diag_linear(x, w_x, b_x).astype(jnp.float32))
    log_a = -RG_C * r * jax.nn.softplus(-lam.astype(jnp.float32))
    a = jnp.exp(log_a)
    mult = jnp.sqrt(jnp.maximum(-jnp.expm1(2.0 * log_a), 0.0))
    first = (jnp.arange(t_len) == 0)[None, :, None]
    mult = jnp.where(first, 1.0, mult)
    b = mult * (i * xf)

    def combine(c1, c2):
        a1, b1 = c1
        a2, b2 = c2
        return a1 * a2, a2 * b1 + b2

    _, h = lax.associative_scan(combine, (a, b), axis=1)
    return h.astype(x.dtype)

def l2norm(x):
    xf = x.astype(jnp.float32)
    return xf * lax.rsqrt(jnp.sum(xf * xf, axis=-1, keepdims=True) + EPS)

def gated_delta_rule_chunked(q, k, v, g, beta):
    b_sz, t_len, n_h, d_k = q.shape
    d_v = v.shape[-1]
    c = GDN_CHUNK
    n_c = t_len // c
    f32 = jnp.float32
    q = q.astype(f32) * (d_k ** -0.5)
    k = k.astype(f32)
    v = v.astype(f32)
    g = g.astype(f32)
    beta = beta.astype(f32)

    def to_chunks(t):
        return jnp.moveaxis(t.reshape((b_sz, n_c, c) + t.shape[2:]), 3, 1)

    qc, kc, vc, bc = to_chunks(q), to_chunks(k), to_chunks(v), to_chunks(beta)
    gc = jnp.cumsum(to_chunks(g), axis=-1)
    idx = jnp.arange(c)
    causal = idx[:, None] >= idx[None, :]
    strict = idx[:, None] > idx[None, :]
    diff = gc[..., :, None] - gc[..., None, :]
    decay = jnp.where(causal, jnp.exp(jnp.where(causal, diff, 0.0)), 0.0)

    kk = jnp.einsum('bhncd,bhnsd->bhncs', kc, kc)
    a_mat = jnp.where(strict, bc[..., None] * kk * decay, 0.0)
    eye = jnp.eye(c, dtype=f32)
    t_mat = lax.linalg.triangular_solve(eye + a_mat, jnp.broadcast_to(eye, a_mat.shape),
                                        left_side=True, lower=True, unit_diagonal=True)
    u = jnp.einsum('bhncs,bhnsd->bhncd', t_mat, vc * bc[..., None])
    w = jnp.einsum('bhncs,bhnsd->bhncd', t_mat, kc * (bc * jnp.exp(gc))[..., None])
    attn_intra = jnp.einsum('bhncd,bhnsd->bhncs', qc, kc) * decay
    q_dec = qc * jnp.exp(gc)[..., None]
    g_last = gc[..., -1]
    k_dec = kc * jnp.exp(g_last[..., None] - gc)[..., None]

    def step(s, inp):
        u_n, w_n, a_n, qd_n, kd_n, gl_n = inp
        v_new = u_n - jnp.einsum('bhcd,bhde->bhce', w_n, s)
        o = jnp.einsum('bhcd,bhde->bhce', qd_n, s) + jnp.einsum('bhcs,bhse->bhce', a_n, v_new)
        s = s * jnp.exp(gl_n)[..., None, None] + jnp.einsum('bhcd,bhce->bhde', kd_n, v_new)
        return s, o

    xs = tuple(jnp.moveaxis(t, 2, 0) for t in (u, w, attn_intra, q_dec, k_dec, g_last))
    s0 = jnp.zeros((b_sz, n_h, d_k, d_v), f32)
    _, o = lax.scan(step, s0, xs)
    return jnp.transpose(o, (1, 0, 3, 2, 4)).reshape(b_sz, t_len, n_h, d_v)

def moe_ffn(xn, router_w, router_b, w_gu, b_gu, w_down, b_down):
    b_sz, t_len, d = xn.shape
    n_tok = b_sz * t_len
    xt = xn.reshape(n_tok, d)
    logits = (xt @ router_w + router_b).astype(jnp.float32)
    top_vals, top_idx = lax.top_k(logits, TOP_K)
    gates = jax.nn.softmax(top_vals, axis=-1)

    n_as = n_tok * TOP_K
    flat_e = top_idx.reshape(n_as).astype(jnp.int32)
    flat_tok = (jnp.arange(n_as, dtype=jnp.int32) // TOP_K)
    flat_w = gates.reshape(n_as)
    order = jnp.argsort(flat_e, stable=True)
    e_sorted = flat_e[order]
    counts = jnp.zeros((N_EXPERTS,), jnp.int32).at[flat_e].add(1)
    starts = jnp.cumsum(counts) - counts
    padded = ((counts + MOE_BLOCK - 1) // MOE_BLOCK) * MOE_BLOCK
    pends = jnp.cumsum(padded)
    pstarts = pends - padded
    rank = jnp.arange(n_as, dtype=jnp.int32) - starts[e_sorted]
    dest = pstarts[e_sorted] + rank
    n_blocks = (n_as + MOE_BLOCK - 1) // MOE_BLOCK + N_EXPERTS
    n_rows = n_blocks * MOE_BLOCK
    row_tok = jnp.zeros((n_rows,), jnp.int32).at[dest].set(flat_tok[order])
    row_w = jnp.zeros((n_rows,), jnp.float32).at[dest].set(flat_w[order])
    block_start = jnp.arange(n_blocks, dtype=jnp.int32) * MOE_BLOCK
    block_e = jnp.minimum(jnp.searchsorted(pends, block_start, side='right'), N_EXPERTS - 1)

    x_rows = xt[row_tok].reshape(n_blocks, MOE_BLOCK, d)

    def expert_block(args):
        xb, e = args
        gu = xb @ w_gu[e] + b_gu[e]
        gate, up = gu[:, :D_EXPERT], gu[:, D_EXPERT:]
        gate = jnp.minimum(gate, SWIGLU_LIMIT)
        up = jnp.clip(up, -SWIGLU_LIMIT, SWIGLU_LIMIT)
        hid = (up + 1.0) * (gate * jax.nn.sigmoid(SWIGLU_ALPHA * gate))
        return hid @ w_down[e] + b_down[e]

    y_rows = lax.map(expert_block, (x_rows, block_e)).reshape(n_rows, d)
    y = jnp.zeros((n_tok, d), jnp.float32).at[row_tok].add(y_rows.astype(jnp.float32) * row_w[:, None])
    return y.reshape(b_sz, t_len, d).astype(xn.dtype)

def setup_inputs(seed: int = 0) -> dict:
    key = jax.random.key(seed)
    ks = jax.random.split(key, 24)
    f32 = jnp.float32
    nrm = lambda k, shape, s: jax.random.normal(k, shape, f32) * s
    gain = lambda k, shape: 1.0 + 0.02 * jax.random.normal(k, shape, f32)
    u = jax.random.uniform(ks[8], (DEPTH, RG_WIDTH), f32, 0.9, 0.999)
    s = u ** (1.0 / RG_C)
    return {
        "x": nrm(ks[0], (BATCH, SEQ, D_MODEL), 1.0),
        "norm_mix_w": gain(ks[1], (DEPTH, D_MODEL)),
        "w_in": nrm(ks[2], (DEPTH, D_MODEL, D_IN), D_MODEL ** -0.5),
        "rg_conv_w": nrm(ks[3], (DEPTH, RG_CONV, RG_WIDTH), RG_CONV ** -0.5),
        "rg_conv_b": nrm(ks[4], (DEPTH, RG_WIDTH), 0.01),
        "rg_gate_a_w": nrm(ks[5], (DEPTH, RG_BLOCKS, RG_BLOCK_DIM, RG_BLOCK_DIM), RG_BLOCK_DIM ** -0.5),
        "rg_gate_a_b": nrm(ks[6], (DEPTH, RG_BLOCKS, RG_BLOCK_DIM), 0.01),
        "rg_gate_x_w": nrm(ks[7], (DEPTH, RG_BLOCKS, RG_BLOCK_DIM, RG_BLOCK_DIM), RG_BLOCK_DIM ** -0.5),
        "rg_gate_x_b": nrm(ks[9], (DEPTH, RG_BLOCKS, RG_BLOCK_DIM), 0.01),
        "rg_lambda": jnp.log(s) - jnp.log1p(-s),
        "gdn_conv_w": nrm(ks[10], (DEPTH, GDN_CONV, 2 * GDN_KEY_DIM + GDN_VAL_DIM), GDN_CONV ** -0.5),
        "gdn_A_log": jnp.log(jax.random.uniform(ks[11], (DEPTH, GDN_V_HEADS), f32, 1.0, 16.0)),
        "gdn_dt_bias": nrm(ks[12], (DEPTH, GDN_V_HEADS), 0.1),
        "gdn_norm_w": gain(ks[13], (DEPTH, GDN_DV)),
        "w_branch_rg": nrm(ks[14], (DEPTH, RG_WIDTH, D_MODEL), RG_WIDTH ** -0.5),
        "w_branch_gdn": nrm(ks[15], (DEPTH, GDN_VAL_DIM, D_MODEL), GDN_VAL_DIM ** -0.5),
        "w_out": nrm(ks[16], (DEPTH, D_MODEL, D_MODEL), D_MODEL ** -0.5),
        "norm_ffn_w": gain(ks[17], (DEPTH, D_MODEL)),
        "router_w": nrm(ks[18], (DEPTH, D_MODEL, N_EXPERTS), D_MODEL ** -0.5),
        "router_b": nrm(ks[19], (DEPTH, N_EXPERTS), 0.01),
        "moe_w_gate_up": nrm(ks[20], (DEPTH, N_EXPERTS, D_MODEL, 2 * D_EXPERT), D_MODEL ** -0.5),
        "moe_b_gate_up": nrm(ks[21], (DEPTH, N_EXPERTS, 2 * D_EXPERT), 0.01),
        "moe_w_down": nrm(ks[22], (DEPTH, N_EXPERTS, D_EXPERT, D_MODEL), D_EXPERT ** -0.5),
        "moe_b_down": nrm(ks[23], (DEPTH, N_EXPERTS, D_MODEL), 0.01),
        "norm_final_w": gain(jax.random.fold_in(key, 99), (D_MODEL,)),
    }

def reference(x, norm_mix_w, w_in, rg_conv_w, rg_conv_b, rg_gate_a_w, rg_gate_a_b, rg_gate_x_w,
              rg_gate_x_b, rg_lambda, gdn_conv_w, gdn_A_log, gdn_dt_bias, gdn_norm_w, w_branch_rg,
              w_branch_gdn, w_out, norm_ffn_w, router_w, router_b, moe_w_gate_up, moe_b_gate_up,
              moe_w_down, moe_b_down, norm_final_w):
    b_sz, t_len, _ = x.shape
    rep = GDN_V_HEADS // GDN_QK_HEADS
    h = x
    for l in range(DEPTH):
        xn = rms_norm(h, norm_mix_w[l])
        z = xn @ w_in[l]
        rg_x, rg_y, q_raw, k_raw, v_raw, z_gate, b_raw, a_raw, gate_a, gate_b = split_cols(z, IN_SIZES)

        xa = causal_depthwise_conv(rg_x, rg_conv_w[l]) + rg_conv_b[l]
        ha = rg_lru(xa, rg_gate_a_w[l], rg_gate_a_b[l], rg_gate_x_w[l], rg_gate_x_b[l], rg_lambda[l])
        ya = (ha * jax.nn.gelu(rg_y)) @ w_branch_rg[l]

        qkv = jax.nn.silu(causal_depthwise_conv(jnp.concatenate([q_raw, k_raw, v_raw], axis=-1), gdn_conv_w[l]))
        q, k, v = split_cols(qkv, (GDN_KEY_DIM, GDN_KEY_DIM, GDN_VAL_DIM))
        q = jnp.repeat(l2norm(q.reshape(b_sz, t_len, GDN_QK_HEADS, GDN_DK)), rep, axis=2)
        k = jnp.repeat(l2norm(k.reshape(b_sz, t_len, GDN_QK_HEADS, GDN_DK)), rep, axis=2)
        v = v.reshape(b_sz, t_len, GDN_V_HEADS, GDN_DV)
        beta = jax.nn.sigmoid(b_raw.astype(jnp.float32))
        g = -jnp.exp(gdn_A_log[l].astype(jnp.float32)) * jax.nn.softplus(
            a_raw.astype(jnp.float32) + gdn_dt_bias[l].astype(jnp.float32))
        o = gated_delta_rule_chunked(q, k, v, g, beta).astype(x.dtype)
        o = rms_norm(o, gdn_norm_w[l]) * jax.nn.silu(z_gate.reshape(b_sz, t_len, GDN_V_HEADS, GDN_DV))
        yb = o.reshape(b_sz, t_len, GDN_VAL_DIM) @ w_branch_gdn[l]

        mix = jax.nn.sigmoid(gate_a) * ya + jax.nn.sigmoid(gate_b) * yb
        h = h + mix @ w_out[l]

        hn = rms_norm(h, norm_ffn_w[l])
        h = h + moe_ffn(hn, router_w[l], router_b[l], moe_w_gate_up[l], moe_b_gate_up[l],
                        moe_w_down[l], moe_b_down[l])
    return rms_norm(h, norm_final_w)


_drawn_inputs = setup_inputs


def setup_inputs(seed=0):
    import zlib

    import numpy as np

    out = dict(_drawn_inputs(seed))
    spreads = {}
    factors = {'rg_gate_a_b': 26.346,
     'rg_gate_x_b': 19.075,
     'moe_b_gate_up': 8.0,
     'moe_b_down': 8.0,
     'norm_final_w': 23.358,
     'gdn_dt_bias': 2.731}
    for name, (base, spread) in spreads.items():
        noise = np.random.default_rng([zlib.crc32(name.encode()), seed]).standard_normal(out[name].shape)
        drawn = base * np.exp(spread * noise) if base else spread * noise
        out[name] = __import__('jax').numpy.asarray(drawn.astype(out[name].dtype))
    for name, factor in factors.items():
        out[name] = (out[name] * factor).astype(out[name].dtype)
    return out
```

```python
from contextlib import ExitStack

import numpy as np

import concourse.bass as bass
from concourse import mybir

F32 = mybir.dt.float32
I32 = mybir.dt.int32
ALU = mybir.AluOpType
ACT = mybir.ActivationFunctionType
AX = mybir.AxisListType.X

P = 128
D = 1024
T = 256
NT = T // P
KT = D // P
RGB = 4
RG_C = 8.0
QKH = 8
VH = 16
DK = 128
LEVELS = 7
NE = 32
TOP = 4
CAP = 64
FT = 8
LIMIT = 7.0
ALPHA = 1.702
EPS = 1e-6
BIG = 1e30
SLOT = 2048
NSLOT = 12
GELU_C = 0.7978845608028654
GELU_A = 0.044715

VEC = {}
_n = 0
for _name, _w in (("norm_mix", KT), ("rg_cw", 4 * KT), ("rg_cb", KT), ("ba", KT), ("bx", KT), ("lam", KT),
                  ("gdn_cw", QKH * 4 * 4), ("gdn_norm", 1)):
    VEC[_name] = (_n, _w)
    _n += _w
NVEC = _n
ROW = {"router_b": (0, NE), "dt_bias": (32, VH), "A_log": (48, VH)}
NROW = 64
CON = {}
_n = 0
for _name, _w in (("ident", P), ("tri_incl", P), ("tri_strict", P), ("ones", P), ("neg", P), ("masks", LEVELS * P),
                  ("ident_qk", 4 * P), ("ident_half", P), ("slots", 2 * CAP)):
    CON[_name] = (_n, _w)
    _n += _w
NCON = _n


def constants():
    s, c = np.arange(P)[:, None], np.arange(P)[None, :]
    con = np.zeros((P, NCON), np.float32)

    def put(name, v):
        o, w = CON[name]
        con[:, o:o + w] = v

    put("ident", s == c)
    put("tri_incl", s <= c)
    put("tri_strict", s < c)
    put("ones", 1.0)
    put("neg", np.where(c < s, -BIG, 0.0))
    masks = []
    for level in range(LEVELS):
        b = 2 ** level
        masks.append((s // (2 * b) == c // (2 * b)) & (s % (2 * b) < b) & (c % (2 * b) >= b))
    put("masks", np.concatenate(masks, axis=1))
    eye = (s == c).astype(np.float32)
    put("ident_qk", np.concatenate([0.5 * eye] * 2 + [0.5 * DK ** -0.5 * eye] * 2, axis=1))
    put("ident_half", 0.5 * eye)
    put("slots", np.tile(np.arange(CAP), 2)[None, :])
    return con


class Steps:

    def __init__(self, sem, names, rounds=1, lacking=(), before=0):
        self.sem, self.names, self.rounds, self.before = sem, names, rounds, before
        self.short = [n for n in names if n not in lacking]
        self.at = 0

    def _list(self, r):
        return self.short if isinstance(r, int) and r == self.rounds - 1 else self.names

    def ends(self, name, r=0):
        names = self._list(r)
        self.at %= len(names)
        assert names[self.at] == name, (name, names[self.at])
        self.at += 1
        return self.sem, 1

    def past(self, name, r=0):
        return self.sem, self.before + r * len(self.names) + self._list(r).index(name) + 1


def build(nc, x, vec, row, con, w_rg, w_rgg, w_ba, w_gdn, w_gates, w_bg, w_br, w_out, ffn_rows,
          moe_gu, moe_down, b_gu, b_down, out):
    ctx = ExitStack()
    with ctx:
        def sb(name, shape, dt=F32):
            return ctx.enter_context(nc.sbuf_tensor(name, shape, dt))

        def sem(name):
            return ctx.enter_context(nc.semaphore(name))

        ring = sb("ring", [P, NSLOT, SLOT])
        h = sb("h", [P, NT, D])
        xnT = sb("xnT", [P, KT, T])
        mixT = sb("mixT", [P, KT, T])
        rgo = sb("rgo", [P, KT, T])
        og = sb("og", [P, VH, T])
        V = sb("V", [P, NVEC])
        R = sb("R", [P, NROW])
        C = sb("C", [P, NCON])
        W_ba = sb("W_ba", [P, KT, 2 * VH])
        W_r = sb("W_r", [P, KT, NE])
        rawp = sb("rawp", [P, 4, 3 + T])
        cqk = sb("cqk", [P, 2, T])
        cv = sb("cv", [P, 2, T])
        thq = sb("thq", [P, 2, T])
        thv = sb("thv", [P, 2, T])
        zraw = sb("zraw", [P, 2, T])
        zs = sb("zs", [P, 2, T])
        QK = sb("QK", [P, NT, 2, P])
        kt0 = sb("kt0", [P, P])
        attT = sb("attT", [P, NT, 2, P])
        MT = sb("MT", [P, NT, 2, P])
        MM = sb("MM", [P, 3, 4, P])
        XU = sb("XU", [P, 4, 2, P])
        vn = sb("vn", [P, NT, 2, P])
        vk = sb("vk", [P, 2, P])
        S1 = sb("S1", [P, 2, P])
        qd = sb("qd", [P, 2, P])
        osq = sb("osq", [P, 2, T])
        ow = sb("ow", [P, 2, T])
        diag = sb("diag", [P, 4, P])
        rowbuf = sb("rowbuf", [P, 2, T])
        rowsel = rowbuf[0:VH, :, :]
        Vt = thv[:, :, :].rearrange("p j (n c) -> p j n c", n=2)
        Dt = thq[:, :, :].rearrange("p j (n c) -> p j n c", n=2)
        P1s = thq[:, :, :].rearrange("p j (n c) -> p (j n) c", n=2)
        rr = vk
        eG = rowbuf[:, :, 0:P]
        beta = sb("beta", [P, NT, VH])
        gcol = sb("gcol", [P, NT, VH])
        gsum = sb("gsum", [P, NT, VH])
        negeg = sb("negeg", [P, NT, VH])
        kdec = sb("kdec", [P, VH])
        gcT = sb("gcT", [VH, T])
        small = sb("small", [P, 8, 48])
        ss = sb("ss", [P, 4, 4])
        half_pow = sb("half_pow", [P, 4])
        sp4 = sb("sp4", [P, KT])
        hb = sb("hb", [P, 2 * KT])
        loops = sb("loops", [P, 1], I32)
        PS = ctx.enter_context(nc.psum_tensor("PS", [P, 8, 512], F32))

        def vcol(name, i, n=1):
            o, _ = VEC[name]
            return V[:, bass.ds(o + i, n)]

        def con_(name, a=0, n=P):
            o, _ = CON[name]
            return C[:, o + a:o + a + n]

        ident, tri_incl, tri_strict = con_("ident"), con_("tri_incl"), con_("tri_strict")
        ones, neg = con_("ones"), con_("neg")

        def mask(level):
            return con_("masks", level * P)

        def bank(i):
            return PS[:, i, :]

        def bank3(i, a):
            return PS[:, i, :].rearrange("p (a n) -> p a n", a=a)

        def mid(ap, n):
            return ap.unsqueeze(1).broadcast_to([ap.shape[0], n, ap.shape[1]])

        def last(ap, n):
            return ap.unsqueeze(2).broadcast_to([ap.shape[0], ap.shape[1], n])

        x_loaded, con_loaded = sem("x_loaded"), sem("con_loaded")
        vec_loaded, row_loaded, ba_loaded = sem("vec_loaded"), sem("row_loaded"), sem("ba_loaded")
        loaded = [sem(f"loaded{s}") for s in range(NSLOT)]
        used = [sem(f"used{s}") for s in range(NSLOT)]
        rows_loaded, bdown_loaded, stored = sem("rows_loaded"), sem("bdown_loaded"), sem("stored")
        bgu_loaded = sem("bgu_loaded")

        A_act = Steps(sem("a_act"), ["ss0", "ss1"])
        A_pool = Steps(sem("a_pool"), ["rstd"])
        A_dve = Steps(sem("a_dve"), ["pow", "ms", "pad", "xn0", "xn1", "ev0", "ev1", "ev2", "ev3"])
        A_pe = Steps(sem("a_pe"), ["tr0", "tr1", "tr2", "tr3"])
        SP_DVE = ["in_ba", "in_lam", "abs", "y2", "s_rec", "s", "s2",
                  "p6", "p5", "p4", "p3", "p2", "p1", "p0", "pos", "sp"]
        B_dve = Steps(sem("b_dve"), SP_DVE + ["sp4", "hb", "beta", "g", "gc", "gc_last", "negeg", "gcT"])
        B_act = Steps(sem("b_act"), ["tanh_b", "exp_abs", "exp_A", "kdec", "eg"])
        B_pe = Steps(sem("b_pe"), ["ba", "cum", "tr"])

        xy_copied = sem("xy_copied")
        C_act = Steps(sem("c_act"), ["y2", "tanh_y", "tanh_a", "tanh_i", "decay", "tanh_l"], RGB)
        C_dve = Steps(sem("c_dve"), [f"conv{j}" for j in range(8)] + ["cub", "cub_y", "l0", "l1", "gated", "dec2",
                                    "mult", "guard", "gelu"], RGB)
        Ct_act = Steps(sem("ct_act"), ["sqrt"])
        Ct_dve = Steps(sem("ct_dve"), ["first", "b"] + [f"scan{k}" for k in range(KT)] + ["out"])

        G_pe = Steps(sem("g_pe"), ["ss_o", "bc_o", "ss_qk", "bc_qk", "G", "kkqk", "trv", "trk", "trU"]
                     + [s for lv in range(1, LEVELS) for s in (f"P1_{lv}", f"P2_{lv}")]
                     + ["vn0", "S1", "kS", "vn1", "O"], QKH)
        G_act = Steps(sem("g_act"), ["tanh_qk", "sq_qk", "tanh_v", "tanh_z", "eG", "Vt", "Dt", "X"]
                      + [f"P1s_{lv}" for lv in range(1, LEVELS)]
                      + ["S1"], QKH)
        G_dve = Steps(sem("g_dve"), [f"cqk{j}" for j in range(8)] + ["s_qk"] + [f"cv{j}" for j in range(8)]
                      + ["ss_o", "diag_o", "og", "rowsel", "ss_qk", "diag_qk", "s_v", "s_z", "QK", "kt0",
                         "D0", "D1", "D2", "D3", "qd", "M0", "M1", "M2", "M3", "att", "U"]
                      + [f"XU_{lv}" for lv in range(1, LEVELS)]
                      + ["vk0", "vk1", "vn00", "vn01", "r0", "r1", "vn10", "vn11", "ow"],
                      QKH)
        G_pool = Steps(sem("g_pool"), ["r_o", "r_qk"] + [f"MM{lv}" for lv in range(LEVELS)], QKH)
        qk_copied, v_copied, z_copied, osq_ready = sem("qk_copied"), sem("v_copied"), sem("z_copied"), sem("osq_ready")
        ow_zero, poly = sem("ow_zero"), sem("poly")
        Z_pe = Steps(sem("z_pe"), ["ss_o", "bc_o"])
        Z_dve = Steps(sem("z_dve"), ["ss_o", "diag_o", "og"])
        Z_pool = Steps(sem("z_pool"), ["r_o"])

        M_act = Steps(sem("m_act"), ["tanh"], KT)
        M_dve = Steps(sem("m_dve"), ["a", "b", "mix"], KT)

        O_pe = Steps(sem("o_pe"), ["tr0", "tr1", "tr2", "tr3", "router", "pos", "trg", "bd"])
        O_act = Steps(sem("o_act"), ["ss0", "ss1", "exp0", "exp1", "gT"])
        O_pool = Steps(sem("o_pool"), ["rstd"])
        O_dve = Steps(sem("o_dve"), ["h0", "h1", "h2", "h3", "ms", "hn0", "hn1", "ev0", "ev1", "ev2", "ev3",
                                     "logits", "max0", "max1", "negm", "gt0", "gt1", "ngt", "eq0", "eq1",
                                     "need", "cum0", "cum1", "ok0", "ok1", "eqok", "sel",
                                     "exs", "sum", "rec", "gate0", "gate1", "pos1", "posm", "cmax",
                                     "c64", "c128", "c192", "csum", "csum2", "loops",
                                     "b0", "b1", "b2", "b3"])

        E_pe0 = Steps(sem("e_pe"), ["gather", "trX"])
        E_pe = Steps(E_pe0.sem, ["trS", "gather", "trH", "trX", "scatter"], before=2)
        E_act0 = Steps(sem("e_act"), ["xg", "xT"])
        E_act = Steps(E_act0.sem, ["th", "ST", "xg", "hidT", "xT", "Y"], before=2)
        E_dve0 = Steps(sem("e_dve"), ["S0", "S1", "SG0", "SG1", "next"])
        E_dve = Steps(E_dve0.sem, ["S0", "S1", "g", "u", "p", "hid", "SG0", "SG1", "next", "y0", "y1", "y2", "y3"],
                      before=5)
        onehot_ready = sem("onehot_ready")
        F_act = Steps(sem("f_act"), ["ss0", "ss1"])
        F_pool = Steps(sem("f_pool"), ["rstd"])
        F_dve = Steps(sem("f_dve"), ["ms", "o0", "o1"])

        S_RG, S_GDN, S_MIX, S_OUT = (0, 1, 2), (3, 4, 5), (6, 7, 8), (9, 10, 11, 0)
        fills = [0] * NSLOT
        for slots, n in ((S_RG, RGB), (S_GDN, QKH), (S_MIX, KT), (S_OUT, 1)):
            for s in slots:
                fills[s] += n

        ring4 = ring[:, :, :].rearrange("p s (t k c) -> p s t k c", t=2, k=KT)
        ring16 = ring[:, :, :].rearrange("p s (k c) -> p s k c", c=P)
        ring2 = ring[:, :, :].rearrange("p s (k n) -> p s k n", k=2)

        spx, spy, spa, sps, sps2, spp = (small[:, i, 0:40] for i in range(6))
        tb, exA = small[:, 6, 0:32], small[:, 7, 0:16]
        xa, ta, ti, L, yraw, q3, ty, y2b = cqk, thq, thv, cv, zraw, zs, osq, ow
        mrg, arg = og[:, 0:KT, :], og[:, KT:2 * KT, :]
        rsc = Dt[:, :, :, :].rearrange("p a b c -> p (a b c)")

        def r32(i):
            return rsc[:, 64 * i:64 * i + 64].rearrange("p (n e) -> p n e", n=NT)

        logits, gt, eq, cum, ok, sel_ = (r32(i) for i in range(6))
        exs, gate = r32(6), r32(7)
        msc = MT[:, :, :, :].rearrange("p a b c -> p (a b c)")
        posm = msc[:, 0:64].rearrange("p (n e) -> p n e", n=NT)
        mx8 = msc[:, 64:80].rearrange("p (n e) -> p n e", n=NT)
        negm, ngt, need, gsm, grec = (msc[:, 80 + 2 * i:82 + 2 * i] for i in range(5))
        cmax, c64, c128, c192 = (msc[:, 96 + i:97 + i] for i in range(4))
        hn = rgo[:, :, :].rearrange("p k t -> p (k t)").rearrange("p (n d) -> p n d", n=NT)
        rows = mixT[:, :, :].rearrange("p k t -> p (k t)").rearrange("p (n d) -> p n d", n=NT)
        ogf = og[:, :, :].rearrange("p k t -> p (k t)")
        gT, bdn = ogf[0:NE, 2816:2816 + T], ogf[0:NE, 3072:3072 + D]
        bgu = xnT[:, :, :].rearrange("p k t -> p (k t)")[0:NE, :]
        eg_, eu, ehid, Y = (ogf[:, 512 * i:512 * (i + 1)] for i in range(4))
        ST = ogf[:, 2048:2304].rearrange("p (n t) -> p n t", n=NT)
        Ssel = ogf[:, 2304:2432].rearrange("p (n s) -> p n s", n=NT)
        SG = ogf[:, 2432:2688].rearrange("p (n s) -> p n s", n=NT)
        onehot = ogf[0:NE, 2688:2688 + CAP]

        def flat3(t):
            return t[:, :, :].rearrange("p a n -> p (a n)")

        def by_tile(t):
            return flat3(t).rearrange("p (b h s) -> p b h s", h=2, s=CAP)

        xgs, eth = flat3(zraw), flat3(thv)
        xT, hidT = by_tile(cqk), by_tile(cv)

        block = ctx.enter_context(nc.Block())

        @block.sync
        def _(sp):
            def fill(slot, n, src, width=SLOT):
                sp.wait_ge(used[slot], n - 1)
                sp.dma_start(ring[:, slot, 0:width], src).then_inc(loaded[slot], 16)

            sp.dma_start(h[:, :, :], x.rearrange("(n p) d -> p n d", p=P)).then_inc(x_loaded, 16)
            sp.dma_start(C[:, :], con).then_inc(con_loaded, 16)
            with sp.Fori(0, RGB) as i:
                fill(S_RG[0], i + 1, w_rg[bass.ds(i, 1), 0].rearrange("a p n -> (a p) n"))
                fill(S_RG[1], i + 1, w_rg[bass.ds(i, 1), 1].rearrange("a p n -> (a p) n"))
                fill(S_RG[2], i + 1, w_rgg[bass.ds(i, 1)].rearrange("a p n -> (a p) n"), D)
            with sp.Fori(0, QKH) as g:
                for j in range(3):
                    fill(S_GDN[j], g + 1, w_gdn[bass.ds(g, 1), j].rearrange("a p n -> (a p) n"))
            w_out_v = w_out.rearrange("(i k p) n -> i p k n", k=2, p=P)

            def fill_out(i):
                s = S_OUT[i]
                sp.wait_ge(used[s], fills[s] - 1)
                sp.dma_start(ring2[:, s, :, :], w_out_v[i]).then_inc(loaded[s], 16)

            for i in range(4):
                fill_out(i)

            def fill_mix(j):
                fill(S_MIX[0], j + 1, w_gates[bass.ds(j, 1)].rearrange("a p n -> (a p) n"))
                fill(S_MIX[1], j + 1, w_bg[bass.ds(j, 1)].rearrange("a p n -> (a p) n"))
                fill(S_MIX[2], j + 1, w_br[bass.ds(j, 1)].rearrange("a p n -> (a p) n"), D)

            fill_mix(0)

            def fill_expert(s, it, e):
                sp.wait_ge(used[s], fills[s] + it)
                if s < FT:
                    src = moe_gu[bass.ds(e, 1), s].rearrange("a p n -> (a p) n")
                    sp.dma_start(ring[:, s, :], src).then_inc(loaded[s], 16)
                else:
                    src = moe_down[bass.ds(e, 1)].rearrange("a (i k p) n -> (a i) p k n", k=2, p=P)[s - FT]
                    sp.dma_start(ring2[:, s, :, :], src).then_inc(loaded[s], 16)

            for s in (1, 2, 3, 4, 5):
                fill_expert(s, 0, 0)
            with sp.Fori(1, KT) as j:
                fill_mix(j)
            for s in (6, 7, 8, 9, 10, 11, 0):
                fill_expert(s, 0, 0)
            sp.wait_ge(*O_dve.past("loops"))
            n_it = sp.value_load(loops[0:1, 0:1], min_val=NE, max_val=4 * NE)
            with sp.Fori(1, n_it) as it:
                for s in range(NSLOT):
                    fill_expert(s, it, it % NE)

        @block.tensor
        def _(pe):
            mm, tr = nc.tensor.matmul, nc.tensor.transpose

            def transposes(src, steps, ready, evacuated, first):
                for b in range(4):
                    if b == 0:
                        pe.wait_ge(*ready)
                    for i in range(4):
                        k, n = 2 * b + i // 2, i % 2
                        ins = tr(PS[:, first + b, i * P:(i + 1) * P], src[:, n, k * P:(k + 1) * P], ident)
                    ins.then_inc(*steps.ends(f"tr{b}"))

            pe.wait_ge(con_loaded, 16)
            transposes(hn, A_pe, A_dve.past("xn1"), None, 0)
            pe.wait_ge(*A_dve.past("ev3"))
            pe.wait_ge(ba_loaded, 32)
            for n in range(NT):
                for k in range(KT):
                    ins = mm(PS[:, 4, n * 32:n * 32 + 32], xnT[:, k, n * P:(n + 1) * P], W_ba[:, k, :],
                             start=(k == 0), stop=(k == KT - 1))
            ins.then_inc(*B_pe.ends("ba"))
            pe.wait_ge(*B_dve.past("g"))
            mm(PS[:, 5, 0:32], tri_incl, gcol[:, :, :], start=True, stop=True)
            mm(PS[:, 5, 32:48], ones, gcol[:, 0, :], start=True, stop=True).then_inc(*B_pe.ends("cum"))
            pe.wait_ge(*B_dve.past("gc"))
            for n in range(NT):
                ins = tr(PS[0:VH, 6, n * P:(n + 1) * P], gsum[:, n, :], ident)
            ins.then_inc(*B_pe.ends("tr"))

            def pair(bank_, slot, a=0, b=2 * KT):
                for i in range(a, b):
                    t, k = i // KT, i % KT
                    ins = mm(PS[:, bank_, t * T:(t + 1) * T], ring4[:, slot, t, k, :], xnT[:, k, :],
                             start=(k == 0), stop=(k == KT - 1))
                return ins

            with pe.Fori(0, RGB) as i:
                pe.wait_ge(loaded[S_RG[0]], 16 * (i + 1))
                pe.wait_ge(xy_copied, 2 * i)
                pair(0, S_RG[0]).then_inc(used[S_RG[0]], 1)
                pe.wait_ge(loaded[S_RG[1]], 16 * (i + 1))
                pair(1, S_RG[1]).then_inc(used[S_RG[1]], 1)
                pe.wait_ge(loaded[S_RG[2]], 16 * (i + 1))
                pe.wait_ge(*C_dve.past("conv7", i))
                for gate_i in range(2):
                    for jt in range(2):
                        for k in range(2):
                            w0 = gate_i * 512 + k * T + jt * P
                            ins = mm(PS[:, 2 + gate_i, jt * T:(jt + 1) * T], ring[:, S_RG[2], w0:w0 + P],
                                     xa[:, k, :], start=(k == 0), stop=(k == 1))
                ins.then_inc(used[S_RG[2]], 1)

            PJ0, PJ1, P1B, PX0, PX1, QKB, GB, TL = range(8)

            def load_wait(j, r):
                pe.wait_ge(loaded[S_GDN[j]], 16 * (r + 1))

            load_wait(0, 0)
            pe.wait_ge(xy_copied, 2 * RGB)
            pair(PJ0, S_GDN[0]).then_inc(used[S_GDN[0]], 1)
            load_wait(1, 0)
            pair(PJ1, S_GDN[1]).then_inc(used[S_GDN[1]], 1)
            load_wait(2, 0)
            pe.wait_ge(qk_copied, 1)
            pair(PJ0, S_GDN[2]).then_inc(used[S_GDN[2]], 1)

            def norm_sums(dst, src, r, steps, name):
                for i in range(4):
                    ins = mm(PS[:, TL, dst + i:dst + i + 1], src[:, i // 2, (i % 2) * P:(i % 2 + 1) * P], ones[:, 0:1],
                             start=True, stop=True)
                ins.then_inc(*steps.ends(name, r))

            def gdn_head(g, final):
                def z(a, b):
                    if final:
                        return
                    if a == 0:
                        load_wait(2, g + 1)
                        pe.wait_ge(qk_copied, g + 2)
                    ins = pair(PJ0, S_GDN[2], a, b)
                    if b == 2 * KT:
                        ins.then_inc(used[S_GDN[2]], 1)

                if not final:
                    load_wait(0, g + 1)
                    pe.wait_ge(z_copied, g + 1)
                    pair(PJ0, S_GDN[0]).then_inc(used[S_GDN[0]], 1)
                pe.wait_ge(osq_ready, g + 1)
                norm_sums(4, osq, g, G_pe, "ss_o")
                pe.wait_ge(*G_dve.past("diag_o", g))
                mm(bank(PX1), ones, diag[:, :, :], start=True, stop=True).then_inc(*G_pe.ends("bc_o", g))
                pe.wait_ge(*G_act.past("sq_qk", g))
                norm_sums(0, thq, g, G_pe, "ss_qk")
                if not final:
                    load_wait(1, g + 1)
                    pe.wait_ge(v_copied, g + 1)
                    pair(PJ1, S_GDN[1], 0, KT)
                pe.wait_ge(*G_dve.past("diag_qk", g))
                mm(bank(PX0), ones, diag[:, :, :], start=True, stop=True).then_inc(*G_pe.ends("bc_qk", g))
                if not final:
                    pair(PJ1, S_GDN[1], KT, 2 * KT).then_inc(used[S_GDN[1]], 1)
                pe.wait_ge(*G_dve.past("rowsel", g))
                for j in range(2):
                    ins = mm(PS[:, GB, j * T:(j + 1) * T], ones[0:VH, :], rowsel[:, j, :], start=True, stop=True)
                ins.then_inc(*G_pe.ends("G", g))
                pe.wait_ge(*G_dve.past("QK", g))
                for n in range(NT):
                    ins = mm(PS[:, QKB, n * T:(n + 1) * T], QK[:, n, 0, :], QK[:, n, :, :], start=True, stop=True)
                ins.then_inc(*G_pe.ends("kkqk", g))
                pe.wait_ge(*G_dve.past("s_v", g))
                for n in range(NT):
                    for j in range(2):
                        ins = tr(PS[:, P1B, (2 * n + j) * P:(2 * n + j + 1) * P], cv[:, j, n * P:(n + 1) * P], ident)
                ins.then_inc(*G_pe.ends("trv", g))
                z(0, 4)
                tr(PS[:, TL, P:2 * P], QK[:, 0, 0, :], ident).then_inc(*G_pe.ends("trk", g))
                pe.wait_ge(*G_dve.past("U", g))
                pe.wait_ge(*G_act.past("Vt", g))
                for u in range(4):
                    ins = tr(PS[:, P1B, u * P:(u + 1) * P], XU[:, u, 1, :], ident)
                ins.then_inc(*G_pe.ends("trU", g))
                z(4, 6)
                for lv in range(1, LEVELS):
                    pe.wait_ge(*G_pool.past(f"MM{lv}", g))
                    if lv == 1:
                        pe.wait_ge(*G_act.past("X", g))
                    else:
                        pe.wait_ge(*G_dve.past(f"XU_{lv - 1}", g))
                    for u in range(4):
                        ins = mm(PS[:, P1B, u * P:(u + 1) * P], MM[:, lv % 3, u, :], XU[:, u, 0, :],
                                 start=True, stop=True)
                    ins.then_inc(*G_pe.ends(f"P1_{lv}", g))
                    if lv < LEVELS - 1:
                        z(5 + lv, 6 + lv)
                    pe.wait_ge(*G_act.past(f"P1s_{lv}", g))
                    for u in range(4):
                        o = PS[:, PX0 + u // 2, (u % 2) * 2 * P:(u % 2 + 1) * 2 * P]
                        if lv < LEVELS - 1:
                            mm(o[:, 0:P], XU[:, u, 1, :], P1s[:, u, :], start=True, stop=True)
                        ins = mm(o[:, P:2 * P], P1s[:, u, :], XU[:, u, 1, :], start=True, stop=True)
                    ins.then_inc(*G_pe.ends(f"P2_{lv}", g))
                pe.wait_ge(*G_dve.past(f"XU_{LEVELS - 1}", g))
                for j in range(2):
                    ins = mm(PS[:, P1B, j * P:(j + 1) * P], XU[:, j, 1, :], Vt[:, 0, j, :], start=True, stop=True)
                ins.then_inc(*G_pe.ends("vn0", g))
                z(11, 12)
                pe.wait_ge(*G_dve.past("vk1", g))
                mm(PS[:, GB, 0:T], kt0[:, :], vk[:, :, :], start=True, stop=True).then_inc(*G_pe.ends("S1", g))
                z(12, 13)
                pe.wait_ge(*G_act.past("S1", g))
                mm(PS[:, PX0, 0:T], QK[:, 1, 0, :], S1[:, :, :], start=True, stop=True).then_inc(*G_pe.ends("kS", g))
                z(13, 14)
                pe.wait_ge(*G_dve.past("r1", g))
                for j in range(2):
                    ins = mm(PS[:, PX0, T + j * P:T + (j + 1) * P], XU[:, 2 + j, 1, :], rr[:, j, :],
                             start=True, stop=True)
                ins.then_inc(*G_pe.ends("vn1", g))
                z(14, 16)
                pe.wait_ge(*G_dve.past("vn11", g))
                for j in range(2):
                    mm(PS[:, QKB, j * T:j * T + P], vn[:, 0, j, :], attT[:, 0, j, :], start=True, stop=True)
                    mm(PS[:, QKB, j * T + P:(j + 1) * T], S1[:, j, :], qd[:, j, :], start=True, stop=False)
                    ins = mm(PS[:, QKB, j * T + P:(j + 1) * T], vn[:, 1, j, :], attT[:, 1, j, :],
                             start=False, stop=True)
                ins.then_inc(*G_pe.ends("O", g))

            with pe.Fori(0, QKH - 1) as g:
                gdn_head(g, False)
            gdn_head(QKH - 1, True)
            pe.wait_ge(osq_ready, QKH + 1)
            norm_sums(4, osq, 0, Z_pe, "ss_o")
            pe.wait_ge(*Z_dve.past("diag_o"))
            mm(bank(PX1), ones, diag[:, :, :], start=True, stop=True).then_inc(*Z_pe.ends("bc_o"))

            with pe.Fori(0, KT) as j:
                pe.wait_ge(loaded[S_MIX[0]], 16 * (j + 1))
                pe.wait_ge(M_dve.sem, j * len(M_dve.names))
                pair(0, S_MIX[0]).then_inc(used[S_MIX[0]], 1)
                pe.wait_ge(loaded[S_MIX[1]], 16 * (j + 1))
                pe.wait_ge(*Z_dve.past("og"))
                for k in range(VH):
                    ins = mm(PS[:, 1, 0:T], ring16[:, S_MIX[1], k, :], og[:, k, :], start=(k == 0), stop=(k == VH - 1))
                ins.then_inc(used[S_MIX[1]], 1)
                pe.wait_ge(loaded[S_MIX[2]], 16 * (j + 1))
                pe.wait_ge(*Ct_dve.past("out"))
                for k in range(KT):
                    ins = mm(PS[:, 2, 0:T], ring16[:, S_MIX[2], k, :], rgo[:, k, :], start=(k == 0), stop=(k == KT - 1))
                ins.then_inc(used[S_MIX[2]], 1)

            pe.wait_ge(*M_dve.past("mix", KT - 1))
            for i in range(4):
                s = S_OUT[i]
                pe.wait_ge(loaded[s], 16 * fills[s])
                for kk in range(2):
                    k = 2 * i + kk
                    for n in range(NT):
                        for f in range(2):
                            ins = mm(PS[:, 4 + 2 * n + f, :], mixT[:, k, n * P:(n + 1) * P],
                                     ring2[:, s, kk, f * 512:(f + 1) * 512], start=(k == 0), stop=(k == KT - 1))
                ins.then_inc(used[s], 1)
            transposes(hn, O_pe, O_dve.past("hn1"), None, 0)
            pe.wait_ge(*O_dve.past("ev3"))
            for n in range(NT):
                for k in range(KT):
                    ins = mm(PS[:, 4, n * NE:(n + 1) * NE], xnT[:, k, n * P:(n + 1) * P], W_r[:, k, :],
                             start=(k == 0), stop=(k == KT - 1))
            ins.then_inc(*O_pe.ends("router"))
            pe.wait_ge(*O_dve.past("sel"))
            mm(PS[:, 5, 0:NE], tri_strict, sel_[:, 0, :], start=True, stop=True)
            mm(PS[:, 5, NE:2 * NE], ones, sel_[:, 0, :], start=True, stop=False)
            mm(PS[:, 5, NE:2 * NE], tri_strict, sel_[:, 1, :], start=False, stop=True)
            mm(PS[:, 5, 2 * NE:3 * NE], ones, sel_[:, 0, :], start=True, stop=False)
            mm(PS[:, 5, 2 * NE:3 * NE], ones, sel_[:, 1, :], start=False, stop=True).then_inc(*O_pe.ends("pos"))
            pe.wait_ge(*O_dve.past("gate1"))
            for n in range(NT):
                ins = tr(PS[0:NE, 6, n * P:(n + 1) * P], gate[:, n, :], ident)
            ins.then_inc(*O_pe.ends("trg"))
            pe.wait_ge(*O_act.past("gT"))
            pe.wait_ge(bdown_loaded, 16)
            for n in range(NT):
                for f in range(2):
                    ins = mm(PS[:, 2 * n + f, :], gT[:, n * P:(n + 1) * P], bdn[:, f * 512:(f + 1) * 512],
                             start=True, stop=True)
            ins.then_inc(*O_pe.ends("bd"))

            GATE, UP, XG, DN, SC = 0, 1, 2, 3, 4

            def gather(steps, sel_done, r):
                pe.wait_ge(*sel_done)
                for n in range(NT):
                    for half in range(2):
                        ins = mm(PS[half * CAP:(half + 1) * CAP, XG, :], Ssel[:, n, :],
                                 hn[:, n, half * 512:(half + 1) * 512], start=(n == 0), stop=(n == NT - 1))
                ins.then_inc(*steps.ends("gather", r))

            def tiles_turned(bank_, src, steps, name, r):
                for b in range(4):
                    ins = tr(PS[:, bank_, b * P:(b + 1) * P], src[:, b * P:(b + 1) * P], ident)
                ins.then_inc(*steps.ends(name, r))

            pe.wait_ge(*O_dve.past("b3"))
            n_it = pe.value_load(loops[0:1, 0:1], min_val=NE, max_val=4 * NE)
            gather(E_pe0, E_dve0.past("S1"), 0)
            pe.wait_ge(*E_act0.past("xg"))
            tiles_turned(SC + 1, xgs, E_pe0, "trX", 0)
            pe.wait_ge(*E_act0.past("xT"))
            pe.wait_ge(bgu_loaded, 16)
            with pe.Fori(0, n_it) as it:
                pe.wait_ge(onehot_ready, it + 1)
                for k in range(-1, KT):
                    if k >= 0:
                        pe.wait_ge(loaded[k], 16 * (fills[k] + 1) + 16 * it)
                    for t, bank_ in enumerate((GATE, UP)):
                        for half in range(2):
                            c0 = t * D + half * 512
                            if k < 0:
                                lhsT, rhs = onehot, bgu[:, c0:c0 + 512]
                            else:
                                lhsT, rhs = xT[:, k % 4, k // 4, :], ring[:, k, c0:c0 + 512]
                            ins = mm(PS[half * CAP:(half + 1) * CAP, bank_, :], lhsT, rhs,
                                     start=(k < 0), stop=(k == KT - 1))
                    if k >= 0:
                        ins.then_inc(used[k], 1)
                pe.wait_ge(E_dve.sem, E_dve.before + it * len(E_dve.names))
                for n in range(NT):
                    ins = tr(PS[:, SC, n * P:(n + 1) * P], SG[:, n, :], ident)
                ins.then_inc(*E_pe.ends("trS", it))
                gather(E_pe, E_dve.past("S1", it), it)
                pe.wait_ge(*E_dve.past("hid", it))
                tiles_turned(SC + 2, ehid, E_pe, "trH", it)
                pe.wait_ge(*E_act.past("xg", it))
                tiles_turned(SC + 1, xgs, E_pe, "trX", it)
                pe.wait_ge(*E_act.past("hidT", it))
                for f in range(FT):
                    s = FT + f // 2
                    if f % 2 == 0:
                        pe.wait_ge(loaded[s], 16 * (fills[s] + 1) + 16 * it)
                    for half in range(2):
                        ins = mm(PS[half * CAP:(half + 1) * CAP, DN, :], hidT[:, f % 4, f // 4, :],
                                 ring2[:, s, f % 2, half * 512:(half + 1) * 512], start=(f == 0), stop=(f == FT - 1))
                    if f % 2:
                        ins.then_inc(used[s], 1)
                pe.wait_ge(*E_act.past("Y", it))
                for n in range(NT):
                    for half in range(2):
                        ins = mm(PS[:, SC + 2 * n + half, :], ST[half * CAP:(half + 1) * CAP, n, :],
                                 Y[half * CAP:(half + 1) * CAP, :], start=True, stop=True)
                ins.then_inc(*E_pe.ends("scatter", it))

        @block.scalar
        def _(act):
            A = nc.scalar.activation
            act.dma_start(V[:, :], vec).then_inc(vec_loaded, 16)
            act.dma_start(R[:, :], row).then_inc(row_loaded, 16)
            act.dma_start(W_ba[:, :, :], w_ba[0]).then_inc(ba_loaded, 16)
            act.dma_start(W_r[:, :, :], w_ba[1]).then_inc(ba_loaded, 16)

            def flat(ap):
                return ap.rearrange("p a n -> p (a n)")

            def squares(src, steps):
                for n in range(NT):
                    A(flat(hn)[:, n * D:(n + 1) * D], src[:, n, :], ACT.Square,
                      accum_out=ss[:, 2, n:n + 1]).then_inc(*steps.ends(f"ss{n}"))

            act.wait_ge(x_loaded, 16)
            squares(h, A_act)
            act.wait_ge(*B_pe.past("ba"))
            A(tb.rearrange("p (n e) -> p n e", n=NT), PS[:, 4, 0:64].rearrange("p (n e) -> p n e", n=NT)[:, :, 0:VH],
              ACT.Tanh, scale=0.5).then_inc(*B_act.ends("tanh_b"))
            act.wait_ge(*B_dve.past("abs"))
            A(spy, spa, ACT.Exp, scale=-1.0).then_inc(*B_act.ends("exp_abs"))
            act.wait_ge(row_loaded, 16)
            A(exA, R[:, 48:64], ACT.Exp).then_inc(*B_act.ends("exp_A"))
            act.wait_ge(*B_dve.past("gc_last"))
            A(kdec[:, :], small[:, 0, 0:VH], ACT.Exp).then_inc(*B_act.ends("kdec"))
            A(small[:, 1, 0:32], gsum[:, :, :].rearrange("p a n -> p (a n)"), ACT.Exp).then_inc(*B_act.ends("eg"))

            with act.Fori(0, RGB) as i:
                act.wait_ge(used[S_RG[0]], i + 1)
                act.wait_ge(*A_dve.past("pad"))
                act.wait_ge(C_dve.sem, i * len(C_dve.names))
                A(rawp[:, 0:2, 3:3 + T], bank3(0, 2), ACT.Copy).then_inc(xy_copied, 1)
                act.wait_ge(used[S_RG[1]], i + 1)
                A(yraw[:, :, :], bank3(1, 2), ACT.Copy).then_inc(xy_copied, 1)
                act.wait_ge(xy_copied, 2 * i + 2)
                A(y2b[:, :, :], yraw[:, :, :], ACT.Square).then_inc(*C_act.ends("y2"))
                act.wait_ge(*C_dve.past("cub_y", i))
                A(ty[:, :, :], q3[:, :, :], ACT.Tanh, scale=GELU_C).then_inc(*C_act.ends("tanh_y"))
                act.wait_ge(used[S_RG[2]], i + 1)
                act.wait_ge(*B_dve.past("hb"))
                for gate_i, (dst, name) in enumerate(((ta, "tanh_a"), (ti, "tanh_i"))):
                    for jt in range(2):
                        ins = A(dst[:, jt, :], PS[:, 2 + gate_i, jt * T:(jt + 1) * T], ACT.Tanh, scale=0.5,
                                bias=hb[:, bass.ds(2 * i + gate_i * KT + jt, 1)])
                    ins.then_inc(*C_act.ends(name))
                act.wait_ge(*C_dve.past("l1", i))
                A(arg[:, bass.ds(2 * i, 2), :], L[:, :, :], ACT.Exp, scale=-1.0).then_inc(*C_act.ends("decay"))
                A(ta[:, :, :], L[:, :, :], ACT.Tanh).then_inc(*C_act.ends("tanh_l"))
            act.wait_ge(used[S_GDN[0]], 1)
            act.wait_ge(*C_dve.past("gelu", RGB - 1))
            A(rawp[:, 0:2, 3:3 + T], bank3(0, 2), ACT.Copy).then_inc(qk_copied, 1)
            act.wait_ge(used[S_GDN[1]], 1)
            A(rawp[:, 2:4, 3:3 + T], bank3(1, 2), ACT.Copy).then_inc(v_copied, 1)
            act.wait_ge(*C_dve.past("guard", RGB - 1))
            A(mrg, mrg, ACT.Sqrt).then_inc(*Ct_act.ends("sqrt"))
            act.wait_ge(used[S_GDN[2]], 1)
            A(zraw[:, :, :], bank3(0, 2), ACT.Copy).then_inc(z_copied, 1)
            act.wait_ge(ow_zero, 1)
            A(osq[:, :, :], ow[:, :, :], ACT.Square).then_inc(osq_ready, 1)

            def gdn_head(g, final):
                act.wait_ge(*G_dve.past("cqk7", g))
                A(thq[:, :, :], cqk[:, :, :], ACT.Tanh, scale=0.5).then_inc(*G_act.ends("tanh_qk", g))
                act.wait_ge(*G_dve.past("s_qk", g))
                A(thq[:, :, :], cqk[:, :, :], ACT.Square, scale=0.5).then_inc(*G_act.ends("sq_qk", g))
                act.wait_ge(*G_dve.past("cv7", g))
                A(thv[:, :, :], cv[:, :, :], ACT.Tanh, scale=0.5).then_inc(*G_act.ends("tanh_v", g))
                act.wait_ge(z_copied, g + 1)
                A(zs[:, :, :], zraw[:, :, :], ACT.Tanh, scale=0.5).then_inc(*G_act.ends("tanh_z", g))
                if not final:
                    act.wait_ge(used[S_GDN[0]], g + 2)
                    A(rawp[:, 0:2, 3:3 + T], bank3(0, 2), ACT.Copy).then_inc(qk_copied, 1)
                    act.wait_ge(used[S_GDN[1]], g + 2)
                    A(rawp[:, 2:4, 3:3 + T], bank3(1, 2), ACT.Copy).then_inc(v_copied, 1)
                act.wait_ge(*G_pe.past("G", g))
                A(eG[:, :, :], bank3(6, 2)[:, :, P:2 * P], ACT.Exp).then_inc(*G_act.ends("eG", g))
                act.wait_ge(*G_pe.past("trv", g))
                A(Vt[:, :, :, :].rearrange("p a b c -> p (a b c)"), bank(2), ACT.Copy, scale=0.5)\
                    .then_inc(*G_act.ends("Vt", g))
                act.wait_ge(*G_dve.past("D3", g))
                A(Dt[:, :, :, :], Dt[:, :, :, :], ACT.Exp).then_inc(*G_act.ends("Dt", g))
                act.wait_ge(*G_pe.past("trU", g))
                A(XU[:, :, 0, :], bank3(2, 4), ACT.Copy).then_inc(*G_act.ends("X", g))
                for lv in range(1, LEVELS):
                    act.wait_ge(*G_pe.past(f"P1_{lv}", g))
                    A(P1s[:, :, :], bank3(2, 4), ACT.Copy).then_inc(*G_act.ends(f"P1s_{lv}", g))
                act.wait_ge(*G_pe.past("S1", g))
                A(flat(S1[:, :, :]), PS[:, 6, 0:T], ACT.Copy).then_inc(*G_act.ends("S1", g))
                act.wait_ge(*G_pe.past("O", g))
                A(osq[:, :, :], bank3(5, 2), ACT.Square).then_inc(osq_ready, 1)
                if not final:
                    act.wait_ge(used[S_GDN[2]], g + 2)
                    act.wait_ge(*G_dve.past("s_z", g))
                    A(zraw[:, :, :], bank3(0, 2), ACT.Copy).then_inc(z_copied, 1)

            with act.Fori(0, QKH - 1) as g:
                gdn_head(g, False)
            gdn_head(QKH - 1, True)

            with act.Fori(0, KT) as j:
                act.wait_ge(used[S_MIX[0]], j + 1)
                act.wait_ge(M_dve.sem, j * len(M_dve.names))
                A(thq[:, :, :], bank3(0, 2), ACT.Tanh, scale=0.5).then_inc(*M_act.ends("tanh"))
            act.wait_ge(used[S_OUT[3]], fills[S_OUT[3]])
            act.dma_start(rows, ffn_rows).then_inc(rows_loaded, 16)
            act.dma_start(bdn[:, :], b_down).then_inc(bdown_loaded, 16)
            act.wait_ge(*O_dve.past("h3"))
            squares(h, O_act)
            act.wait_ge(*O_dve.past("negm"))
            for n in range(NT):
                A(exs[:, n, :], logits[:, n, :], ACT.Exp, bias=negm[:, n:n + 1]).then_inc(*O_act.ends(f"exp{n}"))
            act.dma_start(bgu, b_gu).then_inc(bgu_loaded, 16)
            act.wait_ge(*O_pe.past("trg"))
            A(gT[:, :], PS[0:NE, 6, 0:T], ACT.Copy).then_inc(*O_act.ends("gT"))

            act.wait_ge(*O_dve.past("loops"))
            n_it = act.value_load(loops[0:1, 0:1], min_val=NE, max_val=4 * NE)

            act.wait_ge(*E_pe0.past("gather"))
            A(xgs, bank(2), ACT.Copy).then_inc(*E_act0.ends("xg"))
            act.wait_ge(*E_pe0.past("trX"))
            A(flat(cqk[:, :, :]), bank(5), ACT.Copy).then_inc(*E_act0.ends("xT"))
            with act.Fori(0, n_it) as it:
                act.wait_ge(*E_dve.past("g", it))
                A(eth, eg_, ACT.Tanh, scale=0.5 * ALPHA).then_inc(*E_act.ends("th", it))
                act.wait_ge(*E_pe.past("trS", it))
                A(flat(ST), PS[:, 4, 0:T], ACT.Copy).then_inc(*E_act.ends("ST", it))
                act.wait_ge(*E_pe.past("gather", it))
                A(xgs, bank(2), ACT.Copy).then_inc(*E_act.ends("xg", it))
                act.wait_ge(*E_pe.past("trH", it))
                A(flat(cv[:, :, :]), bank(6), ACT.Copy).then_inc(*E_act.ends("hidT", it))
                act.wait_ge(*E_pe.past("trX", it))
                A(flat(cqk[:, :, :]), bank(5), ACT.Copy).then_inc(*E_act.ends("xT", it))
                act.wait_ge(used[NSLOT - 1], fills[NSLOT - 1] + 1 + it)
                A(Y, bank(3), ACT.Copy, scale=0.5).then_inc(*E_act.ends("Y", it))

            act.wait_ge(E_dve.sem, E_dve.before + n_it * len(E_dve.names))
            squares(h, F_act)

        @block.vector
        def _(dve):
            v = nc.vector

            def convolution(src, dst, tap, bias, steps, names, r):
                if bias is None:
                    ins = v.tensor_scalar(dst, src[:, 3:3 + T], tap(3), None, ALU.mult)
                else:
                    ins = v.tensor_scalar(dst, src[:, 3:3 + T], tap(3), bias, ALU.mult, ALU.add)
                ins.then_inc(*steps.ends(names[0], r))
                for j in range(3):
                    dve.wait_ge(*steps.past(names[j], r))
                    v.scalar_tensor_tensor(dst, src[:, j:j + T], tap(j), dst, ALU.mult, ALU.add)\
                        .then_inc(*steps.ends(names[j + 1], r))

            v.memset(half_pow[:, :], -0.5).then_inc(*A_dve.ends("pow"))
            dve.wait_ge(*A_act.past("ss1"))
            v.tensor_scalar(ss[:, 3, 0:2], ss[:, 2, 0:2], 1.0 / D, EPS, ALU.mult, ALU.add).then_inc(*A_dve.ends("ms"))
            v.memset(rawp[:, :, 0:3], 0.0).then_inc(*A_dve.ends("pad"))
            dve.wait_ge(*A_pool.past("rstd"))
            for n in range(NT):
                v.tensor_scalar(hn[:, n, :], h[:, n, :], ss[:, 1, n:n + 1], None, ALU.mult)\
                    .then_inc(*A_dve.ends(f"xn{n}"))
            dve.wait_ge(vec_loaded, 16)
            for b in range(4):
                dve.wait_ge(*A_pe.past(f"tr{b}"))
                v.tensor_tensor(xnT[:, 2 * b:2 * b + 2, :], bank3(b, 2), last(V[:, 2 * b:2 * b + 2], T), ALU.mult)\
                    .then_inc(*A_dve.ends(f"ev{b}"))

            B = B_dve
            dve.wait_ge(row_loaded, 16)
            dve.wait_ge(*B_act.past("tanh_b"))
            zb = PS[:, 4, 0:64].rearrange("p (n e) -> p n e", n=NT)
            v.tensor_tensor(spx[:, 0:32].rearrange("p (n e) -> p n e", n=NT), zb[:, :, VH:2 * VH], mid(R[:, 32:48], NT), ALU.add)\
                .then_inc(*B.ends("in_ba"))
            o, w = VEC["lam"]
            v.tensor_scalar(spx[:, 32:40], V[:, o:o + w], -1.0, None, ALU.mult).then_inc(*B.ends("in_lam"))
            dve.wait_ge(*B.past("in_lam"))
            v.scalar_tensor_tensor(spa, spx, -1.0, spx, ALU.mult, ALU.max).then_inc(*B.ends("abs"))
            dve.wait_ge(*B_act.past("exp_abs"))
            v.tensor_scalar(spp, spy, 2.0, None, ALU.add).then_inc(*B.ends("y2"))
            dve.wait_ge(*B.past("y2"))
            v.reciprocal(spa, spp).then_inc(*B.ends("s_rec"))
            dve.wait_ge(*B.past("s_rec"))
            v.tensor_tensor(sps, spy, spa, ALU.mult).then_inc(*B.ends("s"))
            dve.wait_ge(*B.past("s"))
            v.tensor_tensor(sps2, sps, sps, ALU.mult).then_inc(*B.ends("s2"))
            dve.wait_ge(*B.past("s2"))
            v.tensor_scalar(spp, sps2, 2.0 / 15, 2.0 / 13, ALU.mult, ALU.add).then_inc(*B.ends("p6"))
            dve.wait_ge(*B.past("p6"))
            for i in range(5, 0, -1):
                v.tensor_tensor(spp, spp, sps2, ALU.mult).then_inc(*B.ends(f"p{i}"))
                dve.wait_ge(*B.past(f"p{i}"))
                v.tensor_scalar(spp, spp, 2.0 / (2 * i + 1), None, ALU.add).then_inc(poly, 1)
                dve.wait_ge(poly, 6 - i)
            v.tensor_tensor(spp, spp, sps2, ALU.mult).then_inc(*B.ends("p0"))
            dve.wait_ge(*B.past("p0"))
            v.scalar_tensor_tensor(spp, spp, 2.0, sps, ALU.add, ALU.mult).then_inc(*B.ends("pos"))
            dve.wait_ge(*B.past("pos"))
            v.scalar_tensor_tensor(sps2, spx, 0.0, spp, ALU.max, ALU.add).then_inc(*B.ends("sp"))
            dve.wait_ge(*B.past("sp"))
            v.tensor_scalar(sp4[:, :], sps2[:, 32:40], RG_C / 2, None, ALU.mult).then_inc(*B.ends("sp4"))
            oa, _ = VEC["ba"]
            v.tensor_scalar(hb[:, :], V[:, oa:oa + 2 * KT], 0.5, None, ALU.mult).then_inc(*B.ends("hb"))
            dve.wait_ge(*B_act.past("tanh_b"))
            v.tensor_scalar(beta[:, :, :].rearrange("p a n -> p (a n)"), tb, 0.5, 0.5, ALU.mult, ALU.add)\
                .then_inc(*B.ends("beta"))
            dve.wait_ge(*B_act.past("exp_A"))
            v.scalar_tensor_tensor(gcol[:, :, :], sps2[:, 0:32].rearrange("p (n e) -> p n e", n=NT), -1.0,
                                   mid(exA, NT), ALU.mult, ALU.mult).then_inc(*B.ends("g"))
            dve.wait_ge(*B_pe.past("cum"))
            v.tensor_copy(gsum[:, :, :].rearrange("p a n -> p (a n)"), PS[:, 5, 0:32]).then_inc(*B.ends("gc"))
            dve.wait_ge(*B.past("gc"))
            v.tensor_tensor(small[:, 0, 0:VH], PS[:, 5, 32:48], gsum[:, 0, :], ALU.subtract)\
                .then_inc(*B.ends("gc_last"))
            dve.wait_ge(*B_act.past("eg"))
            v.tensor_scalar(negeg[:, :, :].rearrange("p a n -> p (a n)"), small[:, 1, 0:32], -1.0, None, ALU.mult)\
                .then_inc(*B.ends("negeg"))
            dve.wait_ge(*B_pe.past("tr"))
            v.tensor_copy(gcT[:, :], PS[0:VH, 6, 0:T]).then_inc(*B.ends("gcT"))

            with dve.Fori(0, RGB) as i:
                S = C_dve
                dve.wait_ge(xy_copied, 2 * i + 1)
                dve.wait_ge(used[S_RG[2]], i)
                for t in range(2):
                    convolution(rawp[:, t, :], xa[:, t, :], lambda j: vcol("rg_cw", j * KT + 2 * i + t),
                                vcol("rg_cb", 2 * i + t), S, [f"conv{4 * t + j}" for j in range(4)], i)
                dve.wait_ge(*C_act.past("y2", i))
                v.tensor_scalar(q3[:, :, :], y2b[:, :, :], GELU_A, 1.0, ALU.mult, ALU.add).then_inc(*S.ends("cub"))
                dve.wait_ge(*S.past("cub", i))
                v.tensor_tensor(q3[:, :, :], q3[:, :, :], yraw[:, :, :], ALU.mult).then_inc(*S.ends("cub_y"))
                dve.wait_ge(*C_act.past("tanh_a", i))
                for jt in range(2):
                    v.tensor_scalar(L[:, jt, :], ta[:, jt, :], 1.0, sp4[:, bass.ds(2 * i + jt, 1)], ALU.add, ALU.mult)\
                        .then_inc(*S.ends(f"l{jt}"))
                dve.wait_ge(*C_act.past("tanh_i", i))
                v.scalar_tensor_tensor(rgo[:, bass.ds(2 * i, 2), :], ti[:, :, :], 1.0, xa[:, :, :], ALU.add, ALU.mult)\
                    .then_inc(*S.ends("gated"))
                dve.wait_ge(*C_act.past("tanh_l", i))
                a_i, m_i = arg[:, bass.ds(2 * i, 2), :], mrg[:, bass.ds(2 * i, 2), :]
                v.tensor_tensor(m_i, a_i, a_i, ALU.mult).then_inc(*S.ends("dec2"))
                dve.wait_ge(*S.past("dec2", i))
                v.scalar_tensor_tensor(m_i, m_i, 1.0, ta[:, :, :], ALU.add, ALU.mult).then_inc(*S.ends("mult"))
                dve.wait_ge(*S.past("mult", i))
                v.tensor_scalar(m_i, m_i, 0.0, None, ALU.max).then_inc(*S.ends("guard"))
                dve.wait_ge(*C_act.past("tanh_y", i))
                v.scalar_tensor_tensor(mixT[:, bass.ds(2 * i, 2), :], ty[:, :, :], 1.0, yraw[:, :, :],
                                       ALU.add, ALU.mult).then_inc(*S.ends("gelu"))
            S = Ct_dve
            dve.wait_ge(*C_dve.past("gelu", RGB - 1))
            v.memset(ow[:, :, :], 0.0).then_inc(ow_zero, 1)
            dve.wait_ge(*Ct_act.past("sqrt"))
            v.memset(mrg[:, :, 0:1], 1.0).then_inc(*S.ends("first"))
            dve.wait_ge(*S.past("first"))
            v.scalar_tensor_tensor(rgo[:, :, :], rgo[:, :, :], 0.5, mrg, ALU.mult, ALU.mult).then_inc(*S.ends("b"))
            dve.wait_ge(*S.past("b"))
            for k in range(KT):
                v.tensor_tensor_scan(mrg[:, k, :], arg[:, k, :], rgo[:, k, :], 0.0, ALU.mult, ALU.add)\
                    .then_inc(*S.ends(f"scan{k}"))
            dve.wait_ge(*S.past(f"scan{KT - 1}"))
            v.scalar_tensor_tensor(rgo[:, :, :], mixT[:, :, :], 0.5, mrg, ALU.mult, ALU.mult).then_inc(*S.ends("out"))
            dve.wait_ge(*S.past("out"))

            def out_norm(steps, pe_steps, pool_steps, g, r):
                dve.wait_ge(*pe_steps.past("ss_o", r))
                v.tensor_scalar(ss[:, 0, :], PS[:, 7, 4:8], 1.0 / DK, EPS, ALU.mult, ALU.add)\
                    .then_inc(*steps.ends("ss_o", r))
                dve.wait_ge(*pool_steps.past("r_o", r))
                v.tensor_tensor(diag[:, :, :], mid(con_("ident_half"), 4), last(ss[:, 1, :], P), ALU.mult)\
                    .then_inc(*steps.ends("diag_o", r))
                dve.wait_ge(*pe_steps.past("bc_o", r))
                v.tensor_tensor(og[:, bass.ds(g, 2), :], ow[:, :, :], bank3(4, 2), ALU.mult)\
                    .then_inc(*steps.ends("og", r))

            def gdn_head(g, g_before):
                S = G_dve
                dve.wait_ge(qk_copied, g + 1)
                for t in range(2):
                    convolution(rawp[:, t, :], cqk[:, t, :], lambda j: vcol("gdn_cw", (g * 4 + t) * 4 + j),
                                None, S, [f"cqk{4 * t + j}" for j in range(4)], g)
                dve.wait_ge(*G_act.past("tanh_qk", g))
                v.scalar_tensor_tensor(cqk[:, :, :], thq[:, :, :], 1.0, cqk[:, :, :], ALU.add, ALU.mult)\
                    .then_inc(*S.ends("s_qk", g))
                dve.wait_ge(v_copied, g + 1)
                for t in range(2):
                    convolution(rawp[:, 2 + t, :], cv[:, t, :], lambda j: vcol("gdn_cw", (g * 4 + 2 + t) * 4 + j),
                                None, S, [f"cv{4 * t + j}" for j in range(4)], g)
                out_norm(S, G_pe, G_pool, g_before, g)
                v.tensor_tensor(rowsel[:, :, :], mid(gcT[:, :], 2),
                                last(C[0:VH, bass.ds(CON["ident"][0] + 2 * g, 2)], T), ALU.mult)\
                    .then_inc(*S.ends("rowsel", g))
                dve.wait_ge(*G_pe.past("ss_qk", g))
                v.tensor_scalar(ss[:, 2, :], PS[:, 7, 0:4], EPS, None, ALU.add).then_inc(*S.ends("ss_qk", g))
                dve.wait_ge(*G_pool.past("r_qk", g))
                v.tensor_tensor(diag[:, :, :], con_("ident_qk", 0, 4 * P).rearrange("p (a n) -> p a n", a=4),
                                last(ss[:, 3, :], P), ALU.mult).then_inc(*S.ends("diag_qk", g))
                dve.wait_ge(*G_act.past("tanh_v", g))
                v.scalar_tensor_tensor(cv[:, :, :], thv[:, :, :], 1.0, cv[:, :, :], ALU.add, ALU.mult)\
                    .then_inc(*S.ends("s_v", g))
                dve.wait_ge(*G_act.past("tanh_z", g))
                v.scalar_tensor_tensor(zs[:, :, :], zs[:, :, :], 1.0, zraw[:, :, :], ALU.add, ALU.mult)\
                    .then_inc(*S.ends("s_z", g))
                dve.wait_ge(*G_pe.past("bc_qk", g))
                v.tensor_tensor(QK[:, :, :, :].rearrange("p n w c -> p w n c"),
                                cqk[:, :, :].rearrange("p w (n c) -> p w n c", n=NT),
                                bank(3).rearrange("p (w n c) -> p w n c", n=NT, w=2), ALU.mult)\
                    .then_inc(*S.ends("QK", g))
                dve.wait_ge(*G_pe.past("trk", g))
                v.tensor_copy(kt0[:, :], PS[:, 7, P:2 * P]).then_inc(*S.ends("kt0", g))
                dve.wait_ge(*G_act.past("eG", g))
                for n in range(NT):
                    for j in range(2):
                        v.scalar_tensor_tensor(Dt[:, n, j, :], PS[:, 6, j * T + n * P:j * T + (n + 1) * P],
                                               gsum[:, n, bass.ds(2 * g + j, 1)], neg, ALU.subtract, ALU.add)\
                            .then_inc(*S.ends(f"D{2 * n + j}", g))
                v.tensor_tensor(qd[:, :, :], eG[:, :, :], mid(QK[:, 1, 1, :], 2), ALU.mult).then_inc(*S.ends("qd", g))
                dve.wait_ge(*G_act.past("Dt", g))
                kkqk = bank(5).rearrange("p (n w c) -> p n w c", n=NT, w=2)
                for n in range(NT):
                    for j in range(2):
                        v.scalar_tensor_tensor(MT[:, n, j, :], Dt[:, n, j, :], beta[:, n, bass.ds(2 * g + j, 1)],
                                               kkqk[:, n, 0, :], ALU.mult, ALU.mult)\
                            .then_inc(*S.ends(f"M{2 * n + j}", g))
                v.tensor_tensor(attT[:, :, :, :], Dt[:, :, :, :],
                                kkqk[:, :, 1, :].unsqueeze(2).broadcast_to([P, NT, 2, P]), ALU.mult)\
                    .then_inc(*S.ends("att", g))
                dve.wait_ge(*G_pool.past("MM0", g))
                v.tensor_tensor(XU[:, :, 1, :], mid(ident, 4), MM[:, 0, :, :], ALU.subtract).then_inc(*S.ends("U", g))
                px = PS[:, 3:5, :].rearrange("p b (u w c) -> p (b u) w c", u=2, w=2)
                for lv in range(1, LEVELS):
                    dve.wait_ge(*G_pe.past(f"P2_{lv}", g))
                    if lv == 1:
                        dve.wait_ge(*S.past("U", g))
                    else:
                        dve.wait_ge(*S.past(f"XU_{lv - 1}", g))
                    if lv < LEVELS - 1:
                        v.tensor_tensor(XU[:, :, :, :], XU[:, :, :, :], px, ALU.subtract)\
                            .then_inc(*S.ends(f"XU_{lv}", g))
                    else:
                        v.tensor_tensor(XU[:, :, 1, :], XU[:, :, 1, :], px[:, :, 1, :], ALU.subtract)\
                            .then_inc(*S.ends(f"XU_{lv}", g))
                dve.wait_ge(*G_pe.past("vn0", g))
                for j in range(2):
                    v.tensor_scalar(vk[:, j, :], PS[:, 2, j * P:(j + 1) * P], beta[:, 0, bass.ds(2 * g + j, 1)],
                                    kdec[:, bass.ds(2 * g + j, 1)], ALU.mult, ALU.mult).then_inc(*S.ends(f"vk{j}", g))
                for j in range(2):
                    v.tensor_scalar(vn[:, 0, j, :], PS[:, 2, j * P:(j + 1) * P], beta[:, 0, bass.ds(2 * g + j, 1)],
                                    None, ALU.mult).then_inc(*S.ends(f"vn0{j}", g))
                dve.wait_ge(*G_pe.past("kS", g))
                for j in range(2):
                    v.scalar_tensor_tensor(rr[:, j, :], PS[:, 3, j * P:(j + 1) * P], negeg[:, 1, bass.ds(2 * g + j, 1)],
                                           Vt[:, 1, j, :], ALU.mult, ALU.add).then_inc(*S.ends(f"r{j}", g))
                dve.wait_ge(*G_pe.past("vn1", g))
                for j in range(2):
                    v.tensor_scalar(vn[:, 1, j, :], PS[:, 3, T + j * P:T + (j + 1) * P],
                                    beta[:, 1, bass.ds(2 * g + j, 1)], None, ALU.mult).then_inc(*S.ends(f"vn1{j}", g))
                dve.wait_ge(osq_ready, g + 2)
                dve.wait_ge(*S.past("s_z", g))
                v.scalar_tensor_tensor(ow[:, :, :], bank3(5, 2), vcol("gdn_norm", 0), zs[:, :, :], ALU.mult, ALU.mult)\
                    .then_inc(*S.ends("ow", g))
                dve.wait_ge(*S.past("ow", g))

            with dve.Fori(0, QKH - 1) as g:
                gdn_head(g, (g + (QKH - 1)) % QKH * 2)
            gdn_head(QKH - 1, 2 * (QKH - 2))
            out_norm(Z_dve, Z_pe, Z_pool, 2 * (QKH - 1), 0)

            with dve.Fori(0, KT) as j:
                S = M_dve
                dve.wait_ge(*M_act.past("tanh", j))
                dve.wait_ge(used[S_MIX[1]], j + 1)
                v.scalar_tensor_tensor(thv[:, 0, :], thq[:, 1, :], 1.0, PS[:, 1, 0:T], ALU.add, ALU.mult)\
                    .then_inc(*S.ends("a"))
                dve.wait_ge(used[S_MIX[2]], j + 1)
                v.scalar_tensor_tensor(thv[:, 1, :], thq[:, 0, :], 1.0, PS[:, 2, 0:T], ALU.add, ALU.mult)\
                    .then_inc(*S.ends("b"))
                dve.wait_ge(*S.past("b", j))
                v.tensor_tensor(mixT[:, bass.ds(j, 1), :].rearrange("p a n -> p (a n)"), thv[:, 0, :], thv[:, 1, :],
                                ALU.add).then_inc(*S.ends("mix"))

            S = O_dve

            def step(name):
                dve.wait_ge(*S.past(name))

            dve.wait_ge(used[S_OUT[3]], fills[S_OUT[3]])
            for i in range(4):
                n, f = i // 2, i % 2
                hh = h[:, n, f * 512:(f + 1) * 512]
                v.scalar_tensor_tensor(hh, bank(4 + i), 0.5, hh, ALU.mult, ALU.add).then_inc(*S.ends(f"h{i}"))
            dve.wait_ge(*O_act.past("ss1"))
            v.tensor_scalar(ss[:, 3, 0:2], ss[:, 2, 0:2], 1.0 / D, EPS, ALU.mult, ALU.add).then_inc(*S.ends("ms"))
            dve.wait_ge(*O_pool.past("rstd"))
            dve.wait_ge(rows_loaded, 16)
            for n in range(NT):
                v.scalar_tensor_tensor(hn[:, n, :], h[:, n, :], ss[:, 1, n:n + 1], rows[:, 0, :], ALU.mult, ALU.mult)\
                    .then_inc(*S.ends(f"hn{n}"))
            for b in range(4):
                dve.wait_ge(*O_pe.past(f"tr{b}"))
                v.tensor_copy(xnT[:, 2 * b:2 * b + 2, :], bank3(b, 2)).then_inc(*S.ends(f"ev{b}"))
            dve.wait_ge(*O_pe.past("router"))
            v.tensor_tensor(logits, PS[:, 4, 0:2 * NE].rearrange("p (n e) -> p n e", n=NT), mid(R[:, 0:NE], NT),
                            ALU.add).then_inc(*S.ends("logits"))
            step("logits")
            for n in range(NT):
                v.max(mx8[:, n, :], logits[:, n, :]).then_inc(*S.ends(f"max{n}"))
            step("max1")
            v.tensor_scalar(negm, mx8[:, :, 0], -1.0, None, ALU.mult).then_inc(*S.ends("negm"))
            for n in range(NT):
                v.tensor_scalar(gt[:, n, :], logits[:, n, :], mx8[:, n, TOP - 1:TOP], None, ALU.is_gt)\
                    .then_inc(*S.ends(f"gt{n}"))
            step("gt1")
            v.tensor_reduce(ngt, gt, AX, ALU.add).then_inc(*S.ends("ngt"))
            for n in range(NT):
                v.tensor_scalar(eq[:, n, :], logits[:, n, :], mx8[:, n, TOP - 1:TOP], None, ALU.is_equal)\
                    .then_inc(*S.ends(f"eq{n}"))
            step("ngt")
            v.tensor_scalar(need, ngt, -1.0, float(TOP), ALU.mult, ALU.add).then_inc(*S.ends("need"))
            step("eq1")
            for n in range(NT):
                v.tensor_tensor_scan(cum[:, n, :], ones[:, 0:NE], eq[:, n, :], 0.0, ALU.mult, ALU.add)\
                    .then_inc(*S.ends(f"cum{n}"))
            step("cum1")
            for n in range(NT):
                v.tensor_scalar(ok[:, n, :], cum[:, n, :], need[:, n:n + 1], None, ALU.is_le)\
                    .then_inc(*S.ends(f"ok{n}"))
            step("ok1")
            v.tensor_tensor(eq, eq, ok, ALU.mult).then_inc(*S.ends("eqok"))
            step("eqok")
            v.tensor_tensor(sel_, gt, eq, ALU.add).then_inc(*S.ends("sel"))
            step("sel")
            dve.wait_ge(*O_act.past("exp1"))
            v.tensor_tensor(exs, exs, sel_, ALU.mult).then_inc(*S.ends("exs"))
            step("exs")
            v.tensor_reduce(gsm, exs, AX, ALU.add).then_inc(*S.ends("sum"))
            step("sum")
            v.reciprocal(grec, gsm).then_inc(*S.ends("rec"))
            step("rec")
            for n in range(NT):
                v.tensor_scalar(gate[:, n, :], exs[:, n, :], grec[:, n:n + 1], None, ALU.mult)\
                    .then_inc(*S.ends(f"gate{n}"))
            dve.wait_ge(*O_pe.past("pos"))
            v.scalar_tensor_tensor(posm, PS[:, 5, 0:2 * NE].rearrange("p (n e) -> p n e", n=NT), 1.0, sel_,
                                   ALU.add, ALU.mult).then_inc(*S.ends("pos1"))
            step("pos1")
            v.tensor_scalar(posm, posm, -1.0, None, ALU.add).then_inc(*S.ends("posm"))
            v.tensor_reduce(cmax, PS[:, 5, 2 * NE:3 * NE], AX, ALU.max).then_inc(*S.ends("cmax"))
            step("cmax")
            for c_, k in ((c64, 1), (c128, 2), (c192, 3)):
                v.tensor_scalar(c_, cmax, float(CAP * k), float(NE), ALU.is_gt, ALU.mult)\
                    .then_inc(*S.ends(f"c{CAP * k}"))
            step("c192")
            v.tensor_tensor(c64, c64, c128, ALU.add).then_inc(*S.ends("csum"))
            step("csum")
            v.tensor_tensor(c64, c64, c192, ALU.add).then_inc(*S.ends("csum2"))
            step("csum2")
            v.tensor_scalar(loops[:, :], c64, float(NE), None, ALU.add).then_inc(*S.ends("loops"))
            step("loops")
            dve.wait_ge(*O_pe.past("bd"))
            for i in range(4):
                n, f = i // 2, i % 2
                hh = h[:, n, f * 512:(f + 1) * 512]
                v.tensor_tensor(hh, hh, bank(i), ALU.add).then_inc(*S.ends(f"b{i}"))

            n_it = dve.value_load(loops[0:1, 0:1], min_val=NE, max_val=4 * NE)

            def select(steps, e, r):
                for n in range(NT):
                    v.tensor_scalar(Ssel[:, n, :], con_("slots", 0, CAP), posm[:, n, bass.ds(e, 1)], None,
                                    ALU.is_equal).then_inc(*steps.ends(f"S{n}", r))

            def select_weighted(steps, e, r):
                for n in range(NT):
                    v.tensor_scalar(SG[:, n, :], con_("slots", 0, 2 * CAP), posm[:, n, bass.ds(e, 1)],
                                    gate[:, n, bass.ds(e, 1)], ALU.is_equal, ALU.mult)\
                        .then_inc(*steps.ends(f"SG{n}", r))
                v.tensor_scalar(onehot, ones[0:NE, 0:CAP], C[0:NE, bass.ds(e + CON["ident"][0], 1)], None, ALU.mult)\
                    .then_inc(onehot_ready, 1)
                dve.wait_ge(*steps.past("SG1", r))
                v.tensor_scalar(posm[:, :, bass.ds(e, 1)], posm[:, :, bass.ds(e, 1)], -float(CAP), None, ALU.add)\
                    .then_inc(*steps.ends("next", r))

            step("b3")
            select(E_dve0, 0, 0)
            select_weighted(E_dve0, 0, 0)
            with dve.Fori(0, n_it) as it:
                S = E_dve
                dve.wait_ge(onehot_ready, it + 1)
                dve.wait_ge(E_dve.sem, E_dve.before + it * len(E_dve.names))
                dve.wait_ge(E_pe.sem, E_pe.before + it * len(E_pe.names))
                select(S, (it + 1) % NE, it)
                dve.wait_ge(used[KT - 1], fills[KT - 1] + 1 + it)
                v.tensor_scalar(eg_, bank(0), LIMIT, None, ALU.min).then_inc(*S.ends("g", it))
                v.tensor_scalar(eu, bank(1), LIMIT, -LIMIT, ALU.min, ALU.max).then_inc(*S.ends("u", it))
                dve.wait_ge(*S.past("u", it))
                v.scalar_tensor_tensor(ehid, eu, 1.0, eg_, ALU.add, ALU.mult).then_inc(*S.ends("p", it))
                dve.wait_ge(*S.past("p", it))
                dve.wait_ge(*E_act.past("th", it))
                v.scalar_tensor_tensor(ehid, eth, 1.0, ehid, ALU.add, ALU.mult).then_inc(*S.ends("hid", it))
                dve.wait_ge(*E_pe.past("trS", it))
                select_weighted(S, (it + 1) % NE, it)
                dve.wait_ge(*E_pe.past("scatter", it))
                for i in range(4):
                    n, f = i // 2, i % 2
                    hh = h[:, n, f * 512:(f + 1) * 512]
                    v.tensor_tensor(hh, hh, bank(4 + i), ALU.add).then_inc(*S.ends(f"y{i}", it))
            dve.wait_ge(E_dve.sem, E_dve.before + n_it * len(E_dve.names))

            S = F_dve
            dve.wait_ge(*F_act.past("ss1"))
            v.tensor_scalar(ss[:, 3, 0:2], ss[:, 2, 0:2], 1.0 / D, EPS, ALU.mult, ALU.add).then_inc(*S.ends("ms"))
            dve.wait_ge(*F_pool.past("rstd"))
            for n in range(NT):
                v.scalar_tensor_tensor(hn[:, n, :], h[:, n, :], ss[:, 1, n:n + 1], rows[:, 1, :], ALU.mult, ALU.mult)\
                    .then_inc(*S.ends(f"o{n}"))

        @block.gpsimd
        def _(pool):
            tt = nc.gpsimd.tensor_tensor

            def rsqrt(dst, src, n, ends):
                tt(dst[:, 0:n], src[:, 0:n], half_pow[:, 0:n], ALU.pow).then_inc(*ends)

            pool.wait_ge(*A_dve.past("ms"))
            rsqrt(ss[:, 1, :], ss[:, 3, :], 2, A_pool.ends("rstd"))

            def gdn_head(g):
                pool.wait_ge(*G_dve.past("ss_o", g))
                rsqrt(ss[:, 1, :], ss[:, 0, :], 4, G_pool.ends("r_o", g))
                pool.wait_ge(*G_dve.past("ss_qk", g))
                rsqrt(ss[:, 3, :], ss[:, 2, :], 4, G_pool.ends("r_qk", g))
                pool.wait_ge(*G_dve.past("M3", g))
                for lv in range(LEVELS):
                    if lv == 3:
                        pool.wait_ge(*G_dve.past("U", g))
                    if lv > 3:
                        pool.wait_ge(*G_pe.past(f"P1_{lv - 3}", g))
                    tt(MM[:, lv % 3, :, :], MT[:, :, :, :].rearrange("p a b c -> p (a b) c"), mid(mask(lv), 4),
                       ALU.mult).then_inc(*G_pool.ends(f"MM{lv}", g))

            with pool.Fori(0, QKH) as g:
                gdn_head(g)
            pool.wait_ge(*Z_dve.past("ss_o"))
            rsqrt(ss[:, 1, :], ss[:, 0, :], 4, Z_pool.ends("r_o"))
            pool.wait_ge(*O_dve.past("ms"))
            rsqrt(ss[:, 1, :], ss[:, 3, :], 2, O_pool.ends("rstd"))
            pool.wait_ge(*F_dve.past("ms"))
            rsqrt(ss[:, 1, :], ss[:, 3, :], 2, F_pool.ends("rstd"))
            pool.wait_ge(*F_dve.past("o1"))
            pool.dma_start(out.rearrange("(n p) d -> p n d", p=P), hn).then_inc(stored, 16)
            pool.wait_ge(stored, 16)


def kernel(**inputs):
    import concourse.bacc as bacc
    from concourse.bass_utils import run_bass_kernel_spmd

    a = {k: np.asarray(v) for k, v in inputs.items()}
    f32 = np.float32

    def cols(v):
        return v.reshape(-1, P).T

    cw = a["gdn_conv_w"][0]
    cq, ck, cv_ = cw[:, :D], cw[:, D:2 * D], cw[:, 2 * D:]
    gcw = np.stack([ck.reshape(4, QKH, P), cq.reshape(4, QKH, P),
                    cv_.reshape(4, QKH, 2, P)[:, :, 0], cv_.reshape(4, QKH, 2, P)[:, :, 1]])
    vec = np.concatenate([
        cols(a["norm_mix_w"][0]),
        a["rg_conv_w"][0].reshape(4, KT, P).transpose(2, 0, 1).reshape(P, 4 * KT),
        cols(a["rg_conv_b"][0]), cols(a["rg_gate_a_b"][0].reshape(-1)), cols(a["rg_gate_x_b"][0].reshape(-1)),
        cols(a["rg_lambda"][0]),
        gcw.transpose(3, 2, 0, 1).reshape(P, QKH * 16),
        a["gdn_norm_w"][0].reshape(P, 1),
    ], axis=1)
    row = np.broadcast_to(np.concatenate([a["router_b"][0], a["gdn_dt_bias"][0], a["gdn_A_log"][0]])[None], (P, NROW))
    ffn_rows = np.broadcast_to(np.stack([a["norm_ffn_w"][0], a["norm_final_w"]])[None], (P, 2, D))

    w_in = a["w_in"][0]
    o_b = 2 * D + 2 * D + 2 * 2 * D
    tiles = w_in[:, :o_b].reshape(KT, P, o_b // P, P).transpose(2, 1, 0, 3)
    gate_tiles = w_in[:, o_b + 2 * VH:].reshape(KT, P, 2 * KT, P).transpose(2, 1, 0, 3)

    def pieces(order, src):
        return src[np.array(order)].reshape(-1, 2, P, D).transpose(0, 2, 1, 3).reshape(-1, P, SLOT)

    rg_x, rg_y, q, k, v, z = 0, 8, 16, 24, 32, 48
    w_rg = pieces([t for i in range(RGB) for o in (rg_x, rg_y) for t in (o + 2 * i, o + 2 * i + 1)], tiles)
    w_gdn = pieces([t for g in range(QKH) for t in (k + g, q + g, v + 2 * g, v + 2 * g + 1, z + 2 * g, z + 2 * g + 1)],
                   tiles)
    w_gates = pieces([t for j in range(KT) for t in (j, KT + j)], gate_tiles)
    w_rgg = np.stack([a["rg_gate_a_w"][0], a["rg_gate_x_w"][0]], 1).reshape(RGB, 2, 2, P, 256)\
        .transpose(0, 3, 1, 2, 4).reshape(RGB, P, D)
    w_ba = np.stack([w_in[:, o_b:o_b + 2 * VH], a["router_w"][0]]).reshape(2, KT, P, 32).transpose(0, 2, 1, 3)
    w_bg = a["w_branch_gdn"][0].reshape(VH, P, KT, P).transpose(2, 1, 0, 3).reshape(KT, P, SLOT)
    w_br = a["w_branch_rg"][0].reshape(KT, P, KT, P).transpose(2, 1, 0, 3).reshape(KT, P, D)
    nc = bacc.Bacc("TRN2", target_bir_lowering=False, num_devices=1)
    arrays, args = {}, []
    for name, v_ in (("x", a["x"][0]), ("vec", vec), ("row", row), ("con", constants()),
                     ("w_rg", w_rg.reshape(RGB, 2, P, SLOT)), ("w_rgg", w_rgg), ("w_ba", w_ba),
                     ("w_gdn", w_gdn.reshape(QKH, 3, P, SLOT)), ("w_gates", w_gates), ("w_bg", w_bg), ("w_br", w_br),
                     ("w_out", a["w_out"][0]), ("ffn_rows", ffn_rows), ("moe_gu", a["moe_w_gate_up"][0].reshape(NE, KT, P, SLOT)),
                     ("moe_down", a["moe_w_down"][0]), ("b_gu", a["moe_b_gate_up"][0]), ("b_down", a["moe_b_down"][0])):
        v_ = np.ascontiguousarray(v_)
        assert v_.dtype == f32
        arrays[name] = v_
        args.append(nc.dram_tensor(name, v_.shape, F32, kind="ExternalInput").ap())
    args.append(nc.dram_tensor("out", (T, D), F32, kind="ExternalOutput").ap())
    build(nc, *args)
    r = run_bass_kernel_spmd(nc, [arrays], core_ids=[0])
    return r.results[0]["out"].reshape(1, T, D)
```

```python
from contextlib import ExitStack

import numpy as np

import concourse.bass as bass
from concourse import mybir

F32 = mybir.dt.float32
I32 = mybir.dt.int32
ALU = mybir.AluOpType
ACT = mybir.ActivationFunctionType
AX = mybir.AxisListType.X

P = 128
D = 1024
T = 256
NT = T // P
KT = D // P
RGB = 4
RG_C = 8.0
QKH = 8
VH = 16
DK = 128
LEVELS = 7
NE = 32
TOP = 4
CAP = 64
FT = 8
LIMIT = 7.0
ALPHA = 1.702
EPS = 1e-6
BIG = 1e30
SLOT = 2048
NSLOT = 12
GELU_C = 0.7978845608028654
GELU_A = 0.044715

VEC = {}
_n = 0
for _name, _w in (("norm_mix", KT), ("rg_cw", 4 * KT), ("rg_cb", KT), ("ba", KT), ("bx", KT), ("lam", KT),
                  ("gdn_cw", QKH * 4 * 4), ("gdn_norm", 1)):
    VEC[_name] = (_n, _w)
    _n += _w
NVEC = _n
ROW = {"router_b": (0, NE), "dt_bias": (32, VH), "A_log": (48, VH)}
NROW = 64
CON = {}
_n = 0
for _name, _w in (("ident", P), ("tri_incl", P), ("tri_strict", P), ("ones", P), ("neg", P), ("masks", LEVELS * P),
                  ("ident_qk", 4 * P), ("ident_half", P), ("slots", 2 * CAP)):
    CON[_name] = (_n, _w)
    _n += _w
NCON = _n


def constants():
    s, c = np.arange(P)[:, None], np.arange(P)[None, :]
    con = np.zeros((P, NCON), np.float32)

    def put(name, v):
        o, w = CON[name]
        con[:, o:o + w] = v

    put("ident", s == c)
    put("tri_incl", s <= c)
    put("tri_strict", s < c)
    put("ones", 1.0)
    put("neg", np.where(c < s, -BIG, 0.0))
    masks = []
    for level in range(LEVELS):
        b = 2 ** level
        masks.append((s // (2 * b) == c // (2 * b)) & (s % (2 * b) < b) & (c % (2 * b) >= b))
    put("masks", np.concatenate(masks, axis=1))
    eye = (s == c).astype(np.float32)
    put("ident_qk", np.concatenate([0.5 * eye] * 2 + [0.5 * DK ** -0.5 * eye] * 2, axis=1))
    put("ident_half", 0.5 * eye)
    put("slots", np.tile(np.arange(CAP), 2)[None, :])
    return con


class Steps:

    def __init__(self, sem, names, rounds=1, lacking=(), before=0):
        self.sem, self.names, self.rounds, self.before = sem, names, rounds, before
        self.short = [n for n in names if n not in lacking]
        self.at = 0

    def _list(self, r):
        return self.short if isinstance(r, int) and r == self.rounds - 1 else self.names

    def ends(self, name, r=0):
        names = self._list(r)
        self.at %= len(names)
        assert names[self.at] == name, (name, names[self.at])
        self.at += 1
        return self.sem, 1

    def past(self, name, r=0):
        return self.sem, self.before + r * len(self.names) + self._list(r).index(name) + 1


def build(nc, x, vec, row, con, w_rg, w_rgg, w_ba, w_gdn, w_gates, w_bg, w_br, w_out, ffn_rows,
          moe_gu, moe_down, b_gu, b_down, out):
    ctx = ExitStack()
    with ctx:
        def sb(name, shape, dt=F32):
            return ctx.enter_context(nc.sbuf_tensor(name, shape, dt))

        def sem(name):
            return ctx.enter_context(nc.semaphore(name))

        ring = sb("ring", [P, NSLOT, SLOT])
        h = sb("h", [P, NT, D])
        xnT = sb("xnT", [P, KT, T])
        mixT = sb("mixT", [P, KT, T])
        rgo = sb("rgo", [P, KT, T])
        og = sb("og", [P, VH, T])
        V = sb("V", [P, NVEC])
        R = sb("R", [P, NROW])
        C = sb("C", [P, NCON])
        W_ba = sb("W_ba", [P, KT, 2 * VH])
        W_r = sb("W_r", [P, KT, NE])
        rawp = sb("rawp", [P, 4, 3 + T])
        cqk = sb("cqk", [P, 2, T])
        cv = sb("cv", [P, 2, T])
        thq = sb("thq", [P, 2, T])
        thv = sb("thv", [P, 2, T])
        zraw = sb("zraw", [P, 2, T])
        zs = sb("zs", [P, 2, T])
        QK = sb("QK", [P, NT, 2, P])
        kt0 = sb("kt0", [P, P])
        attT = sb("attT", [P, NT, 2, P])
        MT = sb("MT", [P, NT, 2, P])
        MM = sb("MM", [P, 3, 4, P])
        XU = sb("XU", [P, 4, 2, P])
        vn = sb("vn", [P, NT, 2, P])
        vk = sb("vk", [P, 2, P])
        S1 = sb("S1", [P, 2, P])
        qd = sb("qd", [P, 2, P])
        osq = sb("osq", [P, 2, T])
        ow = sb("ow", [P, 2, T])
        diag = sb("diag", [P, 4, P])
        rowbuf = sb("rowbuf", [P, 2, T])
        rowsel = rowbuf[0:VH, :, :]
        Vt = mixT[:, 2:4, :].rearrange("p j (n c) -> p j n c", n=2)
        Dt = mixT[:, 0:2, :].rearrange("p j (n c) -> p j n c", n=2)
        P1s = mixT[:, 0:2, :].rearrange("p j (n c) -> p (j n) c", n=2)
        k1 = mixT[:, 4, 0:P]
        rr = vk
        eG = rowbuf[:, :, 0:P]
        beta = sb("beta", [P, NT, VH])
        gcol = sb("gcol", [P, NT, VH])
        gsum = sb("gsum", [P, NT, VH])
        negeg = sb("negeg", [P, NT, VH])
        kdec = sb("kdec", [P, VH])
        gcT = sb("gcT", [VH, T])
        small = sb("small", [P, 8, 48])
        ss = sb("ss", [P, 4, 4])
        half_pow = sb("half_pow", [P, 4])
        sp4 = sb("sp4", [P, KT])
        hb = sb("hb", [P, 2 * KT])
        loops = sb("loops", [P, 1], I32)
        PS = ctx.enter_context(nc.psum_tensor("PS", [P, 8, 512], F32))

        def vcol(name, i, n=1):
            o, _ = VEC[name]
            return V[:, bass.ds(o + i, n)]

        def con_(name, a=0, n=P):
            o, _ = CON[name]
            return C[:, o + a:o + a + n]

        ident, tri_incl, tri_strict = con_("ident"), con_("tri_incl"), con_("tri_strict")
        ones, neg = con_("ones"), con_("neg")

        def mask(level):
            return con_("masks", level * P)

        def bank(i):
            return PS[:, i, :]

        def bank3(i, a):
            return PS[:, i, :].rearrange("p (a n) -> p a n", a=a)

        def mid(ap, n):
            return ap.unsqueeze(1).broadcast_to([ap.shape[0], n, ap.shape[1]])

        def last(ap, n):
            return ap.unsqueeze(2).broadcast_to([ap.shape[0], ap.shape[1], n])

        x_loaded, con_loaded = sem("x_loaded"), sem("con_loaded")
        vec_loaded, row_loaded, ba_loaded = sem("vec_loaded"), sem("row_loaded"), sem("ba_loaded")
        loaded = [sem(f"loaded{s}") for s in range(NSLOT)]
        used = [sem(f"used{s}") for s in range(NSLOT)]
        rows_loaded, bdown_loaded, stored = sem("rows_loaded"), sem("bdown_loaded"), sem("stored")
        bgu_loaded = sem("bgu_loaded")

        A_act = Steps(sem("a_act"), ["ss0", "ss1"])
        A_pool = Steps(sem("a_pool"), ["rstd"])
        A_dve = Steps(sem("a_dve"), ["pow", "ms", "pad", "xn0", "xn1", "ev0", "ev1", "ev2", "ev3"])
        A_pe = Steps(sem("a_pe"), ["tr0", "tr1", "tr2", "tr3"])
        SP_DVE = ["in_ba", "in_lam", "abs", "y2", "s_rec", "s", "s2",
                  "p6", "p5", "p4", "p3", "p2", "p1", "p0", "pos", "sp"]
        B_dve = Steps(sem("b_dve"), SP_DVE + ["sp4", "hb", "beta", "g", "gc", "gc_last", "negeg", "gcT"])
        B_act = Steps(sem("b_act"), ["tanh_b", "exp_abs", "exp_A", "kdec", "eg"])
        B_pe = Steps(sem("b_pe"), ["ba", "cum", "tr"])

        xy_copied = sem("xy_copied")
        C_act = Steps(sem("c_act"), ["y2", "tanh_y", "tanh_a", "tanh_i", "decay", "tanh_l"], RGB)
        C_dve = Steps(sem("c_dve"), [f"conv{j}" for j in range(8)] + ["cub", "cub_y", "l0", "l1", "gated", "dec2",
                                    "mult", "guard", "gelu"], RGB)
        Ct_act = Steps(sem("ct_act"), ["sqrt"])
        Ct_dve = Steps(sem("ct_dve"), ["first", "b"] + [f"scan{k}" for k in range(KT)] + ["out"])

        CQK, CV = [f"cqk{j}" for j in range(8)], [f"cv{j}" for j in range(8)]
        N_pe = Steps(sem("n_pe"), ["ss_qk", "bc_qk"], QKH)
        N_act = Steps(sem("n_act"), ["tanh_qk", "sq_qk", "tanh_v"], QKH)
        N_dve = Steps(sem("n_dve"), CQK + ["s_qk"] + CV[:2] + ["ss_qk"] + CV[2:4] + ["diag_qk"] + CV[4:]
                      + ["rowsel", "QK", "s_v"], QKH)
        N_pool = Steps(sem("n_pool"), ["r_qk"], QKH)
        G_pe = Steps(sem("g_pe"), ["G", "ss_o", "kkqk", "trv", "trk", "bc_o", "trUA", "trUB", "P1A_1", "P2A_1", "P1B_1"]
                     + [s for lv in range(2, LEVELS) for s in (f"P1A_{lv}", f"P2B_{lv - 1}", f"P2A_{lv}", f"P1B_{lv}")]
                     + ["vn0", f"P2B_{LEVELS - 1}", "S1", "kS", "vn1", "O"], QKH)
        G_act = Steps(sem("g_act"), ["eG", "Dt", "tanh_z", "k1", "Vt", "XA", "XB"]
                      + [f"P1s{c}_{lv}" for lv in range(1, LEVELS) for c in "AB"]
                      + ["S1"], QKH)
        G_dve = Steps(sem("g_dve"), ["ss_o", "D0", "D1", "D2", "D3", "diag_o", "M0", "M1", "M2", "M3", "kt0", "att",
                                     "qd", "U", "og", "s_z", "XUA_1"]
                      + [s for lv in range(2, LEVELS) for s in (f"XUB_{lv - 1}", f"XUA_{lv}")]
                      + ["vk0", "vk1", f"XUB_{LEVELS - 1}", "vn00", "vn01", "r0", "r1", "vn10", "vn11", "ow"],
                      QKH)
        G_pool = Steps(sem("g_pool"), ["r_o"] + [f"MM{lv}" for lv in range(LEVELS)], QKH)
        qk_copied, v_copied, z_copied, osq_ready = sem("qk_copied"), sem("v_copied"), sem("z_copied"), sem("osq_ready")
        ow_zero, poly = sem("ow_zero"), sem("poly")
        Z_pe = Steps(sem("z_pe"), ["ss_o", "bc_o"])
        Z_dve = Steps(sem("z_dve"), ["ss_o", "diag_o", "og"])
        Z_pool = Steps(sem("z_pool"), ["r_o"])

        M_act = Steps(sem("m_act"), ["tanh"], KT)
        M_dve = Steps(sem("m_dve"), ["a", "b", "mix"], KT)

        O_pe = Steps(sem("o_pe"), ["tr0", "tr1", "tr2", "tr3", "router", "pos", "trg", "bd"])
        O_act = Steps(sem("o_act"), ["ss0", "ss1", "exp0", "exp1", "gT"])
        O_pool = Steps(sem("o_pool"), ["rstd"])
        O_dve = Steps(sem("o_dve"), ["h0", "h1", "h2", "h3", "ms", "hn0", "hn1", "ev0", "ev1", "ev2", "ev3",
                                     "logits", "max0", "max1", "negm", "gt0", "gt1", "ngt", "eq0", "eq1",
                                     "need", "cum0", "cum1", "ok0", "ok1", "eqok", "sel",
                                     "exs", "sum", "rec", "gate0", "gate1", "pos1", "posm", "cmax",
                                     "c64", "c128", "c192", "csum", "csum2", "loops",
                                     "b0", "b1", "b2", "b3"])

        E_pe0 = Steps(sem("e_pe"), ["gather", "trX"])
        E_pe = Steps(E_pe0.sem, ["trS", "gather", "trH", "trX", "scatter"], before=2)
        E_act0 = Steps(sem("e_act"), ["xg", "xT"])
        E_act = Steps(E_act0.sem, ["th", "ST", "xg", "hidT", "xT", "Y"], before=2)
        E_dve0 = Steps(sem("e_dve"), ["S0", "S1", "SG0", "SG1", "next"])
        E_dve = Steps(E_dve0.sem, ["S0", "S1", "g", "u", "p", "hid", "SG0", "SG1", "next", "y0", "y1", "y2", "y3"],
                      before=5)
        onehot_ready = sem("onehot_ready")
        F_act = Steps(sem("f_act"), ["ss0", "ss1"])
        F_pool = Steps(sem("f_pool"), ["rstd"])
        F_dve = Steps(sem("f_dve"), ["ms", "o0", "o1"])

        S_RG, S_GDN, S_MIX, S_OUT = (0, 1, 2), (3, 4, 5), (6, 7, 8), (9, 10, 11, 0)
        fills = [0] * NSLOT
        for slots, n in ((S_RG, RGB), (S_GDN, QKH), (S_MIX, KT), (S_OUT, 1)):
            for s in slots:
                fills[s] += n

        ring4 = ring[:, :, :].rearrange("p s (t k c) -> p s t k c", t=2, k=KT)
        ring16 = ring[:, :, :].rearrange("p s (k c) -> p s k c", c=P)
        ring2 = ring[:, :, :].rearrange("p s (k n) -> p s k n", k=2)

        spx, spy, spa, sps, sps2, spp = (small[:, i, 0:40] for i in range(6))
        tb, exA = small[:, 6, 0:32], small[:, 7, 0:16]
        xa, ta, ti, L, yraw, q3, ty, y2b = cqk, thq, thv, cv, zraw, zs, osq, ow
        mrg, arg = og[:, 0:KT, :], og[:, KT:2 * KT, :]
        rsc = thq[:, :, :].rearrange("p a n -> p (a n)")

        def r32(i):
            return rsc[:, 64 * i:64 * i + 64].rearrange("p (n e) -> p n e", n=NT)

        logits, gt, eq, cum, ok, sel_ = (r32(i) for i in range(6))
        exs, gate = r32(6), r32(7)
        msc = MT[:, :, :, :].rearrange("p a b c -> p (a b c)")
        posm = msc[:, 0:64].rearrange("p (n e) -> p n e", n=NT)
        mx8 = msc[:, 64:80].rearrange("p (n e) -> p n e", n=NT)
        negm, ngt, need, gsm, grec = (msc[:, 80 + 2 * i:82 + 2 * i] for i in range(5))
        cmax, c64, c128, c192 = (msc[:, 96 + i:97 + i] for i in range(4))
        hn = rgo[:, :, :].rearrange("p k t -> p (k t)").rearrange("p (n d) -> p n d", n=NT)
        rows = mixT[:, :, :].rearrange("p k t -> p (k t)").rearrange("p (n d) -> p n d", n=NT)
        ogf = og[:, :, :].rearrange("p k t -> p (k t)")
        gT, bdn = ogf[0:NE, 2816:2816 + T], ogf[0:NE, 3072:3072 + D]
        bgu = xnT[:, :, :].rearrange("p k t -> p (k t)")[0:NE, :]
        eg_, eu, ehid, Y = (ogf[:, 512 * i:512 * (i + 1)] for i in range(4))
        ST = ogf[:, 2048:2304].rearrange("p (n t) -> p n t", n=NT)
        Ssel = ogf[:, 2304:2432].rearrange("p (n s) -> p n s", n=NT)
        SG = ogf[:, 2432:2688].rearrange("p (n s) -> p n s", n=NT)
        onehot = ogf[0:NE, 2688:2688 + CAP]

        def flat3(t):
            return t[:, :, :].rearrange("p a n -> p (a n)")

        def by_tile(t):
            return flat3(t).rearrange("p (b h s) -> p b h s", h=2, s=CAP)

        xgs, eth = flat3(zraw), flat3(thv)
        xT, hidT = by_tile(cqk), by_tile(cv)

        block = ctx.enter_context(nc.Block())

        @block.sync
        def _(sp):
            def fill(slot, n, src, width=SLOT):
                sp.wait_ge(used[slot], n - 1)
                sp.dma_start(ring[:, slot, 0:width], src).then_inc(loaded[slot], 16)

            sp.dma_start(h[:, :, :], x.rearrange("(n p) d -> p n d", p=P)).then_inc(x_loaded, 16)
            sp.dma_start(C[:, :], con).then_inc(con_loaded, 16)
            with sp.Fori(0, RGB) as i:
                fill(S_RG[0], i + 1, w_rg[bass.ds(i, 1), 0].rearrange("a p n -> (a p) n"))
                fill(S_RG[1], i + 1, w_rg[bass.ds(i, 1), 1].rearrange("a p n -> (a p) n"))
                fill(S_RG[2], i + 1, w_rgg[bass.ds(i, 1)].rearrange("a p n -> (a p) n"), D)
            with sp.Fori(0, QKH) as g:
                for j in range(3):
                    fill(S_GDN[j], g + 1, w_gdn[bass.ds(g, 1), j].rearrange("a p n -> (a p) n"))
            w_out_v = w_out.rearrange("(i k p) n -> i p k n", k=2, p=P)

            def fill_out(i):
                s = S_OUT[i]
                sp.wait_ge(used[s], fills[s] - 1)
                sp.dma_start(ring2[:, s, :, :], w_out_v[i]).then_inc(loaded[s], 16)

            for i in range(4):
                fill_out(i)

            def fill_mix(j):
                fill(S_MIX[0], j + 1, w_gates[bass.ds(j, 1)].rearrange("a p n -> (a p) n"))
                fill(S_MIX[1], j + 1, w_bg[bass.ds(j, 1)].rearrange("a p n -> (a p) n"))
                fill(S_MIX[2], j + 1, w_br[bass.ds(j, 1)].rearrange("a p n -> (a p) n"), D)

            fill_mix(0)

            def fill_expert(s, it, e):
                sp.wait_ge(used[s], fills[s] + it)
                if s < FT:
                    src = moe_gu[bass.ds(e, 1), s].rearrange("a p n -> (a p) n")
                    sp.dma_start(ring[:, s, :], src).then_inc(loaded[s], 16)
                else:
                    src = moe_down[bass.ds(e, 1)].rearrange("a (i k p) n -> (a i) p k n", k=2, p=P)[s - FT]
                    sp.dma_start(ring2[:, s, :, :], src).then_inc(loaded[s], 16)

            for s in (1, 2, 3, 4, 5):
                fill_expert(s, 0, 0)
            with sp.Fori(1, KT) as j:
                fill_mix(j)
            for s in (6, 7, 8, 9, 10, 11, 0):
                fill_expert(s, 0, 0)
            sp.wait_ge(*O_dve.past("loops"))
            n_it = sp.value_load(loops[0:1, 0:1], min_val=NE, max_val=4 * NE)
            with sp.Fori(1, n_it) as it:
                for s in range(NSLOT):
                    fill_expert(s, it, it % NE)

        @block.tensor
        def _(pe):
            mm, tr = nc.tensor.matmul, nc.tensor.transpose

            def transposes(src, steps, ready, evacuated, first):
                for b in range(4):
                    if b == 0:
                        pe.wait_ge(*ready)
                    for i in range(4):
                        k, n = 2 * b + i // 2, i % 2
                        ins = tr(PS[:, first + b, i * P:(i + 1) * P], src[:, n, k * P:(k + 1) * P], ident)
                    ins.then_inc(*steps.ends(f"tr{b}"))

            pe.wait_ge(con_loaded, 16)
            transposes(hn, A_pe, A_dve.past("xn1"), None, 0)
            pe.wait_ge(*A_dve.past("ev3"))
            pe.wait_ge(ba_loaded, 32)
            for n in range(NT):
                for k in range(KT):
                    ins = mm(PS[:, 4, n * 32:n * 32 + 32], xnT[:, k, n * P:(n + 1) * P], W_ba[:, k, :],
                             start=(k == 0), stop=(k == KT - 1))
            ins.then_inc(*B_pe.ends("ba"))
            pe.wait_ge(*B_dve.past("g"))
            mm(PS[:, 5, 0:32], tri_incl, gcol[:, :, :], start=True, stop=True)
            mm(PS[:, 5, 32:48], ones, gcol[:, 0, :], start=True, stop=True).then_inc(*B_pe.ends("cum"))
            pe.wait_ge(*B_dve.past("gc"))
            for n in range(NT):
                ins = tr(PS[0:VH, 6, n * P:(n + 1) * P], gsum[:, n, :], ident)
            ins.then_inc(*B_pe.ends("tr"))

            def pair(bank_, slot, a=0, b=2 * KT):
                for i in range(a, b):
                    t, k = i // KT, i % KT
                    ins = mm(PS[:, bank_, t * T:(t + 1) * T], ring4[:, slot, t, k, :], xnT[:, k, :],
                             start=(k == 0), stop=(k == KT - 1))
                return ins

            with pe.Fori(0, RGB) as i:
                pe.wait_ge(loaded[S_RG[0]], 16 * (i + 1))
                pe.wait_ge(xy_copied, 2 * i)
                pair(0, S_RG[0]).then_inc(used[S_RG[0]], 1)
                pe.wait_ge(loaded[S_RG[1]], 16 * (i + 1))
                pair(1, S_RG[1]).then_inc(used[S_RG[1]], 1)
                pe.wait_ge(loaded[S_RG[2]], 16 * (i + 1))
                pe.wait_ge(*C_dve.past("conv7", i))
                for gate_i in range(2):
                    for jt in range(2):
                        for k in range(2):
                            w0 = gate_i * 512 + k * T + jt * P
                            ins = mm(PS[:, 2 + gate_i, jt * T:(jt + 1) * T], ring[:, S_RG[2], w0:w0 + P],
                                     xa[:, k, :], start=(k == 0), stop=(k == 1))
                ins.then_inc(used[S_RG[2]], 1)

            PJ0, PJ1, P1_A, PX_A, PX_B, QKB, GB, P1_B = range(8)

            def load_wait(j, r):
                pe.wait_ge(loaded[S_GDN[j]], 16 * (r + 1))

            def norm_sums(dst, src):
                for i in range(4):
                    ins = mm(dst[:, i:i + 1], src[:, i // 2, (i % 2) * P:(i % 2 + 1) * P], ones[:, 0:1],
                             start=True, stop=True)
                return ins

            def qk_sums(r):
                pe.wait_ge(*N_act.past("sq_qk", r))
                norm_sums(PS[:, GB, 0:4], thq).then_inc(*N_pe.ends("ss_qk", r))

            def qk_scales(r):
                pe.wait_ge(*N_dve.past("diag_qk", r))
                mm(bank(PX_B), ones, diag[:, :, :], start=True, stop=True).then_inc(*N_pe.ends("bc_qk", r))

            load_wait(0, 0)
            pe.wait_ge(xy_copied, 2 * RGB)
            pair(PJ0, S_GDN[0]).then_inc(used[S_GDN[0]], 1)
            load_wait(1, 0)
            pair(PJ1, S_GDN[1]).then_inc(used[S_GDN[1]], 1)
            load_wait(2, 0)
            pe.wait_ge(qk_copied, 1)
            pair(PJ0, S_GDN[2]).then_inc(used[S_GDN[2]], 1)
            qk_sums(0)
            qk_scales(0)

            def gdn_head(g, final):
                def pj_qk(a, b):
                    if final:
                        return
                    if a == 0:
                        load_wait(0, g + 1)
                        pe.wait_ge(z_copied, g + 1)
                    ins = pair(PJ0, S_GDN[0], a, b)
                    if b == 2 * KT:
                        ins.then_inc(used[S_GDN[0]], 1)

                def pj_vz(a, b):
                    if final:
                        return
                    if a == 0:
                        load_wait(1, g + 1)
                        pe.wait_ge(v_copied, g + 1)
                    if a == 2 * KT:
                        load_wait(2, g + 1)
                        pe.wait_ge(qk_copied, g + 2)
                    if a < 2 * KT:
                        ins = pair(PJ1, S_GDN[1], a, b)
                    else:
                        ins = pair(PJ0, S_GDN[2], a - 2 * KT, b - 2 * KT)
                    if b in (2 * KT, 4 * KT):
                        ins.then_inc(used[S_GDN[1 if b == 2 * KT else 2]], 1)

                pe.wait_ge(*N_dve.past("rowsel", g))
                mm(bank(GB), ones[0:VH, :], rowsel[:, :, :], start=True, stop=True).then_inc(*G_pe.ends("G", g))
                pe.wait_ge(osq_ready, g + 1)
                norm_sums(PS[:, P1_B, 4:8], osq).then_inc(*G_pe.ends("ss_o", g))
                pj_qk(0, 6)
                pe.wait_ge(*G_dve.past("ss_o", g))
                pe.wait_ge(*N_dve.past("QK", g))
                for n in range(NT):
                    ins = mm(PS[:, QKB, n * T:(n + 1) * T], QK[:, n, 0, :], QK[:, n, :, :], start=True, stop=True)
                ins.then_inc(*G_pe.ends("kkqk", g))
                pe.wait_ge(*N_dve.past("s_v", g))
                for n in range(NT):
                    for j in range(2):
                        ins = tr(PS[:, P1_A, (2 * n + j) * P:(2 * n + j + 1) * P], cv[:, j, n * P:(n + 1) * P], ident)
                ins.then_inc(*G_pe.ends("trv", g))
                tr(PS[:, P1_B, P:2 * P], QK[:, 0, 0, :], ident).then_inc(*G_pe.ends("trk", g))
                pj_qk(6, 2 * KT)
                pe.wait_ge(*G_dve.past("diag_o", g))
                mm(bank(PX_B), ones, diag[:, :, :], start=True, stop=True).then_inc(*G_pe.ends("bc_o", g))
                pe.wait_ge(*G_dve.past("U", g))
                pe.wait_ge(*G_act.past("Vt", g))
                for c, bank_ in ((0, P1_A), (1, P1_B)):
                    for u in range(2):
                        ins = tr(PS[:, bank_, u * P:(u + 1) * P], XU[:, 2 * c + u, 1, :], ident)
                    ins.then_inc(*G_pe.ends("trUA" if c == 0 else "trUB", g))

                def m_x(c, lv):
                    for u in (2 * c, 2 * c + 1):
                        ins = mm(PS[:, (P1_A, P1_B)[c], (u % 2) * P:(u % 2 + 1) * P], MM[:, lv % 3, u, :],
                                 XU[:, u, 0, :], start=True, stop=True)
                    ins.then_inc(*G_pe.ends(f"P1{'AB'[c]}_{lv}", g))

                def x_m_x(c, lv):
                    pe.wait_ge(*G_act.past(f"P1s{'AB'[c]}_{lv}", g))
                    for u in (2 * c, 2 * c + 1):
                        o = PS[:, (PX_A, PX_B)[c], (u % 2) * 2 * P:(u % 2 + 1) * 2 * P]
                        if lv < LEVELS - 1:
                            mm(o[:, 0:P], XU[:, u, 1, :], P1s[:, u, :], start=True, stop=True)
                        ins = mm(o[:, P:2 * P], P1s[:, u, :], XU[:, u, 1, :], start=True, stop=True)
                    ins.then_inc(*G_pe.ends(f"P2{'AB'[c]}_{lv}", g))

                for lv in range(1, LEVELS):
                    pe.wait_ge(*G_pool.past(f"MM{lv}", g))
                    if lv == 1:
                        pe.wait_ge(*G_act.past("XA", g))
                        m_x(0, lv)
                    else:
                        pe.wait_ge(*G_dve.past(f"XUA_{lv - 1}", g))
                        m_x(0, lv)
                        x_m_x(1, lv - 1)
                    if lv == 5 and not final:
                        qk_sums(g + 1)
                    x_m_x(0, lv)
                    pj_vz(4 * (lv - 1), 4 * lv - 2)
                    if lv == 1:
                        pe.wait_ge(*G_act.past("XB", g))
                    else:
                        pe.wait_ge(*G_dve.past(f"XUB_{lv - 1}", g))
                    m_x(1, lv)
                    pj_vz(4 * lv - 2, 4 * lv)
                top = LEVELS - 1
                pe.wait_ge(*G_dve.past(f"XUA_{top}", g))
                for j in range(2):
                    ins = mm(PS[:, P1_A, j * P:(j + 1) * P], XU[:, j, 1, :], Vt[:, 0, j, :], start=True, stop=True)
                ins.then_inc(*G_pe.ends("vn0", g))
                x_m_x(1, top)
                pe.wait_ge(*G_dve.past("vk1", g))
                mm(PS[:, GB, 0:T], kt0[:, :], vk[:, :, :], start=True, stop=True).then_inc(*G_pe.ends("S1", g))
                pj_vz(24, 26)
                pe.wait_ge(*G_act.past("S1", g))
                mm(PS[:, PX_A, 0:T], k1, S1[:, :, :], start=True, stop=True).then_inc(*G_pe.ends("kS", g))
                pj_vz(26, 29)
                pe.wait_ge(*G_dve.past("r1", g))
                for j in range(2):
                    ins = mm(PS[:, PX_A, T + j * P:T + (j + 1) * P], XU[:, 2 + j, 1, :], rr[:, j, :],
                             start=True, stop=True)
                ins.then_inc(*G_pe.ends("vn1", g))
                if not final:
                    qk_scales(g + 1)
                pj_vz(29, 32)
                pe.wait_ge(*G_dve.past("vn11", g))
                for j in range(2):
                    mm(PS[:, QKB, j * T:j * T + P], vn[:, 0, j, :], attT[:, 0, j, :], start=True, stop=True)
                    mm(PS[:, QKB, j * T + P:(j + 1) * T], S1[:, j, :], qd[:, j, :], start=True, stop=False)
                    ins = mm(PS[:, QKB, j * T + P:(j + 1) * T], vn[:, 1, j, :], attT[:, 1, j, :],
                             start=False, stop=True)
                ins.then_inc(*G_pe.ends("O", g))

            with pe.Fori(0, QKH - 1) as g:
                gdn_head(g, False)
            gdn_head(QKH - 1, True)
            pe.wait_ge(osq_ready, QKH + 1)
            norm_sums(PS[:, P1_B, 4:8], osq).then_inc(*Z_pe.ends("ss_o"))
            pe.wait_ge(*Z_dve.past("diag_o"))
            mm(bank(PX_B), ones, diag[:, :, :], start=True, stop=True).then_inc(*Z_pe.ends("bc_o"))

            with pe.Fori(0, KT) as j:
                pe.wait_ge(loaded[S_MIX[0]], 16 * (j + 1))
                pe.wait_ge(M_dve.sem, j * len(M_dve.names))
                pair(0, S_MIX[0]).then_inc(used[S_MIX[0]], 1)
                pe.wait_ge(loaded[S_MIX[1]], 16 * (j + 1))
                pe.wait_ge(*Z_dve.past("og"))
                for k in range(VH):
                    ins = mm(PS[:, 1, 0:T], ring16[:, S_MIX[1], k, :], og[:, k, :], start=(k == 0), stop=(k == VH - 1))
                ins.then_inc(used[S_MIX[1]], 1)
                pe.wait_ge(loaded[S_MIX[2]], 16 * (j + 1))
                pe.wait_ge(*Ct_dve.past("out"))
                for k in range(KT):
                    ins = mm(PS[:, 2, 0:T], ring16[:, S_MIX[2], k, :], rgo[:, k, :], start=(k == 0), stop=(k == KT - 1))
                ins.then_inc(used[S_MIX[2]], 1)

            pe.wait_ge(*M_dve.past("mix", KT - 1))
            for i in range(4):
                s = S_OUT[i]
                pe.wait_ge(loaded[s], 16 * fills[s])
                for kk in range(2):
                    k = 2 * i + kk
                    for n in range(NT):
                        for f in range(2):
                            ins = mm(PS[:, 4 + 2 * n + f, :], mixT[:, k, n * P:(n + 1) * P],
                                     ring2[:, s, kk, f * 512:(f + 1) * 512], start=(k == 0), stop=(k == KT - 1))
                ins.then_inc(used[s], 1)
            transposes(hn, O_pe, O_dve.past("hn1"), None, 0)
            pe.wait_ge(*O_dve.past("ev3"))
            for n in range(NT):
                for k in range(KT):
                    ins = mm(PS[:, 4, n * NE:(n + 1) * NE], xnT[:, k, n * P:(n + 1) * P], W_r[:, k, :],
                             start=(k == 0), stop=(k == KT - 1))
            ins.then_inc(*O_pe.ends("router"))
            pe.wait_ge(*O_dve.past("sel"))
            mm(PS[:, 5, 0:NE], tri_strict, sel_[:, 0, :], start=True, stop=True)
            mm(PS[:, 5, NE:2 * NE], ones, sel_[:, 0, :], start=True, stop=False)
            mm(PS[:, 5, NE:2 * NE], tri_strict, sel_[:, 1, :], start=False, stop=True)
            mm(PS[:, 5, 2 * NE:3 * NE], ones, sel_[:, 0, :], start=True, stop=False)
            mm(PS[:, 5, 2 * NE:3 * NE], ones, sel_[:, 1, :], start=False, stop=True).then_inc(*O_pe.ends("pos"))
            pe.wait_ge(*O_dve.past("gate1"))
            for n in range(NT):
                ins = tr(PS[0:NE, 6, n * P:(n + 1) * P], gate[:, n, :], ident)
            ins.then_inc(*O_pe.ends("trg"))
            pe.wait_ge(*O_act.past("gT"))
            pe.wait_ge(bdown_loaded, 16)
            for n in range(NT):
                for f in range(2):
                    ins = mm(PS[:, 2 * n + f, :], gT[:, n * P:(n + 1) * P], bdn[:, f * 512:(f + 1) * 512],
                             start=True, stop=True)
            ins.then_inc(*O_pe.ends("bd"))

            GATE, UP, XG, DN, SC = 0, 1, 2, 3, 4

            def gather(steps, sel_done, r):
                pe.wait_ge(*sel_done)
                for n in range(NT):
                    for half in range(2):
                        ins = mm(PS[half * CAP:(half + 1) * CAP, XG, :], Ssel[:, n, :],
                                 hn[:, n, half * 512:(half + 1) * 512], start=(n == 0), stop=(n == NT - 1))
                ins.then_inc(*steps.ends("gather", r))

            def tiles_turned(bank_, src, steps, name, r):
                for b in range(4):
                    ins = tr(PS[:, bank_, b * P:(b + 1) * P], src[:, b * P:(b + 1) * P], ident)
                ins.then_inc(*steps.ends(name, r))

            pe.wait_ge(*O_dve.past("b3"))
            n_it = pe.value_load(loops[0:1, 0:1], min_val=NE, max_val=4 * NE)
            gather(E_pe0, E_dve0.past("S1"), 0)
            pe.wait_ge(*E_act0.past("xg"))
            tiles_turned(SC + 1, xgs, E_pe0, "trX", 0)
            pe.wait_ge(*E_act0.past("xT"))
            pe.wait_ge(bgu_loaded, 16)
            with pe.Fori(0, n_it) as it:
                pe.wait_ge(onehot_ready, it + 1)
                for k in range(-1, KT):
                    if k >= 0:
                        pe.wait_ge(loaded[k], 16 * (fills[k] + 1) + 16 * it)
                    for t, bank_ in enumerate((GATE, UP)):
                        for half in range(2):
                            c0 = t * D + half * 512
                            if k < 0:
                                lhsT, rhs = onehot, bgu[:, c0:c0 + 512]
                            else:
                                lhsT, rhs = xT[:, k % 4, k // 4, :], ring[:, k, c0:c0 + 512]
                            ins = mm(PS[half * CAP:(half + 1) * CAP, bank_, :], lhsT, rhs,
                                     start=(k < 0), stop=(k == KT - 1))
                    if k >= 0:
                        ins.then_inc(used[k], 1)
                pe.wait_ge(E_dve.sem, E_dve.before + it * len(E_dve.names))
                for n in range(NT):
                    ins = tr(PS[:, SC, n * P:(n + 1) * P], SG[:, n, :], ident)
                ins.then_inc(*E_pe.ends("trS", it))
                gather(E_pe, E_dve.past("S1", it), it)
                pe.wait_ge(*E_dve.past("hid", it))
                tiles_turned(SC + 2, ehid, E_pe, "trH", it)
                pe.wait_ge(*E_act.past("xg", it))
                tiles_turned(SC + 1, xgs, E_pe, "trX", it)
                pe.wait_ge(*E_act.past("hidT", it))
                for f in range(FT):
                    s = FT + f // 2
                    if f % 2 == 0:
                        pe.wait_ge(loaded[s], 16 * (fills[s] + 1) + 16 * it)
                    for half in range(2):
                        ins = mm(PS[half * CAP:(half + 1) * CAP, DN, :], hidT[:, f % 4, f // 4, :],
                                 ring2[:, s, f % 2, half * 512:(half + 1) * 512], start=(f == 0), stop=(f == FT - 1))
                    if f % 2:
                        ins.then_inc(used[s], 1)
                pe.wait_ge(*E_act.past("Y", it))
                for n in range(NT):
                    for half in range(2):
                        ins = mm(PS[:, SC + 2 * n + half, :], ST[half * CAP:(half + 1) * CAP, n, :],
                                 Y[half * CAP:(half + 1) * CAP, :], start=True, stop=True)
                ins.then_inc(*E_pe.ends("scatter", it))

        @block.scalar
        def _(act):
            A = nc.scalar.activation
            act.dma_start(V[:, :], vec).then_inc(vec_loaded, 16)
            act.dma_start(R[:, :], row).then_inc(row_loaded, 16)
            act.dma_start(W_ba[:, :, :], w_ba[0]).then_inc(ba_loaded, 16)
            act.dma_start(W_r[:, :, :], w_ba[1]).then_inc(ba_loaded, 16)

            def flat(ap):
                return ap.rearrange("p a n -> p (a n)")

            def squares(src, steps):
                for n in range(NT):
                    A(flat(hn)[:, n * D:(n + 1) * D], src[:, n, :], ACT.Square,
                      accum_out=ss[:, 2, n:n + 1]).then_inc(*steps.ends(f"ss{n}"))

            act.wait_ge(x_loaded, 16)
            squares(h, A_act)
            act.wait_ge(*B_pe.past("ba"))
            A(tb.rearrange("p (n e) -> p n e", n=NT), PS[:, 4, 0:64].rearrange("p (n e) -> p n e", n=NT)[:, :, 0:VH],
              ACT.Tanh, scale=0.5).then_inc(*B_act.ends("tanh_b"))
            act.wait_ge(*B_dve.past("abs"))
            A(spy, spa, ACT.Exp, scale=-1.0).then_inc(*B_act.ends("exp_abs"))
            act.wait_ge(row_loaded, 16)
            A(exA, R[:, 48:64], ACT.Exp).then_inc(*B_act.ends("exp_A"))
            act.wait_ge(*B_dve.past("gc_last"))
            A(kdec[:, :], small[:, 0, 0:VH], ACT.Exp).then_inc(*B_act.ends("kdec"))
            A(small[:, 1, 0:32], gsum[:, :, :].rearrange("p a n -> p (a n)"), ACT.Exp).then_inc(*B_act.ends("eg"))

            with act.Fori(0, RGB) as i:
                act.wait_ge(used[S_RG[0]], i + 1)
                act.wait_ge(*A_dve.past("pad"))
                act.wait_ge(C_dve.sem, i * len(C_dve.names))
                A(rawp[:, 0:2, 3:3 + T], bank3(0, 2), ACT.Copy).then_inc(xy_copied, 1)
                act.wait_ge(used[S_RG[1]], i + 1)
                A(yraw[:, :, :], bank3(1, 2), ACT.Copy).then_inc(xy_copied, 1)
                act.wait_ge(xy_copied, 2 * i + 2)
                A(y2b[:, :, :], yraw[:, :, :], ACT.Square).then_inc(*C_act.ends("y2"))
                act.wait_ge(*C_dve.past("cub_y", i))
                A(ty[:, :, :], q3[:, :, :], ACT.Tanh, scale=GELU_C).then_inc(*C_act.ends("tanh_y"))
                act.wait_ge(used[S_RG[2]], i + 1)
                act.wait_ge(*B_dve.past("hb"))
                for gate_i, (dst, name) in enumerate(((ta, "tanh_a"), (ti, "tanh_i"))):
                    for jt in range(2):
                        ins = A(dst[:, jt, :], PS[:, 2 + gate_i, jt * T:(jt + 1) * T], ACT.Tanh, scale=0.5,
                                bias=hb[:, bass.ds(2 * i + gate_i * KT + jt, 1)])
                    ins.then_inc(*C_act.ends(name))
                act.wait_ge(*C_dve.past("l1", i))
                A(arg[:, bass.ds(2 * i, 2), :], L[:, :, :], ACT.Exp, scale=-1.0).then_inc(*C_act.ends("decay"))
                A(ta[:, :, :], L[:, :, :], ACT.Tanh).then_inc(*C_act.ends("tanh_l"))
            def tanh_qk(r):
                act.wait_ge(*N_dve.past("cqk7", r))
                A(thq[:, :, :], cqk[:, :, :], ACT.Tanh, scale=0.5).then_inc(*N_act.ends("tanh_qk", r))

            def square_qk(r):
                act.wait_ge(*N_dve.past("s_qk", r))
                A(thq[:, :, :], cqk[:, :, :], ACT.Square, scale=0.5).then_inc(*N_act.ends("sq_qk", r))

            def tanh_v(r):
                act.wait_ge(*N_dve.past("cv7", r))
                A(thv[:, :, :], cv[:, :, :], ACT.Tanh, scale=0.5).then_inc(*N_act.ends("tanh_v", r))

            act.wait_ge(used[S_GDN[0]], 1)
            act.wait_ge(*C_dve.past("gelu", RGB - 1))
            A(rawp[:, 0:2, 3:3 + T], bank3(0, 2), ACT.Copy).then_inc(qk_copied, 1)
            act.wait_ge(used[S_GDN[1]], 1)
            A(rawp[:, 2:4, 3:3 + T], bank3(1, 2), ACT.Copy).then_inc(v_copied, 1)
            act.wait_ge(*C_dve.past("guard", RGB - 1))
            A(mrg, mrg, ACT.Sqrt).then_inc(*Ct_act.ends("sqrt"))
            act.wait_ge(used[S_GDN[2]], 1)
            A(zraw[:, :, :], bank3(0, 2), ACT.Copy).then_inc(z_copied, 1)
            act.wait_ge(ow_zero, 1)
            A(osq[:, :, :], ow[:, :, :], ACT.Square).then_inc(osq_ready, 1)
            tanh_qk(0)
            square_qk(0)
            tanh_v(0)

            def gdn_head(g, final):
                act.wait_ge(*G_pe.past("G", g))
                A(eG[:, :, :], bank3(6, 2)[:, :, P:2 * P], ACT.Exp).then_inc(*G_act.ends("eG", g))
                act.wait_ge(*G_dve.past("D3", g))
                A(Dt[:, :, :, :], Dt[:, :, :, :], ACT.Exp).then_inc(*G_act.ends("Dt", g))
                act.wait_ge(z_copied, g + 1)
                A(zs[:, :, :], zraw[:, :, :], ACT.Tanh, scale=0.5).then_inc(*G_act.ends("tanh_z", g))
                act.wait_ge(*N_dve.past("QK", g))
                A(k1, QK[:, 1, 0, :], ACT.Copy).then_inc(*G_act.ends("k1", g))
                act.wait_ge(*G_pe.past("trv", g))
                A(Vt[:, :, :, :].rearrange("p a b c -> p (a b c)"), bank(2), ACT.Copy, scale=0.5)\
                    .then_inc(*G_act.ends("Vt", g))
                if not final:
                    act.wait_ge(used[S_GDN[0]], g + 2)
                    A(rawp[:, 0:2, 3:3 + T], bank3(0, 2), ACT.Copy).then_inc(qk_copied, 1)
                act.wait_ge(*G_pe.past("trUA", g))
                A(XU[:, 0:2, 0, :], bank3(2, 4)[:, 0:2, :], ACT.Copy).then_inc(*G_act.ends("XA", g))
                act.wait_ge(*G_pe.past("trUB", g))
                A(XU[:, 2:4, 0, :], bank3(7, 4)[:, 0:2, :], ACT.Copy).then_inc(*G_act.ends("XB", g))
                for lv in range(1, LEVELS):
                    act.wait_ge(*G_pe.past(f"P1A_{lv}", g))
                    A(P1s[:, 0:2, :], bank3(2, 4)[:, 0:2, :], ACT.Copy).then_inc(*G_act.ends(f"P1sA_{lv}", g))
                    if lv == 4 and not final:
                        tanh_qk(g + 1)
                    act.wait_ge(*G_pe.past(f"P1B_{lv}", g))
                    A(P1s[:, 2:4, :], bank3(7, 4)[:, 0:2, :], ACT.Copy).then_inc(*G_act.ends(f"P1sB_{lv}", g))
                    if lv == 4 and not final:
                        square_qk(g + 1)
                        act.wait_ge(used[S_GDN[1]], g + 2)
                        A(rawp[:, 2:4, 3:3 + T], bank3(1, 2), ACT.Copy).then_inc(v_copied, 1)
                act.wait_ge(*G_pe.past("S1", g))
                A(flat(S1[:, :, :]), PS[:, 6, 0:T], ACT.Copy).then_inc(*G_act.ends("S1", g))
                if not final:
                    tanh_v(g + 1)
                    act.wait_ge(used[S_GDN[2]], g + 2)
                    act.wait_ge(*G_dve.past("s_z", g))
                    A(zraw[:, :, :], bank3(0, 2), ACT.Copy).then_inc(z_copied, 1)
                act.wait_ge(*G_pe.past("O", g))
                A(osq[:, :, :], bank3(5, 2), ACT.Square).then_inc(osq_ready, 1)

            with act.Fori(0, QKH - 1) as g:
                gdn_head(g, False)
            gdn_head(QKH - 1, True)

            with act.Fori(0, KT) as j:
                act.wait_ge(used[S_MIX[0]], j + 1)
                act.wait_ge(M_dve.sem, j * len(M_dve.names))
                A(thq[:, :, :], bank3(0, 2), ACT.Tanh, scale=0.5).then_inc(*M_act.ends("tanh"))
            act.wait_ge(used[S_OUT[3]], fills[S_OUT[3]])
            act.dma_start(rows, ffn_rows).then_inc(rows_loaded, 16)
            act.dma_start(bdn[:, :], b_down).then_inc(bdown_loaded, 16)
            act.wait_ge(*O_dve.past("h3"))
            squares(h, O_act)
            act.wait_ge(*O_dve.past("negm"))
            for n in range(NT):
                A(exs[:, n, :], logits[:, n, :], ACT.Exp, bias=negm[:, n:n + 1]).then_inc(*O_act.ends(f"exp{n}"))
            act.dma_start(bgu, b_gu).then_inc(bgu_loaded, 16)
            act.wait_ge(*O_pe.past("trg"))
            A(gT[:, :], PS[0:NE, 6, 0:T], ACT.Copy).then_inc(*O_act.ends("gT"))

            act.wait_ge(*O_dve.past("loops"))
            n_it = act.value_load(loops[0:1, 0:1], min_val=NE, max_val=4 * NE)

            act.wait_ge(*E_pe0.past("gather"))
            A(xgs, bank(2), ACT.Copy).then_inc(*E_act0.ends("xg"))
            act.wait_ge(*E_pe0.past("trX"))
            A(flat(cqk[:, :, :]), bank(5), ACT.Copy).then_inc(*E_act0.ends("xT"))
            with act.Fori(0, n_it) as it:
                act.wait_ge(*E_dve.past("g", it))
                A(eth, eg_, ACT.Tanh, scale=0.5 * ALPHA).then_inc(*E_act.ends("th", it))
                act.wait_ge(*E_pe.past("trS", it))
                A(flat(ST), PS[:, 4, 0:T], ACT.Copy).then_inc(*E_act.ends("ST", it))
                act.wait_ge(*E_pe.past("gather", it))
                A(xgs, bank(2), ACT.Copy).then_inc(*E_act.ends("xg", it))
                act.wait_ge(*E_pe.past("trH", it))
                A(flat(cv[:, :, :]), bank(6), ACT.Copy).then_inc(*E_act.ends("hidT", it))
                act.wait_ge(*E_pe.past("trX", it))
                A(flat(cqk[:, :, :]), bank(5), ACT.Copy).then_inc(*E_act.ends("xT", it))
                act.wait_ge(used[NSLOT - 1], fills[NSLOT - 1] + 1 + it)
                A(Y, bank(3), ACT.Copy, scale=0.5).then_inc(*E_act.ends("Y", it))

            act.wait_ge(E_dve.sem, E_dve.before + n_it * len(E_dve.names))
            squares(h, F_act)

        @block.vector
        def _(dve):
            v = nc.vector

            def convolution(src, dst, tap, bias, steps, names, r):
                if bias is None:
                    ins = v.tensor_scalar(dst, src[:, 3:3 + T], tap(3), None, ALU.mult)
                else:
                    ins = v.tensor_scalar(dst, src[:, 3:3 + T], tap(3), bias, ALU.mult, ALU.add)
                ins.then_inc(*steps.ends(names[0], r))
                for j in range(3):
                    dve.wait_ge(*steps.past(names[j], r))
                    v.scalar_tensor_tensor(dst, src[:, j:j + T], tap(j), dst, ALU.mult, ALU.add)\
                        .then_inc(*steps.ends(names[j + 1], r))

            v.memset(half_pow[:, :], -0.5).then_inc(*A_dve.ends("pow"))
            dve.wait_ge(*A_act.past("ss1"))
            v.tensor_scalar(ss[:, 3, 0:2], ss[:, 2, 0:2], 1.0 / D, EPS, ALU.mult, ALU.add).then_inc(*A_dve.ends("ms"))
            v.memset(rawp[:, :, 0:3], 0.0).then_inc(*A_dve.ends("pad"))
            dve.wait_ge(*A_pool.past("rstd"))
            for n in range(NT):
                v.tensor_scalar(hn[:, n, :], h[:, n, :], ss[:, 1, n:n + 1], None, ALU.mult)\
                    .then_inc(*A_dve.ends(f"xn{n}"))
            dve.wait_ge(vec_loaded, 16)
            for b in range(4):
                dve.wait_ge(*A_pe.past(f"tr{b}"))
                v.tensor_tensor(xnT[:, 2 * b:2 * b + 2, :], bank3(b, 2), last(V[:, 2 * b:2 * b + 2], T), ALU.mult)\
                    .then_inc(*A_dve.ends(f"ev{b}"))

            B = B_dve
            dve.wait_ge(row_loaded, 16)
            dve.wait_ge(*B_act.past("tanh_b"))
            zb = PS[:, 4, 0:64].rearrange("p (n e) -> p n e", n=NT)
            v.tensor_tensor(spx[:, 0:32].rearrange("p (n e) -> p n e", n=NT), zb[:, :, VH:2 * VH], mid(R[:, 32:48], NT), ALU.add)\
                .then_inc(*B.ends("in_ba"))
            o, w = VEC["lam"]
            v.tensor_scalar(spx[:, 32:40], V[:, o:o + w], -1.0, None, ALU.mult).then_inc(*B.ends("in_lam"))
            dve.wait_ge(*B.past("in_lam"))
            v.scalar_tensor_tensor(spa, spx, -1.0, spx, ALU.mult, ALU.max).then_inc(*B.ends("abs"))
            dve.wait_ge(*B_act.past("exp_abs"))
            v.tensor_scalar(spp, spy, 2.0, None, ALU.add).then_inc(*B.ends("y2"))
            dve.wait_ge(*B.past("y2"))
            v.reciprocal(spa, spp).then_inc(*B.ends("s_rec"))
            dve.wait_ge(*B.past("s_rec"))
            v.tensor_tensor(sps, spy, spa, ALU.mult).then_inc(*B.ends("s"))
            dve.wait_ge(*B.past("s"))
            v.tensor_tensor(sps2, sps, sps, ALU.mult).then_inc(*B.ends("s2"))
            dve.wait_ge(*B.past("s2"))
            v.tensor_scalar(spp, sps2, 2.0 / 15, 2.0 / 13, ALU.mult, ALU.add).then_inc(*B.ends("p6"))
            dve.wait_ge(*B.past("p6"))
            for i in range(5, 0, -1):
                v.tensor_tensor(spp, spp, sps2, ALU.mult).then_inc(*B.ends(f"p{i}"))
                dve.wait_ge(*B.past(f"p{i}"))
                v.tensor_scalar(spp, spp, 2.0 / (2 * i + 1), None, ALU.add).then_inc(poly, 1)
                dve.wait_ge(poly, 6 - i)
            v.tensor_tensor(spp, spp, sps2, ALU.mult).then_inc(*B.ends("p0"))
            dve.wait_ge(*B.past("p0"))
            v.scalar_tensor_tensor(spp, spp, 2.0, sps, ALU.add, ALU.mult).then_inc(*B.ends("pos"))
            dve.wait_ge(*B.past("pos"))
            v.scalar_tensor_tensor(sps2, spx, 0.0, spp, ALU.max, ALU.add).then_inc(*B.ends("sp"))
            dve.wait_ge(*B.past("sp"))
            v.tensor_scalar(sp4[:, :], sps2[:, 32:40], RG_C / 2, None, ALU.mult).then_inc(*B.ends("sp4"))
            oa, _ = VEC["ba"]
            v.tensor_scalar(hb[:, :], V[:, oa:oa + 2 * KT], 0.5, None, ALU.mult).then_inc(*B.ends("hb"))
            dve.wait_ge(*B_act.past("tanh_b"))
            v.tensor_scalar(beta[:, :, :].rearrange("p a n -> p (a n)"), tb, 0.5, 0.5, ALU.mult, ALU.add)\
                .then_inc(*B.ends("beta"))
            dve.wait_ge(*B_act.past("exp_A"))
            v.scalar_tensor_tensor(gcol[:, :, :], sps2[:, 0:32].rearrange("p (n e) -> p n e", n=NT), -1.0,
                                   mid(exA, NT), ALU.mult, ALU.mult).then_inc(*B.ends("g"))
            dve.wait_ge(*B_pe.past("cum"))
            v.tensor_copy(gsum[:, :, :].rearrange("p a n -> p (a n)"), PS[:, 5, 0:32]).then_inc(*B.ends("gc"))
            dve.wait_ge(*B.past("gc"))
            v.tensor_tensor(small[:, 0, 0:VH], PS[:, 5, 32:48], gsum[:, 0, :], ALU.subtract)\
                .then_inc(*B.ends("gc_last"))
            dve.wait_ge(*B_act.past("eg"))
            v.tensor_scalar(negeg[:, :, :].rearrange("p a n -> p (a n)"), small[:, 1, 0:32], -1.0, None, ALU.mult)\
                .then_inc(*B.ends("negeg"))
            dve.wait_ge(*B_pe.past("tr"))
            v.tensor_copy(gcT[:, :], PS[0:VH, 6, 0:T]).then_inc(*B.ends("gcT"))

            with dve.Fori(0, RGB) as i:
                S = C_dve
                dve.wait_ge(xy_copied, 2 * i + 1)
                dve.wait_ge(used[S_RG[2]], i)
                for t in range(2):
                    convolution(rawp[:, t, :], xa[:, t, :], lambda j: vcol("rg_cw", j * KT + 2 * i + t),
                                vcol("rg_cb", 2 * i + t), S, [f"conv{4 * t + j}" for j in range(4)], i)
                dve.wait_ge(*C_act.past("y2", i))
                v.tensor_scalar(q3[:, :, :], y2b[:, :, :], GELU_A, 1.0, ALU.mult, ALU.add).then_inc(*S.ends("cub"))
                dve.wait_ge(*S.past("cub", i))
                v.tensor_tensor(q3[:, :, :], q3[:, :, :], yraw[:, :, :], ALU.mult).then_inc(*S.ends("cub_y"))
                dve.wait_ge(*C_act.past("tanh_a", i))
                for jt in range(2):
                    v.tensor_scalar(L[:, jt, :], ta[:, jt, :], 1.0, sp4[:, bass.ds(2 * i + jt, 1)], ALU.add, ALU.mult)\
                        .then_inc(*S.ends(f"l{jt}"))
                dve.wait_ge(*C_act.past("tanh_i", i))
                v.scalar_tensor_tensor(rgo[:, bass.ds(2 * i, 2), :], ti[:, :, :], 1.0, xa[:, :, :], ALU.add, ALU.mult)\
                    .then_inc(*S.ends("gated"))
                dve.wait_ge(*C_act.past("tanh_l", i))
                a_i, m_i = arg[:, bass.ds(2 * i, 2), :], mrg[:, bass.ds(2 * i, 2), :]
                v.tensor_tensor(m_i, a_i, a_i, ALU.mult).then_inc(*S.ends("dec2"))
                dve.wait_ge(*S.past("dec2", i))
                v.scalar_tensor_tensor(m_i, m_i, 1.0, ta[:, :, :], ALU.add, ALU.mult).then_inc(*S.ends("mult"))
                dve.wait_ge(*S.past("mult", i))
                v.tensor_scalar(m_i, m_i, 0.0, None, ALU.max).then_inc(*S.ends("guard"))
                dve.wait_ge(*C_act.past("tanh_y", i))
                v.scalar_tensor_tensor(mixT[:, bass.ds(2 * i, 2), :], ty[:, :, :], 1.0, yraw[:, :, :],
                                       ALU.add, ALU.mult).then_inc(*S.ends("gelu"))
            S = Ct_dve
            dve.wait_ge(*C_dve.past("gelu", RGB - 1))
            v.memset(ow[:, :, :], 0.0).then_inc(ow_zero, 1)
            dve.wait_ge(*Ct_act.past("sqrt"))
            v.memset(mrg[:, :, 0:1], 1.0).then_inc(*S.ends("first"))
            dve.wait_ge(*S.past("first"))
            v.scalar_tensor_tensor(rgo[:, :, :], rgo[:, :, :], 0.5, mrg, ALU.mult, ALU.mult).then_inc(*S.ends("b"))
            dve.wait_ge(*S.past("b"))
            for k in range(KT):
                v.tensor_tensor_scan(mrg[:, k, :], arg[:, k, :], rgo[:, k, :], 0.0, ALU.mult, ALU.add)\
                    .then_inc(*S.ends(f"scan{k}"))
            dve.wait_ge(*S.past(f"scan{KT - 1}"))
            v.scalar_tensor_tensor(rgo[:, :, :], mixT[:, :, :], 0.5, mrg, ALU.mult, ALU.mult).then_inc(*S.ends("out"))
            dve.wait_ge(*S.past("out"))

            def out_sums(steps, pe_steps, r):
                dve.wait_ge(*pe_steps.past("ss_o", r))
                v.tensor_scalar(ss[:, 0, :], PS[:, 7, 4:8], 1.0 / DK, EPS, ALU.mult, ALU.add)\
                    .then_inc(*steps.ends("ss_o", r))

            def out_diag(steps, pool_steps, r):
                dve.wait_ge(*pool_steps.past("r_o", r))
                v.tensor_tensor(diag[:, :, :], mid(con_("ident_half"), 4), last(ss[:, 1, :], P), ALU.mult)\
                    .then_inc(*steps.ends("diag_o", r))

            def out_scaled(steps, pe_steps, g, r):
                dve.wait_ge(*pe_steps.past("bc_o", r))
                v.tensor_tensor(og[:, bass.ds(g, 2), :], ow[:, :, :], bank3(4, 2), ALU.mult)\
                    .then_inc(*steps.ends("og", r))

            N = N_dve

            def taps(r, kind, a, b):
                dst, names, t0 = (cqk, CQK, 0) if kind == "qk" else (cv, CV, 2)
                if a == 0:
                    dve.wait_ge(qk_copied if kind == "qk" else v_copied, r + 1)
                for i in range(a, b):
                    t = i % 2
                    j = (3, 0, 1, 2)[i // 2]
                    w = vcol("gdn_cw", (r * 4 + t0 + t) * 4 + j)
                    src = rawp[:, t0 + t, j:j + T]
                    if i < 2:
                        ins = v.tensor_scalar(dst[:, t, :], src, w, None, ALU.mult)
                    else:
                        dve.wait_ge(*N.past(names[i - 2], r))
                        ins = v.scalar_tensor_tensor(dst[:, t, :], src, w, dst[:, t, :], ALU.mult, ALU.add)
                    ins.then_inc(*N.ends(names[i], r))

            def silu_qk(r):
                dve.wait_ge(*N_act.past("tanh_qk", r))
                v.scalar_tensor_tensor(cqk[:, :, :], thq[:, :, :], 1.0, cqk[:, :, :], ALU.add, ALU.mult)\
                    .then_inc(*N.ends("s_qk", r))

            def sums_qk(r):
                dve.wait_ge(*N_pe.past("ss_qk", r))
                v.tensor_scalar(ss[:, 2, :], PS[:, 6, 0:4], EPS, None, ALU.add).then_inc(*N.ends("ss_qk", r))

            def diag_qk(r):
                dve.wait_ge(*N_pool.past("r_qk", r))
                v.tensor_tensor(diag[:, :, :], con_("ident_qk", 0, 4 * P).rearrange("p (a n) -> p a n", a=4),
                                last(ss[:, 3, :], P), ALU.mult).then_inc(*N.ends("diag_qk", r))

            def select_g(r):
                v.tensor_tensor(rowsel[:, :, :], mid(gcT[:, :], 2),
                                last(C[0:VH, bass.ds(CON["ident"][0] + 2 * r, 2)], T), ALU.mult)\
                    .then_inc(*N.ends("rowsel", r))

            def scale_qk(r):
                dve.wait_ge(*N_pe.past("bc_qk", r))
                v.tensor_tensor(QK[:, :, :, :].rearrange("p n w c -> p w n c"),
                                cqk[:, :, :].rearrange("p w (n c) -> p w n c", n=NT),
                                bank(4).rearrange("p (w n c) -> p w n c", n=NT, w=2), ALU.mult)\
                    .then_inc(*N.ends("QK", r))

            def silu_v(r):
                dve.wait_ge(*N_act.past("tanh_v", r))
                v.scalar_tensor_tensor(cv[:, :, :], thv[:, :, :], 1.0, cv[:, :, :], ALU.add, ALU.mult)\
                    .then_inc(*N.ends("s_v", r))

            taps(0, "qk", 0, 8)
            silu_qk(0)
            taps(0, "v", 0, 2)
            sums_qk(0)
            taps(0, "v", 2, 4)
            diag_qk(0)
            taps(0, "v", 4, 8)
            select_g(0)
            scale_qk(0)
            silu_v(0)

            def gdn_head(g, g_before, final):
                S = G_dve

                def prepare(piece, *args):
                    if not final:
                        piece(g + 1, *args)

                def scaled_by_beta(dst, src, n, j, name, more=None):
                    b = beta[:, n, bass.ds(2 * g + j, 1)]
                    if more is None:
                        ins = v.tensor_scalar(dst, src, b, None, ALU.mult)
                    else:
                        ins = v.tensor_scalar(dst, src, b, more, ALU.mult, ALU.mult)
                    ins.then_inc(*S.ends(name, g))

                out_sums(S, G_pe, g)
                dve.wait_ge(*G_act.past("eG", g))
                for n in range(NT):
                    for j in range(2):
                        v.scalar_tensor_tensor(Dt[:, n, j, :], PS[:, 6, j * T + n * P:j * T + (n + 1) * P],
                                               gsum[:, n, bass.ds(2 * g + j, 1)], neg, ALU.subtract, ALU.add)\
                            .then_inc(*S.ends(f"D{2 * n + j}", g))
                out_diag(S, G_pool, g)
                dve.wait_ge(*G_act.past("Dt", g))
                dve.wait_ge(*G_pe.past("kkqk", g))
                kkqk = bank(5).rearrange("p (n w c) -> p n w c", n=NT, w=2)
                for n in range(NT):
                    for j in range(2):
                        v.scalar_tensor_tensor(MT[:, n, j, :], Dt[:, n, j, :], beta[:, n, bass.ds(2 * g + j, 1)],
                                               kkqk[:, n, 0, :], ALU.mult, ALU.mult)\
                            .then_inc(*S.ends(f"M{2 * n + j}", g))
                dve.wait_ge(*G_pe.past("trk", g))
                v.tensor_copy(kt0[:, :], PS[:, 7, P:2 * P]).then_inc(*S.ends("kt0", g))
                v.tensor_tensor(attT[:, :, :, :], Dt[:, :, :, :],
                                kkqk[:, :, 1, :].unsqueeze(2).broadcast_to([P, NT, 2, P]), ALU.mult)\
                    .then_inc(*S.ends("att", g))
                v.tensor_tensor(qd[:, :, :], eG[:, :, :], mid(QK[:, 1, 1, :], 2), ALU.mult).then_inc(*S.ends("qd", g))
                dve.wait_ge(*G_pool.past("MM0", g))
                v.tensor_tensor(XU[:, :, 1, :], mid(ident, 4), MM[:, 0, :, :], ALU.subtract).then_inc(*S.ends("U", g))
                out_scaled(S, G_pe, g_before, g)
                dve.wait_ge(*G_act.past("tanh_z", g))
                v.scalar_tensor_tensor(zs[:, :, :], zs[:, :, :], 1.0, zraw[:, :, :], ALU.add, ALU.mult)\
                    .then_inc(*S.ends("s_z", g))

                def update(c, lv):
                    name = "AB"[c]
                    dve.wait_ge(*G_pe.past(f"P2{name}_{lv}", g))
                    if lv == 1:
                        dve.wait_ge(*G_act.past(f"X{name}", g))
                    else:
                        dve.wait_ge(*S.past(f"XU{name}_{lv - 1}", g))
                    px = PS[:, 3 + c, :].rearrange("p (u w c) -> p u w c", u=2, w=2)
                    xu = XU[:, 2 * c:2 * c + 2, :, :]
                    if lv == LEVELS - 1:
                        px, xu = px[:, :, 1, :], xu[:, :, 1, :]
                    v.tensor_tensor(xu, xu, px, ALU.subtract).then_inc(*S.ends(f"XU{name}_{lv}", g))

                update(0, 1)
                prepare(taps, "qk", 0, 2)
                for lv in range(2, LEVELS):
                    update(1, lv - 1)
                    if lv in (2, 3):
                        prepare(taps, "qk", 4 * lv - 6, 4 * lv - 4)
                    if lv == 5:
                        prepare(silu_qk)
                    if lv == 6:
                        prepare(sums_qk)
                    update(0, lv)
                    if lv == 2:
                        prepare(taps, "qk", 4, 6)
                    if lv == 5:
                        prepare(taps, "v", 0, 2)
                top = LEVELS - 1
                dve.wait_ge(*G_pe.past("vn0", g))
                for j in range(2):
                    scaled_by_beta(vk[:, j, :], PS[:, 2, j * P:(j + 1) * P], 0, j, f"vk{j}",
                                   kdec[:, bass.ds(2 * g + j, 1)])
                update(1, top)
                for j in range(2):
                    scaled_by_beta(vn[:, 0, j, :], PS[:, 2, j * P:(j + 1) * P], 0, j, f"vn0{j}")
                prepare(taps, "v", 2, 4)
                prepare(diag_qk)
                dve.wait_ge(*G_pe.past("kS", g))
                for j in range(2):
                    v.scalar_tensor_tensor(rr[:, j, :], PS[:, 3, j * P:(j + 1) * P], negeg[:, 1, bass.ds(2 * g + j, 1)],
                                           Vt[:, 1, j, :], ALU.mult, ALU.add).then_inc(*S.ends(f"r{j}", g))
                prepare(taps, "v", 4, 8)
                prepare(select_g)
                dve.wait_ge(*G_pe.past("vn1", g))
                for j in range(2):
                    scaled_by_beta(vn[:, 1, j, :], PS[:, 3, T + j * P:T + (j + 1) * P], 1, j, f"vn1{j}")
                prepare(scale_qk)
                prepare(silu_v)
                dve.wait_ge(osq_ready, g + 2)
                dve.wait_ge(*S.past("s_z", g))
                v.scalar_tensor_tensor(ow[:, :, :], bank3(5, 2), vcol("gdn_norm", 0), zs[:, :, :], ALU.mult, ALU.mult)\
                    .then_inc(*S.ends("ow", g))
                dve.wait_ge(*S.past("ow", g))

            with dve.Fori(0, QKH - 1) as g:
                gdn_head(g, (g + (QKH - 1)) % QKH * 2, False)
            gdn_head(QKH - 1, 2 * (QKH - 2), True)
            out_sums(Z_dve, Z_pe, 0)
            out_diag(Z_dve, Z_pool, 0)
            out_scaled(Z_dve, Z_pe, 2 * (QKH - 1), 0)

            with dve.Fori(0, KT) as j:
                S = M_dve
                dve.wait_ge(*M_act.past("tanh", j))
                dve.wait_ge(used[S_MIX[1]], j + 1)
                v.scalar_tensor_tensor(thv[:, 0, :], thq[:, 1, :], 1.0, PS[:, 1, 0:T], ALU.add, ALU.mult)\
                    .then_inc(*S.ends("a"))
                dve.wait_ge(used[S_MIX[2]], j + 1)
                v.scalar_tensor_tensor(thv[:, 1, :], thq[:, 0, :], 1.0, PS[:, 2, 0:T], ALU.add, ALU.mult)\
                    .then_inc(*S.ends("b"))
                dve.wait_ge(*S.past("b", j))
                v.tensor_tensor(mixT[:, bass.ds(j, 1), :].rearrange("p a n -> p (a n)"), thv[:, 0, :], thv[:, 1, :],
                                ALU.add).then_inc(*S.ends("mix"))

            S = O_dve

            def step(name):
                dve.wait_ge(*S.past(name))

            dve.wait_ge(used[S_OUT[3]], fills[S_OUT[3]])
            for i in range(4):
                n, f = i // 2, i % 2
                hh = h[:, n, f * 512:(f + 1) * 512]
                v.scalar_tensor_tensor(hh, bank(4 + i), 0.5, hh, ALU.mult, ALU.add).then_inc(*S.ends(f"h{i}"))
            dve.wait_ge(*O_act.past("ss1"))
            v.tensor_scalar(ss[:, 3, 0:2], ss[:, 2, 0:2], 1.0 / D, EPS, ALU.mult, ALU.add).then_inc(*S.ends("ms"))
            dve.wait_ge(*O_pool.past("rstd"))
            dve.wait_ge(rows_loaded, 16)
            for n in range(NT):
                v.scalar_tensor_tensor(hn[:, n, :], h[:, n, :], ss[:, 1, n:n + 1], rows[:, 0, :], ALU.mult, ALU.mult)\
                    .then_inc(*S.ends(f"hn{n}"))
            for b in range(4):
                dve.wait_ge(*O_pe.past(f"tr{b}"))
                v.tensor_copy(xnT[:, 2 * b:2 * b + 2, :], bank3(b, 2)).then_inc(*S.ends(f"ev{b}"))
            dve.wait_ge(*O_pe.past("router"))
            v.tensor_tensor(logits, PS[:, 4, 0:2 * NE].rearrange("p (n e) -> p n e", n=NT), mid(R[:, 0:NE], NT),
                            ALU.add).then_inc(*S.ends("logits"))
            step("logits")
            for n in range(NT):
                v.max(mx8[:, n, :], logits[:, n, :]).then_inc(*S.ends(f"max{n}"))
            step("max1")
            v.tensor_scalar(negm, mx8[:, :, 0], -1.0, None, ALU.mult).then_inc(*S.ends("negm"))
            for n in range(NT):
                v.tensor_scalar(gt[:, n, :], logits[:, n, :], mx8[:, n, TOP - 1:TOP], None, ALU.is_gt)\
                    .then_inc(*S.ends(f"gt{n}"))
            step("gt1")
            v.tensor_reduce(ngt, gt, AX, ALU.add).then_inc(*S.ends("ngt"))
            for n in range(NT):
                v.tensor_scalar(eq[:, n, :], logits[:, n, :], mx8[:, n, TOP - 1:TOP], None, ALU.is_equal)\
                    .then_inc(*S.ends(f"eq{n}"))
            step("ngt")
            v.tensor_scalar(need, ngt, -1.0, float(TOP), ALU.mult, ALU.add).then_inc(*S.ends("need"))
            step("eq1")
            for n in range(NT):
                v.tensor_tensor_scan(cum[:, n, :], ones[:, 0:NE], eq[:, n, :], 0.0, ALU.mult, ALU.add)\
                    .then_inc(*S.ends(f"cum{n}"))
            step("cum1")
            for n in range(NT):
                v.tensor_scalar(ok[:, n, :], cum[:, n, :], need[:, n:n + 1], None, ALU.is_le)\
                    .then_inc(*S.ends(f"ok{n}"))
            step("ok1")
            v.tensor_tensor(eq, eq, ok, ALU.mult).then_inc(*S.ends("eqok"))
            step("eqok")
            v.tensor_tensor(sel_, gt, eq, ALU.add).then_inc(*S.ends("sel"))
            step("sel")
            dve.wait_ge(*O_act.past("exp1"))
            v.tensor_tensor(exs, exs, sel_, ALU.mult).then_inc(*S.ends("exs"))
            step("exs")
            v.tensor_reduce(gsm, exs, AX, ALU.add).then_inc(*S.ends("sum"))
            step("sum")
            v.reciprocal(grec, gsm).then_inc(*S.ends("rec"))
            step("rec")
            for n in range(NT):
                v.tensor_scalar(gate[:, n, :], exs[:, n, :], grec[:, n:n + 1], None, ALU.mult)\
                    .then_inc(*S.ends(f"gate{n}"))
            dve.wait_ge(*O_pe.past("pos"))
            v.scalar_tensor_tensor(posm, PS[:, 5, 0:2 * NE].rearrange("p (n e) -> p n e", n=NT), 1.0, sel_,
                                   ALU.add, ALU.mult).then_inc(*S.ends("pos1"))
            step("pos1")
            v.tensor_scalar(posm, posm, -1.0, None, ALU.add).then_inc(*S.ends("posm"))
            v.tensor_reduce(cmax, PS[:, 5, 2 * NE:3 * NE], AX, ALU.max).then_inc(*S.ends("cmax"))
            step("cmax")
            for c_, k in ((c64, 1), (c128, 2), (c192, 3)):
                v.tensor_scalar(c_, cmax, float(CAP * k), float(NE), ALU.is_gt, ALU.mult)\
                    .then_inc(*S.ends(f"c{CAP * k}"))
            step("c192")
            v.tensor_tensor(c64, c64, c128, ALU.add).then_inc(*S.ends("csum"))
            step("csum")
            v.tensor_tensor(c64, c64, c192, ALU.add).then_inc(*S.ends("csum2"))
            step("csum2")
            v.tensor_scalar(loops[:, :], c64, float(NE), None, ALU.add).then_inc(*S.ends("loops"))
            step("loops")
            dve.wait_ge(*O_pe.past("bd"))
            for i in range(4):
                n, f = i // 2, i % 2
                hh = h[:, n, f * 512:(f + 1) * 512]
                v.tensor_tensor(hh, hh, bank(i), ALU.add).then_inc(*S.ends(f"b{i}"))

            n_it = dve.value_load(loops[0:1, 0:1], min_val=NE, max_val=4 * NE)

            def select(steps, e, r):
                for n in range(NT):
                    v.tensor_scalar(Ssel[:, n, :], con_("slots", 0, CAP), posm[:, n, bass.ds(e, 1)], None,
                                    ALU.is_equal).then_inc(*steps.ends(f"S{n}", r))

            def select_weighted(steps, e, r):
                for n in range(NT):
                    v.tensor_scalar(SG[:, n, :], con_("slots", 0, 2 * CAP), posm[:, n, bass.ds(e, 1)],
                                    gate[:, n, bass.ds(e, 1)], ALU.is_equal, ALU.mult)\
                        .then_inc(*steps.ends(f"SG{n}", r))
                v.tensor_scalar(onehot, ones[0:NE, 0:CAP], C[0:NE, bass.ds(e + CON["ident"][0], 1)], None, ALU.mult)\
                    .then_inc(onehot_ready, 1)
                dve.wait_ge(*steps.past("SG1", r))
                v.tensor_scalar(posm[:, :, bass.ds(e, 1)], posm[:, :, bass.ds(e, 1)], -float(CAP), None, ALU.add)\
                    .then_inc(*steps.ends("next", r))

            step("b3")
            select(E_dve0, 0, 0)
            select_weighted(E_dve0, 0, 0)
            with dve.Fori(0, n_it) as it:
                S = E_dve
                dve.wait_ge(onehot_ready, it + 1)
                dve.wait_ge(E_dve.sem, E_dve.before + it * len(E_dve.names))
                dve.wait_ge(E_pe.sem, E_pe.before + it * len(E_pe.names))
                select(S, (it + 1) % NE, it)
                dve.wait_ge(used[KT - 1], fills[KT - 1] + 1 + it)
                v.tensor_scalar(eg_, bank(0), LIMIT, None, ALU.min).then_inc(*S.ends("g", it))
                v.tensor_scalar(eu, bank(1), LIMIT, -LIMIT, ALU.min, ALU.max).then_inc(*S.ends("u", it))
                dve.wait_ge(*S.past("u", it))
                v.scalar_tensor_tensor(ehid, eu, 1.0, eg_, ALU.add, ALU.mult).then_inc(*S.ends("p", it))
                dve.wait_ge(*S.past("p", it))
                dve.wait_ge(*E_act.past("th", it))
                v.scalar_tensor_tensor(ehid, eth, 1.0, ehid, ALU.add, ALU.mult).then_inc(*S.ends("hid", it))
                dve.wait_ge(*E_pe.past("trS", it))
                select_weighted(S, (it + 1) % NE, it)
                dve.wait_ge(*E_pe.past("scatter", it))
                for i in range(4):
                    n, f = i // 2, i % 2
                    hh = h[:, n, f * 512:(f + 1) * 512]
                    v.tensor_tensor(hh, hh, bank(4 + i), ALU.add).then_inc(*S.ends(f"y{i}", it))
            dve.wait_ge(E_dve.sem, E_dve.before + n_it * len(E_dve.names))

            S = F_dve
            dve.wait_ge(*F_act.past("ss1"))
            v.tensor_scalar(ss[:, 3, 0:2], ss[:, 2, 0:2], 1.0 / D, EPS, ALU.mult, ALU.add).then_inc(*S.ends("ms"))
            dve.wait_ge(*F_pool.past("rstd"))
            for n in range(NT):
                v.scalar_tensor_tensor(hn[:, n, :], h[:, n, :], ss[:, 1, n:n + 1], rows[:, 1, :], ALU.mult, ALU.mult)\
                    .then_inc(*S.ends(f"o{n}"))

        @block.gpsimd
        def _(pool):
            tt = nc.gpsimd.tensor_tensor

            def rsqrt(dst, src, n, ends):
                tt(dst[:, 0:n], src[:, 0:n], half_pow[:, 0:n], ALU.pow).then_inc(*ends)

            pool.wait_ge(*A_dve.past("ms"))
            rsqrt(ss[:, 1, :], ss[:, 3, :], 2, A_pool.ends("rstd"))

            def rsqrt_qk(r):
                pool.wait_ge(*N_dve.past("ss_qk", r))
                rsqrt(ss[:, 3, :], ss[:, 2, :], 4, N_pool.ends("r_qk", r))

            def gdn_head(g, final):
                pool.wait_ge(*G_dve.past("ss_o", g))
                rsqrt(ss[:, 1, :], ss[:, 0, :], 4, G_pool.ends("r_o", g))
                pool.wait_ge(*G_dve.past("M3", g))
                for lv in range(LEVELS):
                    if lv == 3:
                        pool.wait_ge(*G_dve.past("U", g))
                    if lv > 3:
                        pool.wait_ge(*G_pe.past(f"P1B_{lv - 3}", g))
                    tt(MM[:, lv % 3, :, :], MT[:, :, :, :].rearrange("p a b c -> p (a b) c"), mid(mask(lv), 4),
                       ALU.mult).then_inc(*G_pool.ends(f"MM{lv}", g))
                if not final:
                    rsqrt_qk(g + 1)

            rsqrt_qk(0)
            with pool.Fori(0, QKH - 1) as g:
                gdn_head(g, False)
            gdn_head(QKH - 1, True)
            pool.wait_ge(*Z_dve.past("ss_o"))
            rsqrt(ss[:, 1, :], ss[:, 0, :], 4, Z_pool.ends("r_o"))
            pool.wait_ge(*O_dve.past("ms"))
            rsqrt(ss[:, 1, :], ss[:, 3, :], 2, O_pool.ends("rstd"))
            pool.wait_ge(*F_dve.past("ms"))
            rsqrt(ss[:, 1, :], ss[:, 3, :], 2, F_pool.ends("rstd"))
            pool.wait_ge(*F_dve.past("o1"))
            pool.dma_start(out.rearrange("(n p) d -> p n d", p=P), hn).then_inc(stored, 16)
            pool.wait_ge(stored, 16)


def kernel(**inputs):
    import concourse.bacc as bacc
    from concourse.bass_utils import run_bass_kernel_spmd

    a = {k: np.asarray(v) for k, v in inputs.items()}
    f32 = np.float32

    def cols(v):
        return v.reshape(-1, P).T

    cw = a["gdn_conv_w"][0]
    cq, ck, cv_ = cw[:, :D], cw[:, D:2 * D], cw[:, 2 * D:]
    gcw = np.stack([ck.reshape(4, QKH, P), cq.reshape(4, QKH, P),
                    cv_.reshape(4, QKH, 2, P)[:, :, 0], cv_.reshape(4, QKH, 2, P)[:, :, 1]])
    vec = np.concatenate([
        cols(a["norm_mix_w"][0]),
        a["rg_conv_w"][0].reshape(4, KT, P).transpose(2, 0, 1).reshape(P, 4 * KT),
        cols(a["rg_conv_b"][0]), cols(a["rg_gate_a_b"][0].reshape(-1)), cols(a["rg_gate_x_b"][0].reshape(-1)),
        cols(a["rg_lambda"][0]),
        gcw.transpose(3, 2, 0, 1).reshape(P, QKH * 16),
        a["gdn_norm_w"][0].reshape(P, 1),
    ], axis=1)
    row = np.broadcast_to(np.concatenate([a["router_b"][0], a["gdn_dt_bias"][0], a["gdn_A_log"][0]])[None], (P, NROW))
    ffn_rows = np.broadcast_to(np.stack([a["norm_ffn_w"][0], a["norm_final_w"]])[None], (P, 2, D))

    w_in = a["w_in"][0]
    o_b = 2 * D + 2 * D + 2 * 2 * D
    tiles = w_in[:, :o_b].reshape(KT, P, o_b // P, P).transpose(2, 1, 0, 3)
    gate_tiles = w_in[:, o_b + 2 * VH:].reshape(KT, P, 2 * KT, P).transpose(2, 1, 0, 3)

    def pieces(order, src):
        return src[np.array(order)].reshape(-1, 2, P, D).transpose(0, 2, 1, 3).reshape(-1, P, SLOT)

    rg_x, rg_y, q, k, v, z = 0, 8, 16, 24, 32, 48
    w_rg = pieces([t for i in range(RGB) for o in (rg_x, rg_y) for t in (o + 2 * i, o + 2 * i + 1)], tiles)
    w_gdn = pieces([t for g in range(QKH) for t in (k + g, q + g, v + 2 * g, v + 2 * g + 1, z + 2 * g, z + 2 * g + 1)],
                   tiles)
    w_gates = pieces([t for j in range(KT) for t in (j, KT + j)], gate_tiles)
    w_rgg = np.stack([a["rg_gate_a_w"][0], a["rg_gate_x_w"][0]], 1).reshape(RGB, 2, 2, P, 256)\
        .transpose(0, 3, 1, 2, 4).reshape(RGB, P, D)
    w_ba = np.stack([w_in[:, o_b:o_b + 2 * VH], a["router_w"][0]]).reshape(2, KT, P, 32).transpose(0, 2, 1, 3)
    w_bg = a["w_branch_gdn"][0].reshape(VH, P, KT, P).transpose(2, 1, 0, 3).reshape(KT, P, SLOT)
    w_br = a["w_branch_rg"][0].reshape(KT, P, KT, P).transpose(2, 1, 0, 3).reshape(KT, P, D)
    nc = bacc.Bacc("TRN2", target_bir_lowering=False, num_devices=1)
    arrays, args = {}, []
    for name, v_ in (("x", a["x"][0]), ("vec", vec), ("row", row), ("con", constants()),
                     ("w_rg", w_rg.reshape(RGB, 2, P, SLOT)), ("w_rgg", w_rgg), ("w_ba", w_ba),
                     ("w_gdn", w_gdn.reshape(QKH, 3, P, SLOT)), ("w_gates", w_gates), ("w_bg", w_bg), ("w_br", w_br),
                     ("w_out", a["w_out"][0]), ("ffn_rows", ffn_rows), ("moe_gu", a["moe_w_gate_up"][0].reshape(NE, KT, P, SLOT)),
                     ("moe_down", a["moe_w_down"][0]), ("b_gu", a["moe_b_gate_up"][0]), ("b_down", a["moe_b_down"][0])):
        v_ = np.ascontiguousarray(v_)
        assert v_.dtype == f32
        arrays[name] = v_
        args.append(nc.dram_tensor(name, v_.shape, F32, kind="ExternalInput").ap())
    args.append(nc.dram_tensor("out", (T, D), F32, kind="ExternalOutput").ap())
    build(nc, *args)
    r = run_bass_kernel_spmd(nc, [arrays], core_ids=[0])
    return r.results[0]["out"].reshape(1, T, D)
```

```python
from contextlib import ExitStack

import numpy as np

import concourse.bass as bass
from concourse import mybir

F32 = mybir.dt.float32
I32 = mybir.dt.int32
ALU = mybir.AluOpType
ACT = mybir.ActivationFunctionType
AX = mybir.AxisListType.X

P = 128
HALF = P // 2
D = 1024
T = 256
NT = T // P
KT = D // P
RGB = 4
RG_C = 8.0
QKH = 8
VH = 16
DK = 128
LEVELS = 7
NE = 32
TOP = 4
CAP = 64
FT = 8
LIMIT = 7.0
ALPHA = 1.702
EPS = 1e-6
BIG = 1e30
SLOT = 2048
NSLOT = 12
AHEAD = 4
GELU_C = 0.7978845608028654
GELU_A = 0.044715

VEC = {}
_n = 0
for _name, _w in (("norm_mix", KT), ("rg_cw", 4 * KT), ("rg_cb", KT), ("ba", KT), ("bx", KT), ("lam", KT),
                  ("gdn_cw", QKH * 4 * 4), ("gdn_norm", 1)):
    VEC[_name] = (_n, _w)
    _n += _w
NVEC = _n
ROW = {"router_b": (0, NE), "dt_bias": (32, VH), "A_log": (48, VH)}
NROW = 64
CON = {}
_n = 0
for _name, _w in (("ident", P), ("tri_incl", P), ("tri_strict", P), ("ones", P), ("neg", P), ("masks", LEVELS * P),
                  ("ident_qk", 4 * P), ("ident_half", P), ("slots", 2 * CAP)):
    CON[_name] = (_n, _w)
    _n += _w
NCON = _n


def constants():
    s, c = np.arange(P)[:, None], np.arange(P)[None, :]
    con = np.zeros((P, NCON), np.float32)

    def put(name, v):
        o, w = CON[name]
        con[:, o:o + w] = v

    put("ident", s == c)
    put("tri_incl", s <= c)
    put("tri_strict", s < c)
    put("ones", 1.0)
    put("neg", np.where(c < s, -BIG, 0.0))
    masks = []
    for level in range(LEVELS):
        b = 2 ** level
        masks.append((s // (2 * b) == c // (2 * b)) & (s % (2 * b) < b) & (c % (2 * b) >= b))
    put("masks", np.concatenate(masks, axis=1))
    eye = (s == c).astype(np.float32)
    put("ident_qk", np.concatenate([0.5 * eye] * 2 + [0.5 * DK ** -0.5 * eye] * 2, axis=1))
    put("ident_half", 0.5 * eye)
    put("slots", np.tile(np.arange(CAP), 2)[None, :])
    return con


class Steps:

    def __init__(self, sem, names, rounds=1, lacking=(), before=0):
        self.sem, self.names, self.rounds, self.before = sem, names, rounds, before
        self.short = [n for n in names if n not in lacking]
        self.at = 0

    def _list(self, r):
        return self.short if isinstance(r, int) and r == self.rounds - 1 else self.names

    def ends(self, name, r=0):
        names = self._list(r)
        self.at %= len(names)
        assert names[self.at] == name, (name, names[self.at])
        self.at += 1
        return self.sem, 1

    def past(self, name, r=0):
        return self.sem, self.before + r * len(self.names) + self._list(r).index(name) + 1


def build(nc, x, vec, row, con, w_rg, w_rgg, w_ba, w_gdn, w_gates, w_bg, w_br, w_out, ffn_rows,
          moe_gu, moe_down, b_gu, b_down, out):
    ctx = ExitStack()
    with ctx:
        def sb(name, shape, dt=F32):
            return ctx.enter_context(nc.sbuf_tensor(name, shape, dt))

        def sem(name):
            return ctx.enter_context(nc.semaphore(name))

        ring = sb("ring", [P, NSLOT, SLOT])
        h = sb("h", [P, NT, D])
        xnT = sb("xnT", [P, KT, T])
        mixT = sb("mixT", [P, KT, T])
        rgo = sb("rgo", [P, KT, T])
        og = sb("og", [P, VH, T])
        V = sb("V", [P, NVEC])
        R = sb("R", [P, NROW])
        C = sb("C", [P, NCON])
        W_ba = sb("W_ba", [P, KT, 2 * VH])
        W_r = sb("W_r", [P, KT, NE])
        heads = sb("heads", [P, 4 * (3 + T) + 59 * P])
        taken = [0]

        def head_buffer(*shape):
            n = int(np.prod(shape))
            flat_ = heads[:, taken[0]:taken[0] + n]
            taken[0] += n
            return flat_ if len(shape) == 1 else (
                flat_.rearrange("p (a b) -> p a b", a=shape[0]) if len(shape) == 2 else
                flat_.rearrange("p (a b c) -> p a b c", a=shape[0], b=shape[1]))

        rawp = head_buffer(4, 3 + T)
        cqk = sb("cqk", [P, 2, T])
        cv = sb("cv", [P, 2, T])
        thq = sb("thq", [P, 2, T])
        thv = sb("thv", [P, 2, T])
        zraw = sb("zraw", [P, 2, T])
        zs = head_buffer(2, T)
        QK = head_buffer(NT, 2, P)
        kt0 = head_buffer(P)
        attT = head_buffer(NT, 2, P)
        MT = sb("MT", [P, NT, 2, P])
        MM = head_buffer(3, 4, P)
        XU = head_buffer(4, 2, P)
        vn = head_buffer(NT, 2, P)
        vk = head_buffer(2, P)
        S1 = head_buffer(2, P)
        qd = head_buffer(2, P)
        osq = head_buffer(2, T)
        ow = head_buffer(2, T)
        diag = head_buffer(4, P)
        rowbuf = head_buffer(2, T)
        rowsel = rowbuf[0:VH, :, :]
        Vt = mixT[:, 2:4, :].rearrange("p j (n c) -> p j n c", n=2)
        Dt = mixT[:, 0:2, :].rearrange("p j (n c) -> p j n c", n=2)
        P1s = mixT[:, 0:2, :].rearrange("p j (n c) -> p (j n) c", n=2)
        k1 = mixT[:, 4, 0:P]
        rr = vk
        eG = rowbuf[:, :, 0:P]
        beta = sb("beta", [P, NT, VH])
        gcol = sb("gcol", [P, NT, VH])
        gsum = sb("gsum", [P, NT, VH])
        negeg = sb("negeg", [P, NT, VH])
        kdec = sb("kdec", [P, VH])
        gcT = sb("gcT", [VH, T])
        small = sb("small", [P, 8, 48])
        ss = sb("ss", [P, 4, 4])
        half_pow = sb("half_pow", [P, 4])
        sp4 = sb("sp4", [P, KT])
        hb = sb("hb", [P, 2 * KT])
        loops = sb("loops", [P, 1], I32)
        PS = ctx.enter_context(nc.psum_tensor("PS", [P, 8, 512], F32))

        def vcol(name, i, n=1):
            o, _ = VEC[name]
            return V[:, bass.ds(o + i, n)]

        def con_(name, a=0, n=P):
            o, _ = CON[name]
            return C[:, o + a:o + a + n]

        ident, tri_incl, tri_strict = con_("ident"), con_("tri_incl"), con_("tri_strict")
        ones, neg = con_("ones"), con_("neg")

        def mask(level):
            return con_("masks", level * P)

        def bank(i):
            return PS[:, i, :]

        def bank3(i, a):
            return PS[:, i, :].rearrange("p (a n) -> p a n", a=a)

        def mid(ap, n):
            return ap.unsqueeze(1).broadcast_to([ap.shape[0], n, ap.shape[1]])

        def last(ap, n):
            return ap.unsqueeze(2).broadcast_to([ap.shape[0], ap.shape[1], n])

        x_loaded, con_loaded = [sem(f"x_loaded{n}") for n in range(NT)], sem("con_loaded")
        vec_loaded, row_loaded, ba_loaded = sem("vec_loaded"), sem("row_loaded"), sem("ba_loaded")
        loaded = [sem(f"loaded{s}") for s in range(NSLOT + AHEAD)]
        used = [sem(f"used{s}") for s in range(NSLOT + AHEAD)]
        row_ffn_loaded, row_final_loaded = sem("row_ffn_loaded"), sem("row_final_loaded")
        bdown_loaded, stored = sem("bdown_loaded"), sem("stored")
        bgu_loaded = sem("bgu_loaded")

        A_act = Steps(sem("a_act"), ["ss0", "ss1"])
        A_pool = Steps(sem("a_pool"), ["rstd0", "rstd1"])
        A_dve = Steps(sem("a_dve"), ["pow", "ms0", "pad", "ms1", "xn0", "xn1", "ev0", "ev1", "ev2", "ev3"])
        A_pe = Steps(sem("a_pe"), ["tr0", "tr1", "tr2", "tr3"])
        SP_DVE = ["in_ba", "in_lam", "abs", "y2", "s_rec", "s", "s2",
                  "p6", "p5", "p4", "p3", "p2", "p1", "p0", "pos", "sp"]
        B_dve = Steps(sem("b_dve"), SP_DVE + ["sp4", "hb", "beta", "g", "gc", "gc_last", "negeg", "gcT"])
        B_act = Steps(sem("b_act"), ["tanh_b", "exp_abs", "exp_A", "kdec", "eg"])
        B_pe = Steps(sem("b_pe"), ["ba", "cum", "tr"])

        xy_copied = sem("xy_copied")
        C_act = Steps(sem("c_act"), ["y2", "tanh_y", "tanh_a", "tanh_i", "decay", "tanh_l"], RGB)
        C_dve = Steps(sem("c_dve"), [f"conv{j}" for j in range(8)] + ["cub", "cub_y", "l0", "l1", "gated", "dec2",
                                    "mult", "guard", "gelu"], RGB)
        Ct_act = Steps(sem("ct_act"), ["sqrt"])
        Ct_dve = Steps(sem("ct_dve"), ["first", "b"] + [f"scan{k}" for k in range(KT)] + ["out"])

        CQK, CV = [f"cqk{j}" for j in range(8)], [f"cv{j}" for j in range(8)]
        N_pe = Steps(sem("n_pe"), ["ss_qk", "bc_qk"], QKH)
        N_act = Steps(sem("n_act"), ["tanh_qk", "sq_qk", "tanh_v"], QKH)
        N_dve = Steps(sem("n_dve"), CQK + ["s_qk"] + CV[:2] + ["ss_qk"] + CV[2:4] + ["diag_qk"] + CV[4:]
                      + ["rowsel", "QK", "s_v"], QKH)
        N_pool = Steps(sem("n_pool"), ["r_qk"], QKH)
        G_pe = Steps(sem("g_pe"), ["G", "ss_o", "kkqk", "trv", "trk", "bc_o", "trUA", "trUB", "P1A_1", "P2A_1", "P1B_1"]
                     + [s for lv in range(2, LEVELS) for s in (f"P1A_{lv}", f"P2B_{lv - 1}", f"P2A_{lv}", f"P1B_{lv}")]
                     + ["vn0", f"P2B_{LEVELS - 1}", "S1", "kS", "vn1", "O"], QKH)
        G_act = Steps(sem("g_act"), ["eG", "Dt", "tanh_z", "k1", "Vt", "XA", "XB"]
                      + [f"P1s{c}_{lv}" for lv in range(1, LEVELS) for c in "AB"]
                      + ["S1"], QKH)
        G_dve = Steps(sem("g_dve"), ["ss_o", "D0", "D1", "D2", "D3", "diag_o", "M0", "M1", "M2", "M3", "kt0", "att",
                                     "qd", "U", "og", "s_z", "XUA_1"]
                      + [s for lv in range(2, LEVELS) for s in (f"XUB_{lv - 1}", f"XUA_{lv}")]
                      + ["vk0", "vk1", f"XUB_{LEVELS - 1}", "vn00", "vn01", "r0", "r1", "vn10", "vn11", "ow"],
                      QKH)
        G_pool = Steps(sem("g_pool"), ["r_o"] + [f"MM{lv}" for lv in range(LEVELS)], QKH)
        qk_copied, v_copied, z_copied, osq_ready = sem("qk_copied"), sem("v_copied"), sem("z_copied"), sem("osq_ready")
        ow_zero, poly = sem("ow_zero"), sem("poly")
        Z_pe = Steps(sem("z_pe"), ["ss_o", "bc_o"])
        Z_dve = Steps(sem("z_dve"), ["ss_o", "diag_o", "og"])
        Z_pool = Steps(sem("z_pool"), ["r_o"])

        M_act = Steps(sem("m_act"), ["tanh"], KT)
        M_dve = Steps(sem("m_dve"), ["a", "b", "mix"], KT)

        O_pe = Steps(sem("o_pe"), ["out0", "tr0", "tr1", "router0", "tr2", "tr3", "router1", "pos", "trg", "bd"])
        O_act = Steps(sem("o_act"), ["ss0", "ss1", "exp0", "exp1", "gT"])
        O_pool = Steps(sem("o_pool"), ["rstd0", "rstd1"])
        O_dve = Steps(sem("o_dve"), ["h0", "h1", "ms0", "hn0", "h2", "h3", "ev0", "ev1", "ms1", "hn1", "ev2", "ev3",
                                     "logits", "max0", "max1", "negm", "gt0", "gt1", "ngt", "eq0", "eq1",
                                     "need", "cum0", "cum1", "ok0", "ok1", "eqok", "sel",
                                     "exs", "sum", "rec", "gate0", "gate1", "pos1", "posm", "cmax",
                                     "c64", "c128", "c192", "csum", "csum2", "loops",
                                     "b0", "b1", "b2", "b3"])

        E_pe0 = Steps(sem("e_pe"), ["gather", "trX"])
        E_pe = Steps(E_pe0.sem, ["trS", "gather", "trH", "trX", "scatter0", "scatter1"], before=2)
        E_act0 = Steps(sem("e_act"), ["xg", "xT"])
        E_act = Steps(E_act0.sem, ["th", "ST", "xg", "hidT", "xT", "Y"], before=2)
        E_dve0 = Steps(sem("e_dve"), ["S0", "S1", "SG0", "SG1", "next"])
        E_dve = Steps(E_dve0.sem, ["S0", "S1", "g", "u", "p", "hid", "SG0", "SG1", "next", "y0", "y1", "y2", "y3"],
                      before=5)
        onehot_ready = sem("onehot_ready")
        F_act = Steps(sem("f_act"), ["ss0", "ss1"])
        F_pool = Steps(sem("f_pool"), ["rstd0", "rstd1"])
        F_dve = Steps(sem("f_dve"), ["ms0", "ms1", "o0", "o1"])

        S_RG, S_GDN, S_OUT = (0, 1, 2), (3, 4, 5), (0, 9, 10, 11)
        S_MIX = ((6, 7, 8), S_GDN)
        fills = [0] * (NSLOT + AHEAD)
        for slots, n in ((S_RG, RGB), (S_GDN, QKH), (S_MIX[0], KT // 2), (S_MIX[1], KT // 2), (S_OUT, 1)):
            for s in slots:
                fills[s] += n

        def piece_slot(k, p):
            return NSLOT + k if p and k < AHEAD else k

        def piece_fills(k, p, ii):
            return fills[piece_slot(k, p)] + (ii if k < AHEAD else 2 * ii + p)

        def slot(s):
            return ring[:, s, :] if s < NSLOT else heads[:, (s - NSLOT) * SLOT:(s - NSLOT + 1) * SLOT]

        def mix_fills(p, jj):
            return (0, QKH)[p] + jj + 1

        ring4 = ring[:, :, :].rearrange("p s (t k c) -> p s t k c", t=2, k=KT)
        ring16 = ring[:, :, :].rearrange("p s (k c) -> p s k c", c=P)
        ring2 = ring[:, :, :].rearrange("p s (k n) -> p s k n", k=2)

        spx, spy, spa, sps, sps2, spp = (small[:, i, 0:40] for i in range(6))
        tb, exA = small[:, 6, 0:32], small[:, 7, 0:16]
        xa, ta, ti, L, yraw, q3, ty, y2b = cqk, thq, thv, cv, zraw, zs, osq, ow
        mrg, arg = og[:, 0:KT, :], og[:, KT:2 * KT, :]
        rsc = thq[:, :, :].rearrange("p a n -> p (a n)")

        def r32(i):
            return rsc[:, 64 * i:64 * i + 64].rearrange("p (n e) -> p n e", n=NT)

        logits, gt, eq, cum, ok, sel_ = (r32(i) for i in range(6))
        exs, gate = r32(6), r32(7)
        msc = MT[:, :, :, :].rearrange("p a b c -> p (a b c)")
        posm = msc[:, 0:64].rearrange("p (n e) -> p n e", n=NT)
        mx8 = msc[:, 64:80].rearrange("p (n e) -> p n e", n=NT)
        negm, ngt, need, gsm, grec = (msc[:, 80 + 2 * i:82 + 2 * i] for i in range(5))
        cmax, c64, c128, c192 = (msc[:, 96 + i:97 + i] for i in range(4))
        hn = rgo[:, :, :].rearrange("p k t -> p (k t)").rearrange("p (n d) -> p n d", n=NT)
        row_final = mixT[:, :, :].rearrange("p k t -> p (k t)")[:, 0:D]
        ogf = og[:, :, :].rearrange("p k t -> p (k t)")
        row_ffn = ogf[:, 0:D]
        gT, bdn = ogf[0:NE, 2816:2816 + T], ogf[0:NE, 3072:3072 + D]
        bgu = xnT[:, :, :].rearrange("p k t -> p (k t)")[0:NE, :]
        eg_, eu, ehid, Y = (ogf[:, 512 * i:512 * (i + 1)] for i in range(4))
        ST = ogf[:, 2048:2304].rearrange("p (n t) -> p n t", n=NT)
        Ssel = ogf[:, 2304:2432].rearrange("p (n s) -> p n s", n=NT)
        SG = ogf[:, 2432:2688].rearrange("p (n s) -> p n s", n=NT)
        onehot = ogf[0:NE, 2688:2688 + CAP]

        def flat3(t):
            return t[:, :, :].rearrange("p a n -> p (a n)")

        def by_tile(t):
            return flat3(t).rearrange("p (b h s) -> p b h s", h=2, s=CAP)

        mtanh = (thq[:, :, :], cqk[:, :, :])
        xgs, eth = flat3(zraw), flat3(thv)
        xT, hidT = by_tile(cqk), by_tile(cv)

        block = ctx.enter_context(nc.Block())

        @block.sync
        def _(sp):
            def fill(slot, n, src, width=SLOT):
                if not isinstance(n, int) or n > 1:
                    sp.wait_ge(used[slot], n - 1)
                sp.dma_start(ring[:, slot, 0:width], src).then_inc(loaded[slot], 16)

            x_v = x.rearrange("(n p) d -> n p d", p=P)
            for n in range(NT):
                sp.dma_start(h[:, n, :], x_v[n]).then_inc(x_loaded[n], 16)
            sp.dma_start(C[:, :], con).then_inc(con_loaded, 16)

            def fill_rg(i):
                fill(S_RG[0], i + 1, w_rg[bass.ds(i, 1), 0].rearrange("a p n -> (a p) n"))
                fill(S_RG[1], i + 1, w_rg[bass.ds(i, 1), 1].rearrange("a p n -> (a p) n"))
                fill(S_RG[2], i + 1, w_rgg[bass.ds(i, 1)].rearrange("a p n -> (a p) n"), D)

            def fill_gdn(g):
                for j in range(3):
                    fill(S_GDN[j], g + 1, w_gdn[bass.ds(g, 1), j].rearrange("a p n -> (a p) n"))

            fill_rg(0)
            with sp.Fori(1, RGB) as i:
                fill_rg(i)
            fill_gdn(0)
            with sp.Fori(1, QKH) as g:
                fill_gdn(g)
            w_out_v = w_out.rearrange("(i k p) n -> i p k n", k=2, p=P)

            def fill_out(i):
                s = S_OUT[i]
                if fills[s] > 1:
                    sp.wait_ge(used[s], fills[s] - 1)
                sp.dma_start(ring2[:, s, :, :], w_out_v[i]).then_inc(loaded[s], 16)

            for i in range(4):
                fill_out(i)

            def fill_mix(jj, p):
                j, n, slots = 2 * jj + p, mix_fills(p, jj), S_MIX[p]
                fill(slots[0], n, w_gates[bass.ds(j, 1)].rearrange("a p n -> (a p) n"))
                fill(slots[1], n, w_br[bass.ds(j, 1)].rearrange("a p n -> (a p) n"), D)
                fill(slots[2], n, w_bg[bass.ds(j, 1)].rearrange("a p n -> (a p) n"))

            fill_mix(0, 0)

            def fill_piece(k, p, ii):
                s, e = piece_slot(k, p), (2 * ii + p) % NE
                if s >= NSLOT and isinstance(ii, int):
                    sp.wait_ge(*Z_dve.past("og"))
                else:
                    sp.wait_ge(used[s], piece_fills(k, p, ii))
                if k < FT:
                    src = moe_gu[bass.ds(e, 1), k].rearrange("a p n -> (a p) n")
                    sp.dma_start(slot(s), src).then_inc(loaded[s], 16)
                else:
                    src = moe_down[bass.ds(e, 1)].rearrange("a (i k p) n -> (a i) p k n", k=2, p=P)[k - FT]
                    sp.dma_start(ring2[:, s, :, :], src).then_inc(loaded[s], 16)

            for k in (1, 2):
                fill_piece(k, 0, 0)
            fill_mix(0, 1)
            with sp.Fori(1, KT // 2) as jj:
                for p in range(2):
                    fill_mix(jj, p)
            for k in range(AHEAD):
                fill_piece(k, 1, 0)
            for k in (6, 7, 8, 3, 4, 5, 0, 9, 10, 11):
                fill_piece(k, 0, 0)
            sp.wait_ge(*O_dve.past("loops"))
            n_pairs = sp.value_load(loops[0:1, 0:1], min_val=NE // 2, max_val=2 * NE)
            with sp.Fori(0, n_pairs - 1) as ii:
                for p in range(2):
                    for k in range(AHEAD):
                        fill_piece(k, p, ii + 1)
                    for k in range(AHEAD, NSLOT):
                        fill_piece(k, 1 - p, ii + p)
            for k in range(AHEAD, NSLOT):
                fill_piece(k, 1, n_pairs - 1)
            out_v = out.rearrange("(n p) d -> n p d", p=P)
            for n in range(NT):
                sp.wait_ge(*F_dve.past(f"o{n}"))
                sp.dma_start(out_v[n], hn[:, n, :]).then_inc(stored, 16)
            sp.wait_ge(stored, 16 * NT)

        @block.tensor
        def _(pe):
            mm, tr = nc.tensor.matmul, nc.tensor.transpose

            def transposes(src, steps, n):
                for b in (2 * n, 2 * n + 1):
                    for i in range(4):
                        k = 4 * (b % 2) + i
                        ins = tr(PS[:, b, i * P:(i + 1) * P], src[:, n, k * P:(k + 1) * P], ident)
                    ins.then_inc(*steps.ends(f"tr{b}"))

            pe.wait_ge(con_loaded, 16)
            for n in range(NT):
                pe.wait_ge(*A_dve.past(f"xn{n}"))
                transposes(hn, A_pe, n)
            pe.wait_ge(*A_dve.past("ev3"))
            pe.wait_ge(ba_loaded, 32)
            for n in range(NT):
                for k in range(KT):
                    ins = mm(PS[:, 4, n * 32:n * 32 + 32], xnT[:, k, n * P:(n + 1) * P], W_ba[:, k, :],
                             start=(k == 0), stop=(k == KT - 1))
            ins.then_inc(*B_pe.ends("ba"))
            def pair(bank_, slot, a=0, b=2 * KT):
                for i in range(a, b):
                    t, k = i // KT, i % KT
                    ins = mm(PS[:, bank_, t * T:(t + 1) * T], ring4[:, slot, t, k, :], xnT[:, k, :],
                             start=(k == 0), stop=(k == KT - 1))
                return ins

            def rg_projections(i, between=None):
                pe.wait_ge(loaded[S_RG[0]], 16 * (i + 1))
                if not isinstance(i, int):
                    pe.wait_ge(xy_copied, 2 * i)
                pair(0, S_RG[0]).then_inc(used[S_RG[0]], 1)
                if between:
                    between()
                pe.wait_ge(loaded[S_RG[1]], 16 * (i + 1))
                pair(1, S_RG[1]).then_inc(used[S_RG[1]], 1)

            def rg_gates(i):
                pe.wait_ge(loaded[S_RG[2]], 16 * (i + 1))
                pe.wait_ge(*C_dve.past("conv7", i))
                for gate_i in range(2):
                    for jt in range(2):
                        for k in range(2):
                            w0 = gate_i * 512 + k * T + jt * P
                            ins = mm(PS[:, 2 + gate_i, jt * T:(jt + 1) * T], ring[:, S_RG[2], w0:w0 + P],
                                     xa[:, k, :], start=(k == 0), stop=(k == 1))
                ins.then_inc(used[S_RG[2]], 1)

            def cumulative():
                pe.wait_ge(*B_dve.past("g"))
                mm(PS[:, 5, 0:32], tri_incl, gcol[:, :, :], start=True, stop=True)
                mm(PS[:, 5, 32:48], ones, gcol[:, 0, :], start=True, stop=True).then_inc(*B_pe.ends("cum"))

            rg_projections(0, cumulative)
            pe.wait_ge(*B_dve.past("gc"))
            for n in range(NT):
                ins = tr(PS[0:VH, 6, n * P:(n + 1) * P], gsum[:, n, :], ident)
            ins.then_inc(*B_pe.ends("tr"))
            rg_gates(0)
            with pe.Fori(1, RGB) as i:
                rg_projections(i)
                rg_gates(i)

            PJ0, PJ1, P1_A, PX_A, PX_B, QKB, GB, P1_B = range(8)

            def load_wait(j, r):
                pe.wait_ge(loaded[S_GDN[j]], 16 * (r + 1))

            def norm_sums(dst, src):
                for i in range(4):
                    ins = mm(dst[:, i:i + 1], src[:, i // 2, (i % 2) * P:(i % 2 + 1) * P], ones[:, 0:1],
                             start=True, stop=True)
                return ins

            def qk_sums(r):
                pe.wait_ge(*N_act.past("sq_qk", r))
                norm_sums(PS[:, GB, 0:4], thq).then_inc(*N_pe.ends("ss_qk", r))

            def qk_scales(r):
                pe.wait_ge(*N_dve.past("diag_qk", r))
                mm(bank(PX_B), ones, diag[:, :, :], start=True, stop=True).then_inc(*N_pe.ends("bc_qk", r))

            load_wait(0, 0)
            pe.wait_ge(xy_copied, 2 * RGB)
            pair(PJ0, S_GDN[0]).then_inc(used[S_GDN[0]], 1)
            load_wait(1, 0)
            pair(PJ1, S_GDN[1]).then_inc(used[S_GDN[1]], 1)
            qk_sums(0)
            load_wait(2, 0)
            pe.wait_ge(qk_copied, 1)
            pair(PJ0, S_GDN[2], 0, 10)
            qk_scales(0)
            pair(PJ0, S_GDN[2], 10, 2 * KT).then_inc(used[S_GDN[2]], 1)

            M_BANKS = ((0, 1, 2), (3, 6, 7))

            def merge_gates(jj, p, a=0, b=2 * KT):
                s = S_MIX[p][0]
                if a == 0:
                    pe.wait_ge(loaded[s], 16 * mix_fills(p, jj))
                ins = pair(M_BANKS[p][0], s, a, b)
                if b == 2 * KT:
                    ins.then_inc(used[s], 1)

            def branch_rg(jj, p, a=0, b=KT):
                s = S_MIX[p][1]
                if a == 0:
                    pe.wait_ge(loaded[s], 16 * mix_fills(p, jj))
                    pe.wait_ge(*Ct_dve.past("out"))
                for k in range(a, b):
                    ins = mm(PS[:, M_BANKS[p][1], 0:T], ring16[:, s, k, :], rgo[:, k, :],
                             start=(k == 0), stop=(k == KT - 1))
                if b == KT:
                    ins.then_inc(used[s], 1)

            def branch_gdn(jj, p):
                s = S_MIX[p][2]
                pe.wait_ge(loaded[s], 16 * mix_fills(p, jj))
                pe.wait_ge(*Z_dve.past("og"))
                for k in range(VH):
                    ins = mm(PS[:, M_BANKS[p][2], 0:T], ring16[:, s, k, :], og[:, k, :],
                             start=(k == 0), stop=(k == VH - 1))
                ins.then_inc(used[s], 1)

            def gdn_head(g, final):
                def pj_qk(a, b):
                    if final:
                        if a == 0:
                            pe.wait_ge(z_copied, g + 1)
                            merge_gates(0, 0, 0, 4)
                        if a == 12:
                            merge_gates(0, 0, 4, 6)
                        if a == 14:
                            merge_gates(0, 0, 6, 8)
                        return
                    if a == 0:
                        load_wait(0, g + 1)
                        pe.wait_ge(z_copied, g + 1)
                    ins = pair(PJ0, S_GDN[0], a, b)
                    if b == 2 * KT:
                        ins.then_inc(used[S_GDN[0]], 1)

                def pj_vz(a, b):
                    if final:
                        if b in (8, 12, 16, 20):
                            merge_gates(0, 0, b // 2 + 4, b // 2 + 6)
                        if b == 26:
                            pe.wait_ge(v_copied, g + 1)
                            branch_rg(0, 0, 0, 3)
                        if b in (28, 30):
                            branch_rg(0, 0, b // 2 - 11, b // 2 - 10)
                        if b == 32:
                            branch_rg(0, 0, 5, KT)
                        return
                    if a == 0:
                        load_wait(1, g + 1)
                        pe.wait_ge(v_copied, g + 1)
                    if a == 2 * KT:
                        load_wait(2, g + 1)
                        pe.wait_ge(qk_copied, g + 2)
                    if a < 2 * KT:
                        ins = pair(PJ1, S_GDN[1], a, b)
                    else:
                        ins = pair(PJ0, S_GDN[2], a - 2 * KT, b - 2 * KT)
                    if b in (2 * KT, 4 * KT):
                        ins.then_inc(used[S_GDN[1 if b == 2 * KT else 2]], 1)

                pe.wait_ge(*N_dve.past("rowsel", g))
                mm(bank(GB), ones[0:VH, :], rowsel[:, :, :], start=True, stop=True).then_inc(*G_pe.ends("G", g))
                pe.wait_ge(osq_ready, g + 1)
                norm_sums(PS[:, P1_B, 4:8], osq).then_inc(*G_pe.ends("ss_o", g))
                pj_qk(0, 6)
                pe.wait_ge(*G_dve.past("ss_o", g))
                pe.wait_ge(*N_dve.past("QK", g))
                for n in range(NT):
                    ins = mm(PS[:, QKB, n * T:(n + 1) * T], QK[:, n, 0, :], QK[:, n, :, :], start=True, stop=True)
                ins.then_inc(*G_pe.ends("kkqk", g))
                pe.wait_ge(*N_dve.past("s_v", g))
                for n in range(NT):
                    for j in range(2):
                        ins = tr(PS[:, P1_A, (2 * n + j) * P:(2 * n + j + 1) * P], cv[:, j, n * P:(n + 1) * P], ident)
                ins.then_inc(*G_pe.ends("trv", g))
                tr(PS[:, P1_B, P:2 * P], QK[:, 0, 0, :], ident).then_inc(*G_pe.ends("trk", g))
                pj_qk(6, 12)
                pe.wait_ge(*G_dve.past("diag_o", g))
                mm(bank(PX_B), ones, diag[:, :, :], start=True, stop=True).then_inc(*G_pe.ends("bc_o", g))
                pe.wait_ge(*G_dve.past("U", g))
                pe.wait_ge(*G_act.past("Vt", g))
                for c, bank_ in ((0, P1_A), (1, P1_B)):
                    for u in range(2):
                        ins = tr(PS[:, bank_, u * P:(u + 1) * P], XU[:, 2 * c + u, 1, :], ident)
                    ins.then_inc(*G_pe.ends("trUA" if c == 0 else "trUB", g))
                pj_qk(12, 14)

                def m_x(c, lv):
                    for u in (2 * c, 2 * c + 1):
                        if lv == LEVELS - 1:
                            ins = mm(PS[HALF:P, (P1_A, P1_B)[c], (u % 2) * HALF:(u % 2 + 1) * HALF],
                                     MM[0:HALF, lv % 3, u, HALF:P], XU[0:HALF, u, 0, 0:HALF], start=True, stop=True)
                            continue
                        ins = mm(PS[:, (P1_A, P1_B)[c], (u % 2) * P:(u % 2 + 1) * P], MM[:, lv % 3, u, :],
                                 XU[:, u, 0, :], start=True, stop=True)
                    ins.then_inc(*G_pe.ends(f"P1{'AB'[c]}_{lv}", g))

                def x_m_x(c, lv, fill=()):
                    pe.wait_ge(*G_act.past(f"P1s{'AB'[c]}_{lv}", g))
                    for a in fill:
                        pj_vz(a, a + 1)
                    for u in (2 * c, 2 * c + 1):
                        if lv == LEVELS - 1:
                            ins = mm(PS[0:HALF, (PX_A, PX_B)[c], (u % 2) * HALF:(u % 2 + 1) * HALF],
                                     P1s[HALF:P, u, 0:HALF], XU[HALF:P, u, 1, HALF:P], start=True, stop=True)
                            continue
                        o = PS[:, (PX_A, PX_B)[c], (u % 2) * 2 * P:(u % 2 + 1) * 2 * P]
                        mm(o[:, 0:P], XU[:, u, 1, :], P1s[:, u, :], start=True, stop=True)
                        ins = mm(o[:, P:2 * P], P1s[:, u, :], XU[:, u, 1, :], start=True, stop=True)
                    ins.then_inc(*G_pe.ends(f"P2{'AB'[c]}_{lv}", g))

                top = LEVELS - 1
                for lv in range(1, top):
                    pe.wait_ge(*G_pool.past(f"MM{lv}", g))
                    if lv == 1:
                        pe.wait_ge(*G_act.past("XA", g))
                        m_x(0, lv)
                        pj_qk(14, 2 * KT)
                    else:
                        pe.wait_ge(*G_dve.past(f"XUA_{lv - 1}", g))
                        m_x(0, lv)
                        x_m_x(1, lv - 1)
                    x_m_x(0, lv)
                    pj_vz(4 * (lv - 1), 4 * lv - 2)
                    if lv == 1:
                        pe.wait_ge(*G_act.past("XB", g))
                    else:
                        pe.wait_ge(*G_dve.past(f"XUB_{lv - 1}", g))
                    m_x(1, lv)
                    pj_vz(4 * lv - 2, 4 * lv)
                pe.wait_ge(*G_pool.past(f"MM{top}", g))
                pe.wait_ge(*G_dve.past(f"XUA_{top - 1}", g))
                pj_vz(20, 21)
                m_x(0, top)
                x_m_x(1, top - 1)
                if not final:
                    qk_sums(g + 1)
                x_m_x(0, top, (21,))
                pe.wait_ge(*G_dve.past(f"XUB_{top - 1}", g))
                pj_vz(22, 23)
                m_x(1, top)
                pe.wait_ge(*G_dve.past(f"XUA_{top}", g))
                for j in range(2):
                    ins = mm(PS[:, P1_A, j * P:(j + 1) * P], XU[:, j, 1, :], Vt[:, 0, j, :], start=True, stop=True)
                ins.then_inc(*G_pe.ends("vn0", g))
                x_m_x(1, top, (23,))
                pj_vz(24, 26)
                pe.wait_ge(*G_dve.past("vk1", g))
                mm(PS[:, GB, 0:T], kt0[:, :], vk[:, :, :], start=True, stop=True).then_inc(*G_pe.ends("S1", g))
                pj_vz(26, 28)
                pe.wait_ge(*G_act.past("S1", g))
                mm(PS[:, PX_A, 0:T], k1, S1[:, :, :], start=True, stop=True).then_inc(*G_pe.ends("kS", g))
                pj_vz(28, 30)
                pe.wait_ge(*G_dve.past("r1", g))
                for j in range(2):
                    ins = mm(PS[:, PX_A, T + j * P:T + (j + 1) * P], XU[:, 2 + j, 1, :], rr[:, j, :],
                             start=True, stop=True)
                ins.then_inc(*G_pe.ends("vn1", g))
                if not final:
                    qk_scales(g + 1)
                pj_vz(30, 32)
                pe.wait_ge(*G_dve.past("vn11", g))
                for j in range(2):
                    mm(PS[:, QKB, j * T:j * T + P], vn[:, 0, j, :], attT[:, 0, j, :], start=True, stop=True)
                    mm(PS[:, QKB, j * T + P:(j + 1) * T], S1[:, j, :], qd[:, j, :], start=True, stop=False)
                    ins = mm(PS[:, QKB, j * T + P:(j + 1) * T], vn[:, 1, j, :], attT[:, 1, j, :],
                             start=False, stop=True)
                ins.then_inc(*G_pe.ends("O", g))

            with pe.Fori(0, QKH - 1) as g:
                gdn_head(g, False)
            gdn_head(QKH - 1, True)
            merge_gates(0, 1)
            pe.wait_ge(osq_ready, QKH + 1)
            norm_sums(PS[:, P1_B, 4:8], osq).then_inc(*Z_pe.ends("ss_o"))
            branch_rg(0, 1)
            pe.wait_ge(*Z_dve.past("diag_o"))
            mm(bank(PX_B), ones, diag[:, :, :], start=True, stop=True).then_inc(*Z_pe.ends("bc_o"))

            branch_gdn(0, 0)
            branch_gdn(0, 1)
            with pe.Fori(1, KT // 2) as jj:
                for p in range(2):
                    pe.wait_ge(M_dve.sem, (2 * jj + p - 1) * len(M_dve.names))
                    merge_gates(jj, p)
                    branch_rg(jj, p)
                    branch_gdn(jj, p)

            for n in range(NT):
                for i in range(4):
                    s = S_OUT[i]
                    if n == 0:
                        pe.wait_ge(*M_dve.past("mix", 2 * i + 1))
                        pe.wait_ge(loaded[s], 16 * fills[s])
                    for kk in range(2):
                        k = 2 * i + kk
                        for f in range(2):
                            ins = mm(PS[:, 4 + 2 * n + f, :], mixT[:, k, n * P:(n + 1) * P],
                                     ring2[:, s, kk, f * 512:(f + 1) * 512], start=(k == 0), stop=(k == KT - 1))
                    if n == NT - 1 and i < 3:
                        ins.then_inc(used[s], 1)
                if n == 0:
                    ins.then_inc(*O_pe.ends("out0"))
                else:
                    ins.then_inc(used[S_OUT[3]], 1)
            for n in range(NT):
                pe.wait_ge(*O_dve.past(f"hn{n}"))
                transposes(hn, O_pe, n)
                pe.wait_ge(*O_dve.past(f"ev{2 * n + 1}"))
                for k in range(KT):
                    ins = mm(PS[:, 4, n * NE:(n + 1) * NE], xnT[:, k, n * P:(n + 1) * P], W_r[:, k, :],
                             start=(k == 0), stop=(k == KT - 1))
                ins.then_inc(*O_pe.ends(f"router{n}"))
            pe.wait_ge(*O_dve.past("sel"))
            mm(PS[:, 5, 0:NE], tri_strict, sel_[:, 0, :], start=True, stop=True)
            mm(PS[:, 5, NE:2 * NE], ones, sel_[:, 0, :], start=True, stop=False)
            mm(PS[:, 5, NE:2 * NE], tri_strict, sel_[:, 1, :], start=False, stop=True)
            mm(PS[:, 5, 2 * NE:3 * NE], ones, sel_[:, 0, :], start=True, stop=False)
            mm(PS[:, 5, 2 * NE:3 * NE], ones, sel_[:, 1, :], start=False, stop=True).then_inc(*O_pe.ends("pos"))
            GATE, UP, XG, DN, SC = 0, 1, 2, 3, 4
            BIAS = -1

            def gather(steps, sel_done, r):
                pe.wait_ge(*sel_done)
                for n in range(NT):
                    for half in range(2):
                        ins = mm(PS[half * CAP:(half + 1) * CAP, XG, :], Ssel[:, n, :],
                                 hn[:, n, half * 512:(half + 1) * 512], start=(n == 0), stop=(n == NT - 1))
                ins.then_inc(*steps.ends("gather", r))

            def tiles_turned(bank_, src, steps, name, r):
                for b in range(4):
                    ins = tr(PS[:, bank_, b * P:(b + 1) * P], src[:, b * P:(b + 1) * P], ident)
                ins.then_inc(*steps.ends(name, r))

            pe.wait_ge(*O_dve.past("gate1"))
            for n in range(NT):
                ins = tr(PS[0:NE, 0, n * P:(n + 1) * P], gate[:, n, :], ident)
            ins.then_inc(*O_pe.ends("trg"))
            gather(E_pe0, E_dve0.past("S1"), 0)
            pe.wait_ge(*O_act.past("gT"))
            pe.wait_ge(*O_dve.past("cmax"))
            pe.wait_ge(bdown_loaded, 16)

            def output_biases(n):
                for f in range(2):
                    ins = mm(PS[:, SC + 2 * n + f, :], gT[:, n * P:(n + 1) * P], bdn[:, f * 512:(f + 1) * 512],
                             start=True, stop=True)
                return ins

            output_biases(0)
            pe.wait_ge(*E_act0.past("xg"))
            tiles_turned(DN, xgs, E_pe0, "trX", 0)
            output_biases(1).then_inc(*O_pe.ends("bd"))
            pe.wait_ge(*O_dve.past("loops"))
            n_pairs = pe.value_load(loops[0:1, 0:1], min_val=NE // 2, max_val=2 * NE)
            pe.wait_ge(*E_act0.past("xT"))
            pe.wait_ge(bgu_loaded, 16)

            def turn(ii, p):
                it = 2 * ii + p
                pe.wait_ge(onehot_ready, it + 1)
                for k in (0, BIAS, *range(1, KT)):
                    if k != BIAS:
                        pe.wait_ge(loaded[piece_slot(k, p)], 16 * piece_fills(k, p, ii) + 16)
                    for t, bank_ in enumerate((GATE, UP)):
                        for half in range(2):
                            c0 = t * D + half * 512
                            if k == BIAS:
                                lhsT, rhs = onehot, bgu[:, c0:c0 + 512]
                            else:
                                lhsT, rhs = xT[:, k % 4, k // 4, :], slot(piece_slot(k, p))[:, c0:c0 + 512]
                            ins = mm(PS[half * CAP:(half + 1) * CAP, bank_, :], lhsT, rhs,
                                     start=(k == 0), stop=(k == KT - 1))
                    if k != BIAS:
                        ins.then_inc(used[piece_slot(k, p)], 1)
                pe.wait_ge(*O_dve.past("b3"))
                pe.wait_ge(E_dve.sem, E_dve.before + it * len(E_dve.names))
                for n in range(NT):
                    ins = tr(PS[:, SC, n * P:(n + 1) * P], SG[:, n, :], ident)
                ins.then_inc(*E_pe.ends("trS", it))
                gather(E_pe, E_dve.past("S1", it), it)
                pe.wait_ge(*E_dve.past("hid", it))
                tiles_turned(SC + 2, ehid, E_pe, "trH", it)
                pe.wait_ge(*E_act.past("xg", it))
                tiles_turned(SC + 1, xgs, E_pe, "trX", it)
                pe.wait_ge(*E_act.past("hidT", it))
                for f in range(FT):
                    s = FT + f // 2
                    if f % 2 == 0:
                        pe.wait_ge(loaded[s], 16 * piece_fills(s, p, ii) + 16)
                    for half in range(2):
                        ins = mm(PS[half * CAP:(half + 1) * CAP, DN, :], hidT[:, f % 4, f // 4, :],
                                 ring2[:, s, f % 2, half * 512:(half + 1) * 512], start=(f == 0), stop=(f == FT - 1))
                    if f % 2:
                        ins.then_inc(used[s], 1)
                pe.wait_ge(*E_act.past("Y", it))
                for n in range(NT):
                    for half in range(2):
                        ins = mm(PS[:, SC + 2 * n + half, :], ST[half * CAP:(half + 1) * CAP, n, :],
                                 Y[half * CAP:(half + 1) * CAP, :], start=True, stop=True)
                    ins.then_inc(*E_pe.ends(f"scatter{n}", it))

            with pe.Fori(0, n_pairs) as ii:
                for p in range(2):
                    turn(ii, p)

        @block.scalar
        def _(act):
            A = nc.scalar.activation
            act.dma_start(V[:, :], vec).then_inc(vec_loaded, 16)
            act.dma_start(R[:, :], row).then_inc(row_loaded, 16)
            act.dma_start(W_ba[:, :, :], w_ba[0]).then_inc(ba_loaded, 16)
            act.dma_start(W_r[:, :, :], w_ba[1]).then_inc(ba_loaded, 16)

            def flat(ap):
                return ap.rearrange("p a n -> p (a n)")

            def squares(n, steps):
                A(flat(hn)[:, n * D:(n + 1) * D], h[:, n, :], ACT.Square,
                  accum_out=ss[:, 2, n:n + 1]).then_inc(*steps.ends(f"ss{n}"))

            for n in range(NT):
                act.wait_ge(x_loaded[n], 16)
                squares(n, A_act)
            act.wait_ge(*B_pe.past("ba"))
            A(tb.rearrange("p (n e) -> p n e", n=NT), PS[:, 4, 0:64].rearrange("p (n e) -> p n e", n=NT)[:, :, 0:VH],
              ACT.Tanh, scale=0.5).then_inc(*B_act.ends("tanh_b"))
            act.wait_ge(*B_dve.past("abs"))
            A(spy, spa, ACT.Exp, scale=-1.0).then_inc(*B_act.ends("exp_abs"))
            act.wait_ge(row_loaded, 16)
            A(exA, R[:, 48:64], ACT.Exp).then_inc(*B_act.ends("exp_A"))
            act.wait_ge(*B_dve.past("gc_last"))
            A(kdec[:, :], small[:, 0, 0:VH], ACT.Exp).then_inc(*B_act.ends("kdec"))
            A(small[:, 1, 0:32], gsum[:, :, :].rearrange("p a n -> p (a n)"), ACT.Exp).then_inc(*B_act.ends("eg"))

            def rg_round(i):
                act.wait_ge(used[S_RG[0]], i + 1)
                act.wait_ge(*A_dve.past("pad"))
                if not isinstance(i, int):
                    act.wait_ge(C_dve.sem, i * len(C_dve.names))
                A(rawp[:, 0:2, 3:3 + T], bank3(0, 2), ACT.Copy).then_inc(xy_copied, 1)
                act.wait_ge(used[S_RG[1]], i + 1)
                A(yraw[:, :, :], bank3(1, 2), ACT.Copy).then_inc(xy_copied, 1)
                act.wait_ge(xy_copied, 2 * i + 2)
                A(y2b[:, :, :], yraw[:, :, :], ACT.Square).then_inc(*C_act.ends("y2"))
                act.wait_ge(*C_dve.past("cub_y", i))
                A(ty[:, :, :], q3[:, :, :], ACT.Tanh, scale=GELU_C).then_inc(*C_act.ends("tanh_y"))
                act.wait_ge(used[S_RG[2]], i + 1)
                act.wait_ge(*B_dve.past("hb"))
                for gate_i, (dst, name) in enumerate(((ta, "tanh_a"), (ti, "tanh_i"))):
                    for jt in range(2):
                        ins = A(dst[:, jt, :], PS[:, 2 + gate_i, jt * T:(jt + 1) * T], ACT.Tanh, scale=0.5,
                                bias=hb[:, bass.ds(2 * i + gate_i * KT + jt, 1)])
                    ins.then_inc(*C_act.ends(name))
                act.wait_ge(*C_dve.past("l1", i))
                A(arg[:, bass.ds(2 * i, 2), :], L[:, :, :], ACT.Exp, scale=-1.0).then_inc(*C_act.ends("decay"))
                A(ta[:, :, :], L[:, :, :], ACT.Tanh).then_inc(*C_act.ends("tanh_l"))

            rg_round(0)
            with act.Fori(1, RGB) as i:
                rg_round(i)
            def tanh_qk(r):
                act.wait_ge(*N_dve.past("cqk7", r))
                A(thq[:, :, :], cqk[:, :, :], ACT.Tanh, scale=0.5).then_inc(*N_act.ends("tanh_qk", r))

            def square_qk(r):
                act.wait_ge(*N_dve.past("s_qk", r))
                A(thq[:, :, :], cqk[:, :, :], ACT.Square, scale=0.5).then_inc(*N_act.ends("sq_qk", r))

            def tanh_v(r):
                act.wait_ge(*N_dve.past("cv7", r))
                A(thv[:, :, :], cv[:, :, :], ACT.Tanh, scale=0.5).then_inc(*N_act.ends("tanh_v", r))

            act.wait_ge(used[S_GDN[0]], 1)
            act.wait_ge(*C_dve.past("gelu", RGB - 1))
            A(rawp[:, 0:2, 3:3 + T], bank3(0, 2), ACT.Copy).then_inc(qk_copied, 1)
            tanh_qk(0)
            square_qk(0)
            act.wait_ge(used[S_GDN[1]], 1)
            A(rawp[:, 2:4, 3:3 + T], bank3(1, 2), ACT.Copy).then_inc(v_copied, 1)
            act.wait_ge(ow_zero, 1)
            A(osq[:, :, :], ow[:, :, :], ACT.Square).then_inc(osq_ready, 1)
            A(mrg, mrg, ACT.Sqrt).then_inc(*Ct_act.ends("sqrt"))
            tanh_v(0)
            act.wait_ge(used[S_GDN[2]], 1)
            A(zraw[:, :, :], bank3(0, 2), ACT.Copy).then_inc(z_copied, 1)

            def gdn_head(g, final):
                act.wait_ge(*G_pe.past("G", g))
                A(eG[:, :, :], bank3(6, 2)[:, :, P:2 * P], ACT.Exp).then_inc(*G_act.ends("eG", g))
                act.wait_ge(*G_dve.past("D3", g))
                A(Dt[:, :, :, :], Dt[:, :, :, :], ACT.Exp).then_inc(*G_act.ends("Dt", g))
                act.wait_ge(z_copied, g + 1)
                A(zs[:, :, :], zraw[:, :, :], ACT.Tanh, scale=0.5).then_inc(*G_act.ends("tanh_z", g))
                act.wait_ge(*N_dve.past("QK", g))
                A(k1, QK[:, 1, 0, :], ACT.Copy).then_inc(*G_act.ends("k1", g))
                act.wait_ge(*G_pe.past("trv", g))
                A(Vt[:, :, :, :].rearrange("p a b c -> p (a b c)"), bank(2), ACT.Copy, scale=0.5)\
                    .then_inc(*G_act.ends("Vt", g))
                act.wait_ge(*G_pe.past("trUA", g))
                A(XU[:, 0:2, 0, :], bank3(2, 4)[:, 0:2, :], ACT.Copy).then_inc(*G_act.ends("XA", g))
                act.wait_ge(*G_pe.past("trUB", g))
                A(XU[:, 2:4, 0, :], bank3(7, 4)[:, 0:2, :], ACT.Copy).then_inc(*G_act.ends("XB", g))

                def copy_product(c, bank_, lv):
                    us = slice(2 * c, 2 * c + 2)
                    if lv < LEVELS - 1:
                        ins = A(P1s[:, us, :], bank3(bank_, 4)[:, 0:2, :], ACT.Copy)
                    else:
                        ins = A(P1s[HALF:P, us, 0:HALF], bank3(bank_, 8)[HALF:P, 0:2, :], ACT.Copy)
                    ins.then_inc(*G_act.ends(f"P1s{'AB'[c]}_{lv}", g))

                for lv in range(1, LEVELS):
                    act.wait_ge(*G_pe.past(f"P1A_{lv}", g))
                    copy_product(0, 2, lv)
                    if lv == 4 and not final:
                        tanh_qk(g + 1)
                    act.wait_ge(*G_pe.past(f"P1B_{lv}", g))
                    copy_product(1, 7, lv)
                    if lv == 1 and not final:
                        act.wait_ge(used[S_GDN[0]], g + 2)
                        A(rawp[:, 0:2, 3:3 + T], bank3(0, 2), ACT.Copy).then_inc(qk_copied, 1)
                    if lv == 5 and not final:
                        square_qk(g + 1)
                    if lv == 4 and not final:
                        act.wait_ge(used[S_GDN[1]], g + 2)
                        A(rawp[:, 2:4, 3:3 + T], bank3(1, 2), ACT.Copy).then_inc(v_copied, 1)
                act.wait_ge(*G_pe.past("S1", g))
                A(flat(S1[:, :, :]), PS[:, 6, 0:T], ACT.Copy).then_inc(*G_act.ends("S1", g))
                if not final:
                    tanh_v(g + 1)
                    act.wait_ge(used[S_GDN[2]], g + 2)
                    act.wait_ge(*G_dve.past("s_z", g))
                    A(zraw[:, :, :], bank3(0, 2), ACT.Copy).then_inc(z_copied, 1)
                act.wait_ge(*G_pe.past("O", g))
                A(osq[:, :, :], bank3(5, 2), ACT.Square).then_inc(osq_ready, 1)

            with act.Fori(0, QKH - 1) as g:
                gdn_head(g, False)
            gdn_head(QKH - 1, True)

            def merge_tanh(jj, p):
                act.wait_ge(used[S_MIX[p][0]], mix_fills(p, jj))
                if not isinstance(jj, int):
                    act.wait_ge(M_dve.sem, (2 * jj + p - 1) * len(M_dve.names))
                A(mtanh[p], bank3((0, 3)[p], 2), ACT.Tanh, scale=0.5).then_inc(*M_act.ends("tanh"))

            for p in range(2):
                merge_tanh(0, p)
            with act.Fori(1, KT // 2) as jj:
                for p in range(2):
                    merge_tanh(jj, p)
            act.wait_ge(used[S_MIX[1][2]], mix_fills(1, KT // 2 - 1))
            act.dma_start(row_ffn, ffn_rows[:, 0, :]).then_inc(row_ffn_loaded, 16)
            act.dma_start(bdn[:, :], b_down).then_inc(bdown_loaded, 16)
            for n in range(NT):
                act.wait_ge(*O_dve.past(f"h{2 * n + 1}"))
                squares(n, O_act)
            act.dma_start(row_final, ffn_rows[:, 1, :]).then_inc(row_final_loaded, 16)
            act.wait_ge(*O_dve.past("negm"))
            for n in range(NT):
                A(exs[:, n, :], logits[:, n, :], ACT.Exp, bias=negm[:, n:n + 1]).then_inc(*O_act.ends(f"exp{n}"))
            act.dma_start(bgu, b_gu).then_inc(bgu_loaded, 16)
            act.wait_ge(*O_pe.past("trg"))
            A(gT[:, :], PS[0:NE, 0, 0:T], ACT.Copy).then_inc(*O_act.ends("gT"))

            act.wait_ge(*O_dve.past("loops"))
            n_pairs = act.value_load(loops[0:1, 0:1], min_val=NE // 2, max_val=2 * NE)

            act.wait_ge(*E_pe0.past("gather"))
            A(xgs, bank(2), ACT.Copy).then_inc(*E_act0.ends("xg"))
            act.wait_ge(*E_pe0.past("trX"))
            A(flat(cqk[:, :, :]), bank(3), ACT.Copy).then_inc(*E_act0.ends("xT"))

            def turn(it):
                act.wait_ge(*E_dve.past("g", it))
                A(eth, eg_, ACT.Tanh, scale=0.5 * ALPHA).then_inc(*E_act.ends("th", it))
                act.wait_ge(*E_pe.past("trS", it))
                A(flat(ST), PS[:, 4, 0:T], ACT.Copy).then_inc(*E_act.ends("ST", it))
                act.wait_ge(*E_pe.past("gather", it))
                A(xgs, bank(2), ACT.Copy).then_inc(*E_act.ends("xg", it))
                act.wait_ge(*E_pe.past("trH", it))
                A(flat(cv[:, :, :]), bank(6), ACT.Copy).then_inc(*E_act.ends("hidT", it))
                act.wait_ge(*E_pe.past("trX", it))
                A(flat(cqk[:, :, :]), bank(5), ACT.Copy).then_inc(*E_act.ends("xT", it))
                act.wait_ge(used[NSLOT - 1], fills[NSLOT - 1] + 1 + it)
                A(Y, bank(3), ACT.Copy, scale=0.5).then_inc(*E_act.ends("Y", it))

            with act.Fori(0, n_pairs) as ii:
                for p in range(2):
                    turn(2 * ii + p)

            for n in range(NT):
                act.wait_ge(E_dve.sem, E_dve.before - 2 * (NT - 1 - n) + n_pairs * (2 * len(E_dve.names)))
                squares(n, F_act)

        @block.vector
        def _(dve):
            v = nc.vector

            v.memset(half_pow[:, :], -0.5).then_inc(*A_dve.ends("pow"))
            def mean_square(n, act_steps, steps):
                dve.wait_ge(*act_steps.past(f"ss{n}"))
                v.tensor_scalar(ss[:, 3, n:n + 1], ss[:, 2, n:n + 1], 1.0 / D, EPS, ALU.mult, ALU.add)\
                    .then_inc(*steps.ends(f"ms{n}"))

            mean_square(0, A_act, A_dve)
            v.memset(rawp[:, :, 0:3], 0.0).then_inc(*A_dve.ends("pad"))
            mean_square(1, A_act, A_dve)
            for n in range(NT):
                dve.wait_ge(*A_pool.past(f"rstd{n}"))
                v.tensor_scalar(hn[:, n, :], h[:, n, :], ss[:, 1, n:n + 1], None, ALU.mult)\
                    .then_inc(*A_dve.ends(f"xn{n}"))
            dve.wait_ge(vec_loaded, 16)
            for b in range(4):
                n, k0 = b // 2, 4 * (b % 2)
                dve.wait_ge(*A_pe.past(f"tr{b}"))
                v.tensor_tensor(xnT[:, k0:k0 + 4, n * P:(n + 1) * P], bank3(b, 4), last(V[:, k0:k0 + 4], P), ALU.mult)\
                    .then_inc(*A_dve.ends(f"ev{b}"))

            B = B_dve
            dve.wait_ge(row_loaded, 16)
            dve.wait_ge(*B_act.past("tanh_b"))
            zb = PS[:, 4, 0:64].rearrange("p (n e) -> p n e", n=NT)
            v.tensor_tensor(spx[:, 0:32].rearrange("p (n e) -> p n e", n=NT), zb[:, :, VH:2 * VH],
                            mid(R[:, 32:48], NT), ALU.add)\
                .then_inc(*B.ends("in_ba"))
            o, w = VEC["lam"]
            v.tensor_scalar(spx[:, 32:40], V[:, o:o + w], -1.0, None, ALU.mult).then_inc(*B.ends("in_lam"))
            dve.wait_ge(*B.past("in_lam"))
            v.scalar_tensor_tensor(spa, spx, -1.0, spx, ALU.mult, ALU.max).then_inc(*B.ends("abs"))
            dve.wait_ge(*B_act.past("exp_abs"))
            v.tensor_scalar(spp, spy, 2.0, None, ALU.add).then_inc(*B.ends("y2"))
            dve.wait_ge(*B.past("y2"))
            v.reciprocal(spa, spp).then_inc(*B.ends("s_rec"))
            dve.wait_ge(*B.past("s_rec"))
            v.tensor_tensor(sps, spy, spa, ALU.mult).then_inc(*B.ends("s"))
            dve.wait_ge(*B.past("s"))
            v.tensor_tensor(sps2, sps, sps, ALU.mult).then_inc(*B.ends("s2"))
            dve.wait_ge(*B.past("s2"))
            v.tensor_scalar(spp, sps2, 2.0 / 15, 2.0 / 13, ALU.mult, ALU.add).then_inc(*B.ends("p6"))
            dve.wait_ge(*B.past("p6"))
            for i in range(5, 0, -1):
                v.tensor_tensor(spp, spp, sps2, ALU.mult).then_inc(*B.ends(f"p{i}"))
                dve.wait_ge(*B.past(f"p{i}"))
                v.tensor_scalar(spp, spp, 2.0 / (2 * i + 1), None, ALU.add).then_inc(poly, 1)
                dve.wait_ge(poly, 6 - i)
            v.tensor_tensor(spp, spp, sps2, ALU.mult).then_inc(*B.ends("p0"))
            dve.wait_ge(*B.past("p0"))
            v.scalar_tensor_tensor(spp, spp, 2.0, sps, ALU.add, ALU.mult).then_inc(*B.ends("pos"))
            dve.wait_ge(*B.past("pos"))
            v.scalar_tensor_tensor(sps2, spx, 0.0, spp, ALU.max, ALU.add).then_inc(*B.ends("sp"))
            dve.wait_ge(*B.past("sp"))
            v.tensor_scalar(sp4[:, :], sps2[:, 32:40], RG_C / 2, None, ALU.mult).then_inc(*B.ends("sp4"))
            oa, _ = VEC["ba"]
            v.tensor_scalar(hb[:, :], V[:, oa:oa + 2 * KT], 0.5, None, ALU.mult).then_inc(*B.ends("hb"))
            dve.wait_ge(*B_act.past("tanh_b"))
            v.tensor_scalar(beta[:, :, :].rearrange("p a n -> p (a n)"), tb, 0.5, 0.5, ALU.mult, ALU.add)\
                .then_inc(*B.ends("beta"))
            dve.wait_ge(*B_act.past("exp_A"))
            v.scalar_tensor_tensor(gcol[:, :, :], sps2[:, 0:32].rearrange("p (n e) -> p n e", n=NT), -1.0,
                                   mid(exA, NT), ALU.mult, ALU.mult).then_inc(*B.ends("g"))
            dve.wait_ge(*B_pe.past("cum"))
            v.tensor_copy(gsum[:, :, :].rearrange("p a n -> p (a n)"), PS[:, 5, 0:32]).then_inc(*B.ends("gc"))
            dve.wait_ge(*B.past("gc"))
            v.tensor_tensor(small[:, 0, 0:VH], PS[:, 5, 32:48], gsum[:, 0, :], ALU.subtract)\
                .then_inc(*B.ends("gc_last"))
            dve.wait_ge(*B_act.past("eg"))
            v.tensor_scalar(negeg[:, :, :].rearrange("p a n -> p (a n)"), small[:, 1, 0:32], -1.0, None, ALU.mult)\
                .then_inc(*B.ends("negeg"))

            def rg_round(i):
                S = C_dve
                dve.wait_ge(xy_copied, 2 * i + 1)
                if not isinstance(i, int):
                    dve.wait_ge(used[S_RG[2]], i)
                for c in range(8):
                    t, j = c % 2, (3, 0, 1, 2)[c // 2]
                    src, w = rawp[:, t, j:j + T], vcol("rg_cw", j * KT + 2 * i + t)
                    if c < 2:
                        ins = v.tensor_scalar(xa[:, t, :], src, w, vcol("rg_cb", 2 * i + t), ALU.mult, ALU.add)
                    else:
                        dve.wait_ge(*S.past(f"conv{c - 2}", i))
                        ins = v.scalar_tensor_tensor(xa[:, t, :], src, w, xa[:, t, :], ALU.mult, ALU.add)
                    ins.then_inc(*S.ends(f"conv{c}"))
                dve.wait_ge(*C_act.past("y2", i))
                v.tensor_scalar(q3[:, :, :], y2b[:, :, :], GELU_A, 1.0, ALU.mult, ALU.add).then_inc(*S.ends("cub"))
                dve.wait_ge(*S.past("cub", i))
                v.tensor_tensor(q3[:, :, :], q3[:, :, :], yraw[:, :, :], ALU.mult).then_inc(*S.ends("cub_y"))
                dve.wait_ge(*C_act.past("tanh_a", i))
                for jt in range(2):
                    v.tensor_scalar(L[:, jt, :], ta[:, jt, :], 1.0, sp4[:, bass.ds(2 * i + jt, 1)], ALU.add, ALU.mult)\
                        .then_inc(*S.ends(f"l{jt}"))
                dve.wait_ge(*C_act.past("tanh_i", i))
                v.scalar_tensor_tensor(rgo[:, bass.ds(2 * i, 2), :], ti[:, :, :], 1.0, xa[:, :, :], ALU.add, ALU.mult)\
                    .then_inc(*S.ends("gated"))
                dve.wait_ge(*C_act.past("tanh_l", i))
                a_i, m_i = arg[:, bass.ds(2 * i, 2), :], mrg[:, bass.ds(2 * i, 2), :]
                v.tensor_tensor(m_i, a_i, a_i, ALU.mult).then_inc(*S.ends("dec2"))
                dve.wait_ge(*S.past("dec2", i))
                v.scalar_tensor_tensor(m_i, m_i, 1.0, ta[:, :, :], ALU.add, ALU.mult).then_inc(*S.ends("mult"))
                dve.wait_ge(*S.past("mult", i))
                v.tensor_scalar(m_i, m_i, 0.0, None, ALU.max).then_inc(*S.ends("guard"))
                dve.wait_ge(*C_act.past("tanh_y", i))
                v.scalar_tensor_tensor(mixT[:, bass.ds(2 * i, 2), :], ty[:, :, :], 1.0, yraw[:, :, :],
                                       ALU.add, ALU.mult).then_inc(*S.ends("gelu"))

            rg_round(0)
            dve.wait_ge(*B_pe.past("tr"))
            v.tensor_copy(gcT[:, :], PS[0:VH, 6, 0:T]).then_inc(*B.ends("gcT"))
            with dve.Fori(1, RGB) as i:
                rg_round(i)
            dve.wait_ge(*C_dve.past("gelu", RGB - 1))
            v.memset(ow[:, :, :], 0.0).then_inc(ow_zero, 1)

            def recurrence():
                S = Ct_dve
                dve.wait_ge(*Ct_act.past("sqrt"))
                v.memset(mrg[:, :, 0:1], 1.0).then_inc(*S.ends("first"))
                dve.wait_ge(*S.past("first"))
                v.scalar_tensor_tensor(rgo[:, :, :], rgo[:, :, :], 0.5, mrg, ALU.mult, ALU.mult).then_inc(*S.ends("b"))
                dve.wait_ge(*S.past("b"))
                for k in range(KT):
                    v.tensor_tensor_scan(mrg[:, k, :], arg[:, k, :], rgo[:, k, :], 0.0, ALU.mult, ALU.add)\
                        .then_inc(*S.ends(f"scan{k}"))
                dve.wait_ge(*S.past(f"scan{KT - 1}"))
                v.scalar_tensor_tensor(rgo[:, :, :], mixT[:, :, :], 0.5, mrg, ALU.mult, ALU.mult)\
                    .then_inc(*S.ends("out"))
                dve.wait_ge(*S.past("out"))

            def out_sums(steps, pe_steps, r):
                dve.wait_ge(*pe_steps.past("ss_o", r))
                v.tensor_scalar(ss[:, 0, :], PS[:, 7, 4:8], 1.0 / DK, EPS, ALU.mult, ALU.add)\
                    .then_inc(*steps.ends("ss_o", r))

            def out_diag(steps, pool_steps, r):
                dve.wait_ge(*pool_steps.past("r_o", r))
                v.tensor_tensor(diag[:, :, :], mid(con_("ident_half"), 4), last(ss[:, 1, :], P), ALU.mult)\
                    .then_inc(*steps.ends("diag_o", r))

            def out_scaled(steps, pe_steps, g, r):
                dve.wait_ge(*pe_steps.past("bc_o", r))
                v.tensor_tensor(og[:, bass.ds(g, 2), :], ow[:, :, :], bank3(4, 2), ALU.mult)\
                    .then_inc(*steps.ends("og", r))

            N = N_dve

            def taps(r, kind, a, b):
                dst, names, t0 = (cqk, CQK, 0) if kind == "qk" else (cv, CV, 2)
                if a == 0:
                    dve.wait_ge(qk_copied if kind == "qk" else v_copied, r + 1)
                for i in range(a, b):
                    t = i % 2
                    j = (3, 0, 1, 2)[i // 2]
                    w = vcol("gdn_cw", (r * 4 + t0 + t) * 4 + j)
                    src = rawp[:, t0 + t, j:j + T]
                    if i < 2:
                        ins = v.tensor_scalar(dst[:, t, :], src, w, None, ALU.mult)
                    else:
                        dve.wait_ge(*N.past(names[i - 2], r))
                        ins = v.scalar_tensor_tensor(dst[:, t, :], src, w, dst[:, t, :], ALU.mult, ALU.add)
                    ins.then_inc(*N.ends(names[i], r))

            def silu_qk(r):
                dve.wait_ge(*N_act.past("tanh_qk", r))
                v.scalar_tensor_tensor(cqk[:, :, :], thq[:, :, :], 1.0, cqk[:, :, :], ALU.add, ALU.mult)\
                    .then_inc(*N.ends("s_qk", r))

            def sums_qk(r):
                dve.wait_ge(*N_pe.past("ss_qk", r))
                v.tensor_scalar(ss[:, 2, :], PS[:, 6, 0:4], EPS, None, ALU.add).then_inc(*N.ends("ss_qk", r))

            def diag_qk(r):
                dve.wait_ge(*N_pool.past("r_qk", r))
                v.tensor_tensor(diag[:, :, :], con_("ident_qk", 0, 4 * P).rearrange("p (a n) -> p a n", a=4),
                                last(ss[:, 3, :], P), ALU.mult).then_inc(*N.ends("diag_qk", r))

            def select_g(r):
                v.tensor_tensor(rowsel[:, :, :], mid(gcT[:, :], 2),
                                last(C[0:VH, bass.ds(CON["ident"][0] + 2 * r, 2)], T), ALU.mult)\
                    .then_inc(*N.ends("rowsel", r))

            def scale_qk(r):
                dve.wait_ge(*N_pe.past("bc_qk", r))
                v.tensor_tensor(QK[:, :, :, :].rearrange("p n w c -> p w n c"),
                                cqk[:, :, :].rearrange("p w (n c) -> p w n c", n=NT),
                                bank(4).rearrange("p (w n c) -> p w n c", n=NT, w=2), ALU.mult)\
                    .then_inc(*N.ends("QK", r))

            def silu_v(r):
                dve.wait_ge(*N_act.past("tanh_v", r))
                v.scalar_tensor_tensor(cv[:, :, :], thv[:, :, :], 1.0, cv[:, :, :], ALU.add, ALU.mult)\
                    .then_inc(*N.ends("s_v", r))

            taps(0, "qk", 0, 8)
            silu_qk(0)
            taps(0, "v", 0, 2)
            sums_qk(0)
            taps(0, "v", 2, 4)
            diag_qk(0)
            taps(0, "v", 4, 8)
            select_g(0)
            scale_qk(0)
            recurrence()
            silu_v(0)

            def gdn_head(g, g_before, final):
                S = G_dve

                def prepare(piece, *args):
                    if not final:
                        piece(g + 1, *args)

                def scaled_by_beta(dst, src, n, j, name, more=None):
                    b = beta[:, n, bass.ds(2 * g + j, 1)]
                    if more is None:
                        ins = v.tensor_scalar(dst, src, b, None, ALU.mult)
                    else:
                        ins = v.tensor_scalar(dst, src, b, more, ALU.mult, ALU.mult)
                    ins.then_inc(*S.ends(name, g))

                out_sums(S, G_pe, g)
                dve.wait_ge(*G_act.past("eG", g))
                for n in range(NT):
                    for j in range(2):
                        v.scalar_tensor_tensor(Dt[:, n, j, :], PS[:, 6, j * T + n * P:j * T + (n + 1) * P],
                                               gsum[:, n, bass.ds(2 * g + j, 1)], neg, ALU.subtract, ALU.add)\
                            .then_inc(*S.ends(f"D{2 * n + j}", g))
                out_diag(S, G_pool, g)
                dve.wait_ge(*G_act.past("Dt", g))
                dve.wait_ge(*G_pe.past("kkqk", g))
                kkqk = bank(5).rearrange("p (n w c) -> p n w c", n=NT, w=2)
                for n in range(NT):
                    for j in range(2):
                        v.scalar_tensor_tensor(MT[:, n, j, :], Dt[:, n, j, :], beta[:, n, bass.ds(2 * g + j, 1)],
                                               kkqk[:, n, 0, :], ALU.mult, ALU.mult)\
                            .then_inc(*S.ends(f"M{2 * n + j}", g))
                dve.wait_ge(*G_pe.past("trk", g))
                v.tensor_copy(kt0[:, :], PS[:, 7, P:2 * P]).then_inc(*S.ends("kt0", g))
                v.tensor_tensor(attT[:, :, :, :], Dt[:, :, :, :],
                                kkqk[:, :, 1, :].unsqueeze(2).broadcast_to([P, NT, 2, P]), ALU.mult)\
                    .then_inc(*S.ends("att", g))
                v.tensor_tensor(qd[:, :, :], eG[:, :, :], mid(QK[:, 1, 1, :], 2), ALU.mult).then_inc(*S.ends("qd", g))
                dve.wait_ge(*G_pool.past("MM0", g))
                v.tensor_tensor(XU[:, :, 1, :], mid(ident, 4), MM[:, 0, :, :], ALU.subtract).then_inc(*S.ends("U", g))
                out_scaled(S, G_pe, g_before, g)
                dve.wait_ge(*G_act.past("tanh_z", g))
                v.scalar_tensor_tensor(zs[:, :, :], zs[:, :, :], 1.0, zraw[:, :, :], ALU.add, ALU.mult)\
                    .then_inc(*S.ends("s_z", g))

                def update(c, lv):
                    name = "AB"[c]
                    dve.wait_ge(*G_pe.past(f"P2{name}_{lv}", g))
                    if lv == 1:
                        dve.wait_ge(*G_act.past(f"X{name}", g))
                    else:
                        dve.wait_ge(*S.past(f"XU{name}_{lv - 1}", g))
                    px = PS[:, 3 + c, :].rearrange("p (u w c) -> p u w c", u=2, w=2)
                    xu = XU[:, 2 * c:2 * c + 2, :, :]
                    if lv == LEVELS - 1:
                        px, xu = bank3(3 + c, 8)[0:HALF, 0:2, :], xu[0:HALF, :, 1, HALF:P]
                    v.tensor_tensor(xu, xu, px, ALU.subtract).then_inc(*S.ends(f"XU{name}_{lv}", g))

                update(0, 1)
                for lv in range(2, LEVELS):
                    update(1, lv - 1)
                    if lv in (2, 3):
                        prepare(taps, "qk", 4 * lv - 8, 4 * lv - 6)
                    if lv == 5:
                        prepare(silu_qk)
                    update(0, lv)
                    if lv in (2, 3):
                        prepare(taps, "qk", 4 * lv - 6, 4 * lv - 4)
                    if lv == 5:
                        prepare(taps, "v", 0, 2)
                top = LEVELS - 1
                prepare(sums_qk)
                dve.wait_ge(*G_pe.past("vn0", g))
                for j in range(2):
                    scaled_by_beta(vk[:, j, :], PS[:, 2, j * P:(j + 1) * P], 0, j, f"vk{j}",
                                   kdec[:, bass.ds(2 * g + j, 1)])
                update(1, top)
                for j in range(2):
                    scaled_by_beta(vn[:, 0, j, :], PS[:, 2, j * P:(j + 1) * P], 0, j, f"vn0{j}")
                prepare(taps, "v", 2, 4)
                prepare(diag_qk)
                dve.wait_ge(*G_pe.past("kS", g))
                for j in range(2):
                    v.scalar_tensor_tensor(rr[:, j, :], PS[:, 3, j * P:(j + 1) * P], negeg[:, 1, bass.ds(2 * g + j, 1)],
                                           Vt[:, 1, j, :], ALU.mult, ALU.add).then_inc(*S.ends(f"r{j}", g))
                prepare(taps, "v", 4, 8)
                prepare(select_g)
                dve.wait_ge(*G_pe.past("vn1", g))
                for j in range(2):
                    scaled_by_beta(vn[:, 1, j, :], PS[:, 3, T + j * P:T + (j + 1) * P], 1, j, f"vn1{j}")
                prepare(scale_qk)
                prepare(silu_v)
                dve.wait_ge(osq_ready, g + 2)
                dve.wait_ge(*S.past("s_z", g))
                v.scalar_tensor_tensor(ow[:, :, :], bank3(5, 2), vcol("gdn_norm", 0), zs[:, :, :], ALU.mult, ALU.mult)\
                    .then_inc(*S.ends("ow", g))
                dve.wait_ge(*S.past("ow", g))

            with dve.Fori(0, QKH - 1) as g:
                gdn_head(g, (g + (QKH - 1)) % QKH * 2, False)
            gdn_head(QKH - 1, 2 * (QKH - 2), True)
            out_sums(Z_dve, Z_pe, 0)
            out_diag(Z_dve, Z_pool, 0)
            out_scaled(Z_dve, Z_pe, 2 * (QKH - 1), 0)

            def merge(jj, p):
                S, j, n = M_dve, 2 * jj + p, mix_fills(p, jj)
                br, bg = ((1, 2), (6, 7))[p]
                tj = mtanh[p]
                dve.wait_ge(*M_act.past("tanh", j))
                dve.wait_ge(used[S_MIX[p][1]], n)
                v.scalar_tensor_tensor(thv[:, 1, :], tj[:, 0, :], 1.0, PS[:, br, 0:T], ALU.add, ALU.mult)\
                    .then_inc(*S.ends("a"))
                dve.wait_ge(used[S_MIX[p][2]], n)
                v.scalar_tensor_tensor(thv[:, 0, :], tj[:, 1, :], 1.0, PS[:, bg, 0:T], ALU.add, ALU.mult)\
                    .then_inc(*S.ends("b"))
                dve.wait_ge(*S.past("b", j))
                v.tensor_tensor(mixT[:, bass.ds(j, 1), :].rearrange("p a n -> p (a n)"), thv[:, 0, :], thv[:, 1, :],
                                ALU.add).then_inc(*S.ends("mix"))
                dve.wait_ge(*S.past("mix", j))

            for p in range(2):
                merge(0, p)
            with dve.Fori(1, KT // 2) as jj:
                for p in range(2):
                    merge(jj, p)

            S = O_dve

            def step(name):
                dve.wait_ge(*S.past(name))

            def add_projection(n):
                for f in range(2):
                    hh = h[:, n, f * 512:(f + 1) * 512]
                    v.scalar_tensor_tensor(hh, bank(4 + 2 * n + f), 0.5, hh, ALU.mult, ALU.add)\
                        .then_inc(*S.ends(f"h{2 * n + f}"))

            def norm(n):
                mean_square(n, O_act, S)
                dve.wait_ge(*O_pool.past(f"rstd{n}"))
                dve.wait_ge(row_ffn_loaded, 16)
                v.scalar_tensor_tensor(hn[:, n, :], h[:, n, :], ss[:, 1, n:n + 1], row_ffn, ALU.mult, ALU.mult)\
                    .then_inc(*S.ends(f"hn{n}"))

            def evacuate(n):
                for b in (2 * n, 2 * n + 1):
                    k0 = 4 * (b % 2)
                    dve.wait_ge(*O_pe.past(f"tr{b}"))
                    v.tensor_copy(xnT[:, k0:k0 + 4, n * P:(n + 1) * P], bank3(b, 4)).then_inc(*S.ends(f"ev{b}"))

            dve.wait_ge(*O_pe.past("out0"))
            add_projection(0)
            norm(0)
            dve.wait_ge(used[S_OUT[3]], fills[S_OUT[3]])
            add_projection(1)
            evacuate(0)
            norm(1)
            evacuate(1)
            def select(steps, e, r):
                for n in range(NT):
                    v.tensor_scalar(Ssel[:, n, :], con_("slots", 0, CAP), posm[:, n, bass.ds(e, 1)], None,
                                    ALU.is_equal).then_inc(*steps.ends(f"S{n}", r))

            def select_weighted(steps, e, r):
                for n in range(NT):
                    v.tensor_scalar(SG[:, n, :], con_("slots", 0, 2 * CAP), posm[:, n, bass.ds(e, 1)],
                                    gate[:, n, bass.ds(e, 1)], ALU.is_equal, ALU.mult)\
                        .then_inc(*steps.ends(f"SG{n}", r))
                v.tensor_scalar(onehot, ones[0:NE, 0:CAP], C[0:NE, bass.ds(e + CON["ident"][0], 1)], None, ALU.mult)\
                    .then_inc(onehot_ready, 1)
                dve.wait_ge(*steps.past("SG1", r))
                v.tensor_scalar(posm[:, :, bass.ds(e, 1)], posm[:, :, bass.ds(e, 1)], -float(CAP), None, ALU.add)\
                    .then_inc(*steps.ends("next", r))

            dve.wait_ge(*O_pe.past("router1"))
            v.tensor_tensor(logits, PS[:, 4, 0:2 * NE].rearrange("p (n e) -> p n e", n=NT), mid(R[:, 0:NE], NT),
                            ALU.add).then_inc(*S.ends("logits"))
            step("logits")
            for n in range(NT):
                v.max(mx8[:, n, :], logits[:, n, :]).then_inc(*S.ends(f"max{n}"))
            step("max1")
            v.tensor_scalar(negm, mx8[:, :, 0], -1.0, None, ALU.mult).then_inc(*S.ends("negm"))
            for n in range(NT):
                v.tensor_scalar(gt[:, n, :], logits[:, n, :], mx8[:, n, TOP - 1:TOP], None, ALU.is_gt)\
                    .then_inc(*S.ends(f"gt{n}"))
            step("gt1")
            v.tensor_reduce(ngt, gt, AX, ALU.add).then_inc(*S.ends("ngt"))
            for n in range(NT):
                v.tensor_scalar(eq[:, n, :], logits[:, n, :], mx8[:, n, TOP - 1:TOP], None, ALU.is_equal)\
                    .then_inc(*S.ends(f"eq{n}"))
            step("ngt")
            v.tensor_scalar(need, ngt, -1.0, float(TOP), ALU.mult, ALU.add).then_inc(*S.ends("need"))
            step("eq1")
            for n in range(NT):
                v.tensor_tensor_scan(cum[:, n, :], ones[:, 0:NE], eq[:, n, :], 0.0, ALU.mult, ALU.add)\
                    .then_inc(*S.ends(f"cum{n}"))
            step("cum1")
            for n in range(NT):
                v.tensor_scalar(ok[:, n, :], cum[:, n, :], need[:, n:n + 1], None, ALU.is_le)\
                    .then_inc(*S.ends(f"ok{n}"))
            step("ok1")
            v.tensor_tensor(eq, eq, ok, ALU.mult).then_inc(*S.ends("eqok"))
            step("eqok")
            v.tensor_tensor(sel_, gt, eq, ALU.add).then_inc(*S.ends("sel"))
            step("sel")
            dve.wait_ge(*O_act.past("exp1"))
            v.tensor_tensor(exs, exs, sel_, ALU.mult).then_inc(*S.ends("exs"))
            step("exs")
            v.tensor_reduce(gsm, exs, AX, ALU.add).then_inc(*S.ends("sum"))
            step("sum")
            v.reciprocal(grec, gsm).then_inc(*S.ends("rec"))
            step("rec")
            for n in range(NT):
                v.tensor_scalar(gate[:, n, :], exs[:, n, :], grec[:, n:n + 1], None, ALU.mult)\
                    .then_inc(*S.ends(f"gate{n}"))
            dve.wait_ge(*O_pe.past("pos"))
            v.scalar_tensor_tensor(posm, PS[:, 5, 0:2 * NE].rearrange("p (n e) -> p n e", n=NT), 1.0, sel_,
                                   ALU.add, ALU.mult).then_inc(*S.ends("pos1"))
            step("pos1")
            v.tensor_scalar(posm, posm, -1.0, None, ALU.add).then_inc(*S.ends("posm"))
            step("posm")
            select(E_dve0, 0, 0)
            v.tensor_reduce(cmax, PS[:, 5, 2 * NE:3 * NE], AX, ALU.max).then_inc(*S.ends("cmax"))
            step("cmax")
            for c_, k in ((c64, 1), (c128, 2), (c192, 3)):
                v.tensor_scalar(c_, cmax, float(CAP * k), float(NE // 2), ALU.is_gt, ALU.mult)\
                    .then_inc(*S.ends(f"c{CAP * k}"))
            step("c192")
            v.tensor_tensor(c64, c64, c128, ALU.add).then_inc(*S.ends("csum"))
            step("csum")
            v.tensor_tensor(c64, c64, c192, ALU.add).then_inc(*S.ends("csum2"))
            step("csum2")
            v.tensor_scalar(loops[:, :], c64, float(NE // 2), None, ALU.add).then_inc(*S.ends("loops"))
            select_weighted(E_dve0, 0, 0)
            step("loops")
            dve.wait_ge(*O_pe.past("bd"))
            for i in range(4):
                n, f = i // 2, i % 2
                hh = h[:, n, f * 512:(f + 1) * 512]
                v.tensor_tensor(hh, hh, bank(4 + i), ALU.add).then_inc(*S.ends(f"b{i}"))

            n_pairs = dve.value_load(loops[0:1, 0:1], min_val=NE // 2, max_val=2 * NE)

            step("b3")

            def turn(it):
                S = E_dve
                dve.wait_ge(onehot_ready, it + 1)
                dve.wait_ge(E_dve.sem, E_dve.before + it * len(E_dve.names))
                dve.wait_ge(E_pe.sem, E_pe.before + it * len(E_pe.names))
                select(S, (it + 1) % NE, it)
                dve.wait_ge(used[KT - 1], fills[KT - 1] + 1 + it)
                v.tensor_scalar(eg_, bank(0), LIMIT, None, ALU.min).then_inc(*S.ends("g", it))
                v.tensor_scalar(eu, bank(1), LIMIT, -LIMIT, ALU.min, ALU.max).then_inc(*S.ends("u", it))
                dve.wait_ge(*S.past("u", it))
                v.scalar_tensor_tensor(ehid, eu, 1.0, eg_, ALU.add, ALU.mult).then_inc(*S.ends("p", it))
                dve.wait_ge(*S.past("p", it))
                dve.wait_ge(*E_act.past("th", it))
                v.scalar_tensor_tensor(ehid, eth, 1.0, ehid, ALU.add, ALU.mult).then_inc(*S.ends("hid", it))
                dve.wait_ge(*E_pe.past("trS", it))
                select_weighted(S, (it + 1) % NE, it)
                for i in range(4):
                    n, f = i // 2, i % 2
                    dve.wait_ge(*E_pe.past(f"scatter{n}", it))
                    hh = h[:, n, f * 512:(f + 1) * 512]
                    v.tensor_tensor(hh, hh, bank(4 + i), ALU.add).then_inc(*S.ends(f"y{i}", it))

            with dve.Fori(0, n_pairs) as ii:
                for p in range(2):
                    turn(2 * ii + p)
            dve.wait_ge(E_dve.sem, E_dve.before + n_pairs * (2 * len(E_dve.names)))

            S = F_dve
            for n in range(NT):
                mean_square(n, F_act, S)
            dve.wait_ge(row_final_loaded, 16)
            for n in range(NT):
                dve.wait_ge(*F_pool.past(f"rstd{n}"))
                v.scalar_tensor_tensor(hn[:, n, :], h[:, n, :], ss[:, 1, n:n + 1], row_final, ALU.mult, ALU.mult)\
                    .then_inc(*S.ends(f"o{n}"))

        @block.gpsimd
        def _(pool):
            tt = nc.gpsimd.tensor_tensor

            def rsqrt(dst, src, n, ends):
                tt(dst[:, 0:n], src[:, 0:n], half_pow[:, 0:n], ALU.pow).then_inc(*ends)

            def rstd(steps, dve_steps):
                for n in range(NT):
                    pool.wait_ge(*dve_steps.past(f"ms{n}"))
                    rsqrt(ss[:, 1, n:n + 1], ss[:, 3, n:n + 1], 1, steps.ends(f"rstd{n}"))

            rstd(A_pool, A_dve)

            def rsqrt_qk(r):
                pool.wait_ge(*N_dve.past("ss_qk", r))
                rsqrt(ss[:, 3, :], ss[:, 2, :], 4, N_pool.ends("r_qk", r))

            def gdn_head(g, final):
                pool.wait_ge(*G_dve.past("ss_o", g))
                rsqrt(ss[:, 1, :], ss[:, 0, :], 4, G_pool.ends("r_o", g))
                pool.wait_ge(*G_dve.past("M3", g))
                for lv in range(LEVELS):
                    if lv == 3:
                        pool.wait_ge(*G_dve.past("U", g))
                    if lv > 3:
                        pool.wait_ge(*G_pe.past(f"P1B_{lv - 3}", g))
                    tt(MM[:, lv % 3, :, :], MT[:, :, :, :].rearrange("p a b c -> p (a b) c"), mid(mask(lv), 4),
                       ALU.mult).then_inc(*G_pool.ends(f"MM{lv}", g))
                if not final:
                    rsqrt_qk(g + 1)

            rsqrt_qk(0)
            with pool.Fori(0, QKH - 1) as g:
                gdn_head(g, False)
            gdn_head(QKH - 1, True)
            pool.wait_ge(*Z_dve.past("ss_o"))
            rsqrt(ss[:, 1, :], ss[:, 0, :], 4, Z_pool.ends("r_o"))
            rstd(O_pool, O_dve)
            rstd(F_pool, F_dve)


def kernel(**inputs):
    import concourse.bacc as bacc
    from concourse.bass_utils import run_bass_kernel_spmd

    a = {k: np.asarray(v) for k, v in inputs.items()}
    f32 = np.float32

    def cols(v):
        return v.reshape(-1, P).T

    cw = a["gdn_conv_w"][0]
    cq, ck, cv_ = cw[:, :D], cw[:, D:2 * D], cw[:, 2 * D:]
    gcw = np.stack([ck.reshape(4, QKH, P), cq.reshape(4, QKH, P),
                    cv_.reshape(4, QKH, 2, P)[:, :, 0], cv_.reshape(4, QKH, 2, P)[:, :, 1]])
    vec = np.concatenate([
        cols(a["norm_mix_w"][0]),
        a["rg_conv_w"][0].reshape(4, KT, P).transpose(2, 0, 1).reshape(P, 4 * KT),
        cols(a["rg_conv_b"][0]), cols(a["rg_gate_a_b"][0].reshape(-1)), cols(a["rg_gate_x_b"][0].reshape(-1)),
        cols(a["rg_lambda"][0]),
        gcw.transpose(3, 2, 0, 1).reshape(P, QKH * 16),
        a["gdn_norm_w"][0].reshape(P, 1),
    ], axis=1)
    row = np.broadcast_to(np.concatenate([a["router_b"][0], a["gdn_dt_bias"][0], a["gdn_A_log"][0]])[None], (P, NROW))
    ffn_rows = np.broadcast_to(np.stack([a["norm_ffn_w"][0], a["norm_final_w"]])[None], (P, 2, D))

    w_in = a["w_in"][0]
    o_b = 2 * D + 2 * D + 2 * 2 * D
    tiles = w_in[:, :o_b].reshape(KT, P, o_b // P, P).transpose(2, 1, 0, 3)
    gate_tiles = w_in[:, o_b + 2 * VH:].reshape(KT, P, 2 * KT, P).transpose(2, 1, 0, 3)

    def pieces(order, src):
        return src[np.array(order)].reshape(-1, 2, P, D).transpose(0, 2, 1, 3).reshape(-1, P, SLOT)

    rg_x, rg_y, q, k, v, z = 0, 8, 16, 24, 32, 48
    w_rg = pieces([t for i in range(RGB) for o in (rg_x, rg_y) for t in (o + 2 * i, o + 2 * i + 1)], tiles)
    w_gdn = pieces([t for g in range(QKH) for t in (k + g, q + g, v + 2 * g, v + 2 * g + 1, z + 2 * g, z + 2 * g + 1)],
                   tiles)
    w_gates = pieces([t for j in range(KT) for t in (j, KT + j)], gate_tiles)
    w_rgg = np.stack([a["rg_gate_a_w"][0], a["rg_gate_x_w"][0]], 1).reshape(RGB, 2, 2, P, 256)\
        .transpose(0, 3, 1, 2, 4).reshape(RGB, P, D)
    w_ba = np.stack([w_in[:, o_b:o_b + 2 * VH], a["router_w"][0]]).reshape(2, KT, P, 32).transpose(0, 2, 1, 3)
    w_bg = a["w_branch_gdn"][0].reshape(VH, P, KT, P).transpose(2, 1, 0, 3).reshape(KT, P, SLOT)
    w_br = a["w_branch_rg"][0].reshape(KT, P, KT, P).transpose(2, 1, 0, 3).reshape(KT, P, D)
    nc = bacc.Bacc("TRN2", target_bir_lowering=False, num_devices=1)
    arrays, args = {}, []
    for name, v_ in (("x", a["x"][0]), ("vec", vec), ("row", row), ("con", constants()),
                     ("w_rg", w_rg.reshape(RGB, 2, P, SLOT)), ("w_rgg", w_rgg), ("w_ba", w_ba),
                     ("w_gdn", w_gdn.reshape(QKH, 3, P, SLOT)), ("w_gates", w_gates), ("w_bg", w_bg), ("w_br", w_br),
                     ("w_out", a["w_out"][0]), ("ffn_rows", ffn_rows),
                     ("moe_gu", a["moe_w_gate_up"][0].reshape(NE, KT, P, SLOT)),
                     ("moe_down", a["moe_w_down"][0]), ("b_gu", a["moe_b_gate_up"][0]), ("b_down", a["moe_b_down"][0])):
        v_ = np.ascontiguousarray(v_)
        assert v_.dtype == f32
        arrays[name] = v_
        args.append(nc.dram_tensor(name, v_.shape, F32, kind="ExternalInput").ap())
    args.append(nc.dram_tensor("out", (T, D), F32, kind="ExternalOutput").ap())
    build(nc, *args)
    r = run_bass_kernel_spmd(nc, [arrays], core_ids=[0])
    return r.results[0]["out"].reshape(1, T, D)
```
